# Optimizing a Trainium2 kernel written in Bass

```python
import jax, jax.numpy as jnp
from jax import lax
import numpy as np

D_MODEL = 1024
BATCH = 1
SEQ = 4096
DEPTH = 1
DEC_BATCH = 8
DEC_SEQ = 16
PAST_LEN = 512

CHUNK = 64
MIX_WIDTH = D_MODEL
RMS_EPS = 1e-6
GLA_WIDTH = MIX_WIDTH // 2
GLA_HEADS = 4
GLA_DV = GLA_WIDTH // GLA_HEADS
GLA_DK = GLA_DV // 2
GLA_KEY = GLA_HEADS * GLA_DK
GLA_RANK = 16
GLA_TEMP = 16.0
GLA_COLS = 2 * GLA_KEY + 2 * GLA_WIDTH + GLA_RANK
RWKV_WIDTH = MIX_WIDTH - GLA_WIDTH
RWKV_HEAD = 64
RWKV_HEADS = RWKV_WIDTH // RWKV_HEAD
RWKV_RANK_W = 64
RWKV_RANK_A = 64
SHIFT_W = 3 * RWKV_WIDTH + RWKV_RANK_W + RWKV_RANK_A
RWKV_GN_EPS = 64e-5
RWKV_DECAY_SCALE = 0.606531
IN_COLS = GLA_COLS + SHIFT_W + RWKV_WIDTH

kernel_name = "gla_rwkv7_parallel_heads_streaming"

def rms_norm(x, g):
    xf = x.astype(jnp.float32)
    y = xf * lax.rsqrt(jnp.mean(xf * xf, -1, keepdims=True) + RMS_EPS)
    return (y * g.astype(jnp.float32)).astype(x.dtype)

def gla_recurrence(q, k, v, log_a, s0):
    B, T, H, _ = q.shape
    L = min(CHUNK, T)
    n = -(-T // L)
    pad = n * L - T

    def blocks(t):
        t = jnp.pad(t, ((0, 0), (0, pad), (0, 0), (0, 0)))
        return t.reshape(B, n, L, H, t.shape[-1]).transpose(1, 0, 3, 2, 4)

    qb, kb, vb, gb = blocks(q), blocks(k), blocks(v), blocks(log_a)
    causal = jnp.tril(jnp.ones((L, L), dtype=bool))

    def step(s, inp):
        qc, kc, vc, gc = inp
        b = jnp.cumsum(gc, axis=2)
        diff = b[:, :, :, None, :] - b[:, :, None, :, :]
        decay = jnp.exp(jnp.where(causal[:, :, None], diff, -jnp.inf))
        att = jnp.einsum('bhtd,bhtsd,bhsd->bhts', qc, decay, kc)
        o = (jnp.einsum('bhtd,bhde->bhte', qc * jnp.exp(b), s)
             + jnp.einsum('bhts,bhse->bhte', att, vc))
        b_last = b[:, :, -1:, :]
        s_new = (jnp.exp(b_last[:, :, 0, :])[..., None] * s
                 + jnp.einsum('bhsd,bhse->bhde', kc * jnp.exp(b_last - b), vc))
        return s_new, o

    s_fin, ob = lax.scan(step, s0, (qb, kb, vb, gb))
    o = ob.transpose(1, 0, 3, 2, 4).reshape(B, n * L, H, v.shape[-1])[:, :T]
    return o, s_fin

def rwkv7_recurrence(r, w, k, v, kk, a, s0):
    def step(s, inp):
        r_t, w_t, k_t, v_t, kk_t, a_t = inp
        sa = jnp.einsum('bhij,bhj->bhi', s, -kk_t)
        s = (s * w_t[:, :, None, :] + sa[..., None] * (kk_t * a_t)[:, :, None, :]
             + v_t[..., None] * k_t[:, :, None, :])
        y = jnp.einsum('bhij,bhj->bhi', s, r_t)
        return s, y

    xs = tuple(jnp.moveaxis(t, 1, 0) for t in (r, w, k, v, kk, a))
    s_fin, ys = lax.scan(step, s0, xs)
    return jnp.moveaxis(ys, 0, 1), s_fin

def hybrid_layer(x, s_gla, s_rwkv, s_shift, norm_pre, norm_post, w_in, gla_a_up,
                 gla_a_bias, gla_norm, rwkv_mu, rwkv_w_up, rwkv_w0, rwkv_a_up,
                 rwkv_a0, rwkv_k_k, rwkv_k_a, rwkv_r_k, rwkv_ln_w, rwkv_ln_b, w_out):
    B, T, _ = x.shape
    f32 = jnp.float32
    h = rms_norm(x, norm_pre)
    p = jnp.einsum('btd,dc->btc', h, w_in).astype(f32)
    p_gla = p[..., :GLA_COLS]
    p_shift = p[..., GLA_COLS:GLA_COLS + SHIFT_W]
    z_r = p[..., GLA_COLS + SHIFT_W:]

    q, k, v, z_g, gd = jnp.split(
        p_gla, [GLA_KEY, 2 * GLA_KEY, 2 * GLA_KEY + GLA_WIDTH, 2 * GLA_KEY + 2 * GLA_WIDTH], -1)
    q = q.reshape(B, T, GLA_HEADS, GLA_DK) * (GLA_DK ** -0.5)
    k = k.reshape(B, T, GLA_HEADS, GLA_DK)
    v = v.reshape(B, T, GLA_HEADS, GLA_DV)
    log_a = jax.nn.log_sigmoid(gd @ gla_a_up.astype(f32) + gla_a_bias.astype(f32)) / GLA_TEMP
    log_a = log_a.reshape(B, T, GLA_HEADS, GLA_DK)
    o, s_gla_new = gla_recurrence(q, k, v, log_a, s_gla.astype(f32))
    o = o * lax.rsqrt(jnp.mean(o * o, -1, keepdims=True) + RMS_EPS) * gla_norm.astype(f32)
    o_gla = o.reshape(B, T, GLA_WIDTH) * jax.nn.silu(z_g)

    prev = jnp.concatenate([s_shift.astype(f32)[:, None], p_shift[:, :-1]], axis=1)
    xm = p_shift + rwkv_mu.astype(f32) * (prev - p_shift)
    r, kr, vr, wd, ad = jnp.split(
        xm, [RWKV_WIDTH, 2 * RWKV_WIDTH, 3 * RWKV_WIDTH, 3 * RWKV_WIDTH + RWKV_RANK_W], -1)
    w = jnp.exp(-RWKV_DECAY_SCALE * jax.nn.sigmoid(
        rwkv_w0.astype(f32) + jnp.tanh(wd) @ rwkv_w_up.astype(f32)))
    a = jax.nn.sigmoid(rwkv_a0.astype(f32) + ad @ rwkv_a_up.astype(f32))
    kk = kr * rwkv_k_k.astype(f32)
    kr = kr * (1.0 + (a - 1.0) * rwkv_k_a.astype(f32))
    hd = lambda t: t.reshape(B, T, RWKV_HEADS, RWKV_HEAD)
    r, w, kr, vr, kk, a = hd(r), hd(w), hd(kr), hd(vr), hd(kk), hd(a)
    kk = kk / jnp.maximum(jnp.sqrt(jnp.sum(kk * kk, -1, keepdims=True)), 1e-12)
    y, s_rwkv_new = rwkv7_recurrence(r, w, kr, vr, kk, a, s_rwkv.astype(f32))
    mu = jnp.mean(y, -1, keepdims=True)
    var = jnp.mean(jnp.square(y - mu), -1, keepdims=True)
    y = ((y - mu) * lax.rsqrt(var + RWKV_GN_EPS)).reshape(B, T, RWKV_WIDTH)
    y = y * rwkv_ln_w.astype(f32) + rwkv_ln_b.astype(f32)
    bonus = jnp.sum(r * kr * rwkv_r_k.astype(f32), -1, keepdims=True) * vr
    o_rwkv = (y + bonus.reshape(B, T, RWKV_WIDTH)) * jax.nn.silu(z_r)

    m = jnp.concatenate([o_gla, o_rwkv], -1).astype(x.dtype)
    m = jnp.einsum('btc,cd->btd', m, w_out)
    x = x + rms_norm(m, norm_post)
    return x, s_gla_new, s_rwkv_new, p_shift[:, -1]

def setup_inputs(seed: int = 0) -> dict:
    key = jax.random.key(seed)
    ks = jax.random.split(key, 24)
    n = lambda i, shape, s: jax.random.normal(ks[i], shape, jnp.float32) * s
    return {
        "x_prompt": n(0, (BATCH, SEQ, D_MODEL), 1.0),
        "x_sample": n(1, (DEC_BATCH, DEC_SEQ, D_MODEL), 1.0),
        "state_gla": n(2, (DEPTH, DEC_BATCH, GLA_HEADS, GLA_DK, GLA_DV), 0.5),
        "state_rwkv": n(3, (DEPTH, DEC_BATCH, RWKV_HEADS, RWKV_HEAD, RWKV_HEAD), 0.5),
        "state_shift": n(4, (DEPTH, DEC_BATCH, SHIFT_W), 1.0),
        "norm_pre": 1.0 + n(5, (DEPTH, D_MODEL), 0.05),
        "norm_post": 1.0 + n(6, (DEPTH, D_MODEL), 0.05),
        "w_in": n(7, (DEPTH, D_MODEL, IN_COLS), D_MODEL ** -0.5),
        "gla_a_up": n(8, (DEPTH, GLA_RANK, GLA_KEY), GLA_RANK ** -0.5),
        "gla_a_bias": 1.0 + n(9, (DEPTH, GLA_KEY), 0.5),
        "gla_norm": 1.0 + n(10, (DEPTH, GLA_DV), 0.05),
        "rwkv_mu": jax.random.uniform(ks[11], (DEPTH, SHIFT_W), jnp.float32),
        "rwkv_w_up": n(12, (DEPTH, RWKV_RANK_W, RWKV_WIDTH), RWKV_RANK_W ** -0.5),
        "rwkv_w0": n(13, (DEPTH, RWKV_WIDTH), 0.5),
        "rwkv_a_up": n(14, (DEPTH, RWKV_RANK_A, RWKV_WIDTH), RWKV_RANK_A ** -0.5),
        "rwkv_a0": n(15, (DEPTH, RWKV_WIDTH), 0.5),
        "rwkv_k_k": 0.85 + n(16, (DEPTH, RWKV_WIDTH), 0.05),
        "rwkv_k_a": 1.0 + n(17, (DEPTH, RWKV_WIDTH), 0.05),
        "rwkv_r_k": n(18, (DEPTH, RWKV_HEADS, RWKV_HEAD), 0.1),
        "rwkv_ln_w": 1.0 + n(19, (DEPTH, RWKV_WIDTH), 0.05),
        "rwkv_ln_b": n(20, (DEPTH, RWKV_WIDTH), 0.02),
        "w_out": n(21, (DEPTH, MIX_WIDTH, D_MODEL), MIX_WIDTH ** -0.5),
    }

def reference(x_prompt, x_sample, state_gla, state_rwkv, state_shift, norm_pre, norm_post,
              w_in, gla_a_up, gla_a_bias, gla_norm, rwkv_mu, rwkv_w_up, rwkv_w0, rwkv_a_up,
              rwkv_a0, rwkv_k_k, rwkv_k_a, rwkv_r_k, rwkv_ln_w, rwkv_ln_b, w_out):
    bp = x_prompt.shape[0]
    yp, ys = x_prompt, x_sample
    gla_p, gla_s, rwkv_p, rwkv_s, shift_p, shift_s = [], [], [], [], [], []
    for l in range(DEPTH):
        params = (norm_pre[l], norm_post[l], w_in[l], gla_a_up[l], gla_a_bias[l], gla_norm[l],
                  rwkv_mu[l], rwkv_w_up[l], rwkv_w0[l], rwkv_a_up[l], rwkv_a0[l], rwkv_k_k[l],
                  rwkv_k_a[l], rwkv_r_k[l], rwkv_ln_w[l], rwkv_ln_b[l], w_out[l])
        z_gla = jnp.zeros((bp, GLA_HEADS, GLA_DK, GLA_DV), jnp.float32)
        z_rwkv = jnp.zeros((bp, RWKV_HEADS, RWKV_HEAD, RWKV_HEAD), jnp.float32)
        z_shift = jnp.zeros((bp, SHIFT_W), jnp.float32)
        yp, g1, r1, s1 = hybrid_layer(yp, z_gla, z_rwkv, z_shift, *params)
        ys, g2, r2, s2 = hybrid_layer(ys, state_gla[l], state_rwkv[l], state_shift[l], *params)
        gla_p.append(g1); rwkv_p.append(r1); shift_p.append(s1)
        gla_s.append(g2.astype(state_gla.dtype)); rwkv_s.append(r2.astype(state_rwkv.dtype))
        shift_s.append(s2.astype(state_shift.dtype))
    return (yp, ys, jnp.stack(gla_p), jnp.stack(gla_s), jnp.stack(rwkv_p), jnp.stack(rwkv_s),
            jnp.stack(shift_p), jnp.stack(shift_s))


_drawn_inputs = setup_inputs


def setup_inputs(seed=0):
    import zlib

    import numpy as np

    out = dict(_drawn_inputs(seed))
    spreads = {}
    factors = {'rwkv_k_k': 4.81, 'rwkv_ln_b': 5.938}
    for name, (base, spread) in spreads.items():
        noise = np.random.default_rng([zlib.crc32(name.encode()), seed]).standard_normal(out[name].shape)
        drawn = base * np.exp(spread * noise) if base else spread * noise
        out[name] = __import__('jax').numpy.asarray(drawn.astype(out[name].dtype))
    for name, factor in factors.items():
        out[name] = (out[name] * factor).astype(out[name].dtype)
    return out
```

```python
from contextlib import ExitStack

import numpy as np

import concourse.bass as bass
from concourse import mybir

ALU = mybir.AluOpType
ACT = mybir.ActivationFunctionType
F32 = mybir.dt.float32
F16 = mybir.dt.float16

P = 128
D = 1024
KT = D // P
SEQ = 4096
BLK = 256
NB = 1 + SEQ // BLK
LAST = NB - 1
STREAMS, SLEN = 8, 16
SHIFT_W = 1664
GLA_COLS = 1552
RMS_EPS = 1e-6
GN_EPS = 64e-5
DECAY = 0.606531
GLA_TEMP = 16.0

H_SCALE = 64.0
W_SCALE = 256.0
M_SCALE = 16.0
UNSCALE = 1.0 / (H_SCALE * W_SCALE)

PAR = {}
for _name, _n in (("npre", 8), ("gla_bias", 2), ("gla_norm", 1), ("mu", 13), ("w0", 4), ("a0", 4),
                  ("k_k", 4), ("k_a", 4), ("r_k", 4), ("ln_w", 4), ("ln_b", 4)):
    PAR[_name] = (sum(n for _, n in PAR.values()), _n)
NPAR = sum(n for _, n in PAR.values())

C_Q, C_K, C_V, C_ZG, C_GD, C_ZR, W1_COLS = 0, 256, 512, 1024, 1536, 1552, 2064
W2_COLS = SHIFT_W


class Signal:

    def __init__(self, sem, name, first, rest, step=1):
        self.sem, self.name, self.first, self.rest, self.step = sem, name, first, rest, step
        self.seen = {}

    def at(self, b, k):
        if isinstance(b, int) and b == 0:
            return k * self.step
        return b * (self.rest * self.step) + (self.first - self.rest + k) * self.step

    def up(self, b):
        key = b if isinstance(b, int) else "loop"
        self.seen[key] = self.seen.get(key, 0) + 1
        return self.sem, self.step

    def check(self):
        for key, n in self.seen.items():
            assert n == (self.first if key == 0 else self.rest), (self.name, key, n)


def tiles(b):
    return 1 if isinstance(b, int) and b == 0 else BLK // P


def is_sample(b):
    return isinstance(b, int) and b == 0


def build(nc, t):
    with ExitStack() as ctx:
        def sb(name, shape, dt=F32):
            return ctx.enter_context(nc.sbuf_tensor(name, shape, dt))

        def sem(name):
            return ctx.enter_context(nc.semaphore(name))

        c = {}
        c["par"] = sb("par", [P, NPAR])
        c["ident"] = sb("ident", [P, P])
        c["consts"] = sb("consts", [P, 8])
        c["bar"] = sem("s_phase")
        setup(nc, t, c)
        gla_phase(nc, t, c)
        rwkv_phase(nc, t, c)


K_ONE, K_RMS, K_LNH, K_GN, K_LNM, K_KK = range(6)


def setup(nc, t, c):
    par, ident, consts = c["par"], c["ident"], c["consts"]
    with ExitStack() as ctx:
        loaded = ctx.enter_context(nc.semaphore("s_par_loaded"))
        zeroed = ctx.enter_context(nc.semaphore("s_ident_zeroed"))
        made = ctx.enter_context(nc.semaphore("s_ident_made"))
        block = ctx.enter_context(nc.Block())

        @block.sync
        def _(sp):
            sp.dma_start(par[:, :], t["par"]).then_inc(loaded, 16)
            sp.wait_ge(loaded, 16)

        @block.gpsimd
        def _(pool):
            pool.memset(ident[:, :], 0.0).then_inc(zeroed, 1)
            pool.wait_ge(zeroed, 1)
            pool.affine_select(out=ident[:, :], in_=ident[:, :], compare_op=ALU.not_equal, fill=1.0,
                               base=0, pattern=[[-1, P]], channel_multiplier=1).then_inc(made, 1)
            for k, v in ((K_ONE, 1.0), (K_RMS, RMS_EPS), (K_LNH, float(np.log(H_SCALE))), (K_GN, GN_EPS),
                         (K_LNM, -float(np.log(M_SCALE * W_SCALE))), (K_KK, 10 * float(np.log(2.0)))):
                pool.memset(consts[:, k:k + 1], v).then_inc(made, 1)
            pool.wait_ge(made, 7)


def gla_phase(nc, t, c):
    par, ident, consts = c["par"], c["ident"], c["consts"]

    def pcol(name, g=0):
        return par[:, PAR[name][0] + g:PAR[name][0] + g + 1]

    def const(k):
        return consts[:, k:k + 1]

    with ExitStack() as ctx:
        def sb(name, shape, dt=F32):
            return ctx.enter_context(nc.sbuf_tensor(name, shape, dt))

        def bank(name):
            return ctx.enter_context(nc.psum_tensor(name, [P, 512], F32))

        signals = []

        def sig(name, first, rest, step=1):
            s = Signal(ctx.enter_context(nc.semaphore("s_" + name)), name, first, rest, step)
            signals.append(s)
            return s

        w_hi = sb("w1_hi", [P, KT, W1_COLS], F16)
        w_lo = sb("w1_lo", [P, KT, W1_COLS], F16)
        stage = sb("w1_stage", [P, 2, W1_COLS])
        gscale = sb("gscale", [P, KT])
        a_up = sb("a_up", [16, 256])
        g_norm = sb("g_norm", [P, 1])
        ones_dv = sb("ones_dv", [P, P])
        mask_prompt = sb("mask_prompt", [P, P])
        mask_sample = sb("mask_sample", [P, P])
        seg_rows = sb("seg_rows", [P, STREAMS])
        run_prompt = sb("run_prompt", [P, 2 * BLK])
        run_sample = sb("run_sample", [P, 2 * P])
        x_tok = sb("x_tok", [P, 2, D])
        junk = sb("junk", [P, D], F16)
        ssq = sb("ssq", [P, 2])
        lnx = sb("lnx", [P, 2])
        rstd = sb("rstd", [P, 2])
        diag = sb("diag", [P, 2, P])
        hT = sb("hT", [P, 2, KT, BLK], F16)
        gd_sb = sb("gd_sb", [16, BLK])
        q_sb = sb("q_sb", [P, 2, BLK])
        k_sb = sb("k_sb", [P, 2, BLK])
        qd = sb("qd", [P, 2, 2, BLK])
        kd = sb("kd", [P, 2, BLK])
        v_tok = sb("v_tok", [P, 2, 512])
        zg = sb("zg", [P, 4, BLK])
        zr = sb("zr", [P, 4, BLK])
        th = sb("th", [P, 2, BLK])
        absx = sb("absx", [P, 2, BLK])
        minx = sb("minx", [P, 2, BLK])
        cum = sb("cum", [P, 2, BLK])
        eb = sb("eb", [P, 2, BLK])
        enb = sb("enb", [P, 2, BLK])
        dmid = sb("dmid", [P, 2, 8])
        dlast = sb("dlast", [P, 2, 8])
        S = sb("S", [P, 2, P])
        Sd = sb("Sd", [P, 2, P])
        Ss = sb("Ss", [P, STREAMS, 2, P])
        att_m = sb("att_m", [P, 4, P])
        k_tok = sb("k_tok", [P, 2, P])
        k_seg = sb("k_seg", [P, 2, P])
        o_sb = sb("o_sb", [P, 4, P])
        o_sq = sb("o_sq", [P, 4, P])
        r_o = sb("r_o", [P, 4, P])
        mg = sb("mg", [P, 4, P])
        m_hl = sb("m_hl", [P, 2, 4, P], F16)

        tr_bank = [bank("tr0"), bank("tr1")]
        d_bank = [bank("d0"), bank("d1"), bank("d2")]
        att = bank("att").rearrange("p (h t) -> p h t", h=4)
        obank = bank("obank").rearrange("p (h t) -> p h t", h=4)
        kbank = bank("kbank").rearrange("p (a g t) -> p a g t", a=2, g=2)

        with ExitStack() as pre:
            w_in = [pre.enter_context(nc.semaphore(f"s_w1_in{i}")) for i in range(2)]
            w_split = pre.enter_context(nc.semaphore("s_w1_split"))
            w_high = pre.enter_context(nc.semaphore("s_w1_high"))
            small = pre.enter_context(nc.semaphore("s_small_in"))
            scaled = pre.enter_context(nc.semaphore("s_scaled"))
            pset = pre.enter_context(nc.semaphore("s_pool_set"))
            block = pre.enter_context(nc.Block())

            @block.sync
            def _(sp):
                sp.dma_start(a_up[:, :], t["gla_a_up"]).then_inc(small, 16)
                sp.dma_start(Ss[:, :, :, :], t["state_gla"]).then_inc(small, 16)
                for k in range(KT):
                    if k >= 2:
                        sp.wait_ge(w_split, k - 1)
                    rows = t["w_in"][k * P:(k + 1) * P, :]
                    sp.dma_start(stage[:, k % 2, 0:GLA_COLS], rows[:, 0:GLA_COLS]).then_inc(w_in[k % 2], 16)
                    sp.dma_start(stage[:, k % 2, GLA_COLS:W1_COLS],
                                 rows[:, GLA_COLS + SHIFT_W:]).then_inc(w_in[k % 2], 16)
                sp.wait_ge(small, 32)

            @block.scalar
            def _(act):
                act.wait_ge(scaled, 1)
                for k in range(KT):
                    act.wait_ge(w_in[k % 2], 32 * (k // 2 + 1))
                    cols = (0, 512, 1024)
                    act.activation(w_hi[:, k, :], stage[:, k % 2, :], ACT.Identity,
                                   scale=gscale[:, k:k + 1]).then_inc(w_high, 1)

            @block.vector
            def _(dve):
                dve.tensor_scalar(gscale[:, :], par[:, 0:KT], W_SCALE, None, ALU.mult).then_inc(scaled, 1)
                dve.wait_ge(scaled, 1)
                dve.tensor_scalar(g_norm[:, :], pcol("gla_norm"), M_SCALE * UNSCALE * 0.5, None,
                                  ALU.mult).then_inc(scaled, 1)
                for k in range(KT):
                    dve.wait_ge(w_high, k + 1)
                    dve.scalar_tensor_tensor(out=w_lo[:, k, :], in0=stage[:, k % 2, :],
                                             scalar=gscale[:, k:k + 1], in1=w_hi[:, k, :],
                                             op0=ALU.mult, op1=ALU.subtract).then_inc(w_split, 1)

            @block.gpsimd
            def _(pool):
                n = 0
                for m, v in ((ones_dv, 1.0 / P), (mask_prompt, 1.0), (mask_sample, 1.0), (seg_rows, 1.0),
                             (run_prompt, 1.0), (run_sample, 1.0), (S, 0.0), (qd, 0.0)):
                    ap = m[:, :, :] if m is S else m[:, :, :, :] if m is qd else m[:, :]
                    pool.memset(ap, v).then_inc(pset, 1)
                    n += 1
                pool.wait_ge(pset, n)
                pool.affine_select(out=mask_prompt[:, :], in_=mask_prompt[:, :], compare_op=ALU.is_ge, fill=0.0,
                                   base=0, pattern=[[1, P]], channel_multiplier=-1).then_inc(pset, 1)
                pool.affine_select(out=mask_sample[:, :], in_=mask_sample[:, :], compare_op=ALU.is_ge, fill=0.0,
                                   base=0, pattern=[[1, P]], channel_multiplier=-1).then_inc(pset, 1)
                pool.affine_select(out=seg_rows[:, :], in_=seg_rows[:, :], compare_op=ALU.is_ge, fill=0.0,
                                   base=0, pattern=[[-SLEN, STREAMS]], channel_multiplier=1).then_inc(pset, 1)
                pool.memset(run_prompt[:, :].rearrange("p (c t) -> p c t", t=P)[:, :, 0:1], 0.0).then_inc(pset, 1)
                pool.memset(run_sample[:, :].rearrange("p (c t) -> p c t", t=SLEN)[:, :, 0:1], 0.0).then_inc(pset, 1)
                n += 5
                pool.wait_ge(pset, n)
                pool.affine_select(out=mask_sample[:, :], in_=mask_sample[:, :], compare_op=ALU.is_ge, fill=0.0,
                                   base=0, pattern=[[-SLEN, STREAMS], [0, SLEN]],
                                   channel_multiplier=1).then_inc(pset, 1)
                pool.affine_select(out=seg_rows[:, :], in_=seg_rows[:, :], compare_op=ALU.is_ge, fill=0.0,
                                   base=SLEN - 1, pattern=[[SLEN, STREAMS]], channel_multiplier=-1).then_inc(pset, 1)
                n += 2
                pool.wait_ge(pset, n)

        x_in = [sig("x_in0", 1, 1, 16), sig("x_in1", 0, 1, 16)]
        h_out = sig("h_out", 1, 1, 16)
        zr_out = sig("zr_out", 1, 1, 16)
        mg_out = sig("mg_out", 1, 2, 16)
        st_out = sig("gla_state_out", 1, 0, 16)
        x_stat = sig("x_stat", 3, 6)
        diag_ok = sig("diag", 1, 2)
        tr_full = sig("tr_full", 2, 4)
        h_high = sig("h_high", 2, 4)
        h_low = sig("h_low", 2, 4)
        d_full = sig("d_full", 9, 10)
        ms_full = sig("ms_full", 1, 2)
        gd_ok = sig("gd", 1, 1)
        absx_ok = sig("absx", 2, 2)
        minx_ok = sig("minx", 3, 3)
        ln_ok = sig("logsig", 2, 2)
        cum_ok = sig("cum", 3, 3)
        eb_ok = sig("eb", 4, 4)
        qk_ok = sig("qk_decayed", 3, 3)
        k_sb_ok = sig("k_sb", 1, 1)
        q_sb_ok = sig("q_sb", 1, 1)
        th_ok = sig("tanh", 4, 4)
        z_ok = sig("z_gated", 4, 4)
        v_ok = sig("v_tok", 1, 2)
        g1_full = sig("g1_full", 1, 2)
        att_ok = sig("att_masked", 1, 2)
        ktok_ok = sig("k_tok", 1, 2)
        sd_ok = sig("state_mid", 2 * STREAMS, 4)
        o_full = sig("o_full", 1, 2)
        s_full = sig("state_full", STREAMS, 2)
        kseg_ok = sig("k_seg", STREAMS, 0)
        ssum_ok = sig("state_sum", STREAMS, 2)
        s_ok = sig("state_ok", 2 * STREAMS, 4)
        o_ok = sig("o_sb", 2, 4)
        r_ok = sig("r_o", 2, 4)
        m_ok = sig("m_steps", 2, 4)
        mh_ok = sig("m_high", 1, 2)
        ml_ok = sig("m_low", 1, 2)

        def rounds(b):
            r = [("gd", 0), ("q", 0), ("k", 0), ("up", 0), ("zg", 0), ("zg", 2), ("zr", 0), ("zr", 2), ("v", 0)]
            return r if is_sample(b) else r + [("v", 1)]

        READER = {0: (gd_ok, 1), 1: (q_sb_ok, 1), 2: (k_sb_ok, 1), 3: (minx_ok, 2), 4: (z_ok, 1), 5: (z_ok, 2),
                  6: (z_ok, 3), 7: (z_ok, 4), 8: (v_ok, 1), 9: (v_ok, 2)}

        def wait_slot(pe, b, r):
            if r >= 3:
                s, k = READER[r - 3]
                pe.wait_ge(s.sem, s.at(b, k))
            elif not is_sample(b):
                for s in (v_ok, z_ok if r == 0 else r_ok):
                    pe.wait_ge(s.sem, s.at(b, 0))

        W_COL = {"q": C_Q, "k": C_K, "zg": C_ZG, "zr": C_ZR}

        def seg(b):
            return (SLEN, SLEN // 2 - 1) if is_sample(b) else (P, P // 2 - 1)

        block = ctx.enter_context(nc.Block())

        @block.sync
        def _(sp):
            def load_x(b, after_tr):
                for i in range(tiles(b)):
                    if is_sample(b):
                        src = t["x_sample"]
                    else:
                        if after_tr:
                            sp.wait_ge(tr_full.sem, tr_full.at(b - 1, 2 * (i + 1) if not is_sample(b - 1) else 2))
                        src = t["x_prompt"][(b - 1) * 2 + i]
                    sp.dma_start(x_tok[:, i, :], src).then_inc(*x_in[i].up(b))

            def body(b, has_next=True):
                n = tiles(b) * P
                sp.wait_ge(h_low.sem, h_low.at(b, 2 * tiles(b)))
                sp.dma_start(t["hT"][b][:, :, :, 0:n], hT[:, :, :, 0:n]).then_inc(*h_out.up(b))
                if has_next:
                    load_x(b + 1, True)
                sp.wait_ge(z_ok.sem, z_ok.at(b, 4))
                sp.dma_start(t["zr"][b][:, :, 0:n], zr[:, :, 0:n]).then_inc(*zr_out.up(b))
                for i in range(tiles(b)):
                    sp.wait_ge(ml_ok.sem, ml_ok.at(b, i + 1))
                    sp.dma_start(t["mg"][b][:, i], m_hl[:, :, :, :]).then_inc(*mg_out.up(b))
                if is_sample(b):
                    sp.wait_ge(s_ok.sem, s_ok.at(b, 2 * STREAMS))
                    sp.dma_start(t["gla_sample"], Ss[:, :, :, :]).then_inc(*st_out.up(b))

            load_x(0, False)
            body(0)
            with sp.Fori(1, LAST) as b:
                body(b)
            body(LAST, has_next=False)
            sp.wait_ge(s_ok.sem, s_ok.at(LAST, 4))
            sp.dma_start(t["gla_prompt"], S[:, :, :]).then_inc(st_out.sem, 16)
            sp.wait_ge(st_out.sem, 32)
            sp.wait_ge(h_out.sem, h_out.at(LAST, 1))
            sp.wait_ge(zr_out.sem, zr_out.at(LAST, 1))
            sp.wait_ge(mg_out.sem, mg_out.at(LAST, 2))

        @block.tensor
        def _(pe):
            def transpose_round(b, r):
                i, half = r // 2, r % 2
                pe.wait_ge(diag_ok.sem, diag_ok.at(b, i + 1))
                pe.wait_ge(x_in[i].sem, x_in[i].at(b, 1))
                if r >= 2:
                    pe.wait_ge(h_low.sem, h_low.at(b, r - 1))
                elif not is_sample(b):
                    pe.wait_ge(h_low.sem, h_low.at(b, 0))
                for k in range(4):
                    mm = pe.matmul(tr_bank[r % 2][:, k * P:(k + 1) * P],
                                   x_tok[:, i, (4 * half + k) * P:(4 * half + k + 1) * P], diag[:, i, :],
                                   start=True, stop=True)
                mm.then_inc(*tr_full.up(b))

            def product(out, lhs, rhs):
                for k in range(KT):
                    for n, (a, w) in enumerate(((0, 0), (1, 0), (0, 1))):
                        mm = pe.matmul(out, lhs(k, a, w), rhs(k, a, w),
                                       start=(k == 0 and n == 0), stop=(k == KT - 1 and n == 2))
                return mm

            def wcols(k, w, c0, n):
                return (w_hi, w_lo)[w][:, k, c0:c0 + n]

            def projection(b):
                n = tiles(b) * P
                pe.wait_ge(h_low.sem, h_low.at(b, 2 * tiles(b)))
                for r, (kind, g0) in enumerate(rounds(b)):
                    slot = r % 3
                    wait_slot(pe, b, r)
                    out = d_bank[slot]
                    if kind == "gd":
                        mm = product(out[0:16, 0:n], lambda k, a, w: wcols(k, w, C_GD, 16),
                                     lambda k, a, w: hT[:, a, k, 0:n])
                    elif kind == "up":
                        pe.wait_ge(gd_ok.sem, gd_ok.at(b, 1))
                        for g in range(2):
                            mm = pe.matmul(out[:, g * n:(g + 1) * n], a_up[:, g * P:(g + 1) * P], gd_sb[:, 0:n],
                                           start=True, stop=True)
                    elif kind == "v":
                        mm = product(out[:, :], lambda k, a, w: hT[:, a, k, g0 * P:(g0 + 1) * P],
                                     lambda k, a, w: wcols(k, w, C_V, 512))
                    else:
                        for g in range(2):
                            mm = product(out[:, g * n:(g + 1) * n],
                                         lambda k, a, w: wcols(k, w, W_COL[kind] + (g0 + g) * P, P),
                                         lambda k, a, w: hT[:, a, k, 0:n])
                    mm.then_inc(*d_full.up(b))

            def attention(b, i):
                pe.wait_ge(qk_ok.sem, qk_ok.at(b, 3))
                if i:
                    pe.wait_ge(att_ok.sem, att_ok.at(b, i))
                    pe.wait_ge(ssum_ok.sem, ssum_ok.at(b, i))
                elif not is_sample(b):
                    pe.wait_ge(att_ok.sem, att_ok.at(b, 0))
                    pe.wait_ge(ssum_ok.sem, ssum_ok.at(b, 0))
                for h in range(4):
                    pe.matmul(att[:, h, :], kd[:, h // 2, i * P:(i + 1) * P],
                              qd[:, h % 2, h // 2, i * P:(i + 1) * P], start=True, stop=True)
                for g in range(2):
                    mm = pe.transpose(kbank[:, 0, g, :], kd[:, g, i * P:(i + 1) * P], ident[:, :])
                mm.then_inc(*g1_full.up(b))

            def outputs(b, i):
                pe.wait_ge(att_ok.sem, att_ok.at(b, i + 1))
                pe.wait_ge(v_ok.sem, v_ok.at(b, i + 1))
                if i:
                    pe.wait_ge(o_ok.sem, o_ok.at(b, 2 * i))
                elif not is_sample(b):
                    pe.wait_ge(o_ok.sem, o_ok.at(b, 0))
                if is_sample(b):
                    pe.wait_ge(sd_ok.sem, sd_ok.at(b, 2 * STREAMS))
                else:
                    pe.wait_ge(sd_ok.sem, sd_ok.at(b, 2 * (i + 1)))
                for h in range(4):
                    for j in range(STREAMS if is_sample(b) else 1):
                        cols = slice(j * SLEN, (j + 1) * SLEN) if is_sample(b) else slice(0, P)
                        qcols = slice(i * P + cols.start, i * P + cols.stop)
                        start = Ss[:, j, h // 2, :] if is_sample(b) else Sd[:, h // 2, :]
                        pe.matmul(obank[:, h, cols], v_tok[:, i, h * P:(h + 1) * P], att_m[:, h, cols],
                                  start=True, stop=False)
                        mm = pe.matmul(obank[:, h, cols], start, qd[:, h % 2, h // 2, qcols],
                                       start=False, stop=True)
                mm.then_inc(*o_full.up(b))
                if not is_sample(b):
                    pe.wait_ge(ktok_ok.sem, ktok_ok.at(b, i + 1))
                for j in range(STREAMS if is_sample(b) else 1):
                    if is_sample(b):
                        pe.wait_ge(kseg_ok.sem, kseg_ok.at(b, j + 1))
                        if j:
                            pe.wait_ge(ssum_ok.sem, ssum_ok.at(b, j))
                    keys = k_seg if is_sample(b) else k_tok
                    for h in range(4):
                        rows = slice((h % 2) * 64, (h % 2) * 64 + 64)
                        mm = pe.matmul(kbank[rows, 1, h // 2, :], keys[:, h // 2, rows],
                                       v_tok[:, i, h * P:(h + 1) * P], start=True, stop=True)
                    mm.then_inc(*s_full.up(b))

            def mean_squares(b, i):
                slot = 1 + i
                s, k = READER[7 + i]
                pe.wait_ge(s.sem, s.at(b, k))
                pe.wait_ge(o_ok.sem, o_ok.at(b, 2 * i + 2))
                pe.matmul(d_bank[slot][:, :], ones_dv[:, :], o_sq[:, :, :], start=True,
                          stop=True).then_inc(*ms_full.up(b))

            def body(b, has_next=True):
                projection(b)
                attention(b, 0)
                if has_next:
                    transpose_round(b + 1, 0)
                outputs(b, 0)
                if has_next:
                    transpose_round(b + 1, 1)
                if not is_sample(b):
                    attention(b, 1)
                if has_next:
                    transpose_round(b + 1, 2)
                mean_squares(b, 0)
                if not is_sample(b):
                    outputs(b, 1)
                if has_next:
                    transpose_round(b + 1, 3)
                if not is_sample(b):
                    mean_squares(b, 1)

            transpose_round(0, 0)
            transpose_round(0, 1)
            body(0)
            with pe.Fori(1, LAST) as b:
                body(b)
            body(LAST, has_next=False)

        @block.scalar
        def _(act):
            def x_stats(b):
                for i in range(tiles(b)):
                    act.wait_ge(x_in[i].sem, x_in[i].at(b, 1))
                    act.activation(junk[:, :], x_tok[:, i, :], ACT.Square,
                                   accum_out=ssq[:, i:i + 1]).then_inc(*x_stat.up(b))
                    act.wait_ge(x_stat.sem, x_stat.at(b, 3 * i + 1))
                    act.activation(lnx[:, i:i + 1], ssq[:, i:i + 1], ACT.Ln, bias=const(K_RMS),
                                   scale=1.0 / D).then_inc(*x_stat.up(b))
                    act.wait_ge(x_stat.sem, x_stat.at(b, 3 * i + 2))
                    act.activation(rstd[:, i:i + 1], lnx[:, i:i + 1], ACT.Exp, bias=const(K_LNH),
                                   scale=-0.5).then_inc(*x_stat.up(b))

            def high_part(b, r):
                i, half = r // 2, r % 2
                act.wait_ge(tr_full.sem, tr_full.at(b, r + 1))
                if r == 0 and not is_sample(b):
                    act.wait_ge(h_out.sem, h_out.at(b, 0))
                act.activation(hT[:, 0, 4 * half:4 * half + 4, i * P:(i + 1) * P],
                               tr_bank[r % 2].rearrange("p (k t) -> p k t", k=4), ACT.Copy).then_inc(*h_high.up(b))

            def projection(b):
                n = tiles(b) * P
                L, mid = seg(b)
                for r, (kind, g0) in enumerate(rounds(b)):
                    bk = d_bank[r % 3]
                    pair = bk[:, 0:2 * n].rearrange("p (g t) -> p g t", g=2)
                    if kind != "k":
                        act.wait_ge(d_full.sem, d_full.at(b, r + 1))
                    if kind == "gd":
                        act.activation(gd_sb[:, 0:n], bk[0:16, 0:n], ACT.Copy, scale=UNSCALE).then_inc(*gd_ok.up(b))
                    elif kind == "q":
                        act.activation(q_sb[:, :, 0:n], pair, ACT.Copy, scale=UNSCALE * 0.125)\
                           .then_inc(*q_sb_ok.up(b))
                    elif kind == "up":
                        for g in range(2):
                            act.activation(absx[:, g, 0:n], pair[:, g, :], ACT.Abs,
                                           bias=pcol("gla_bias", g)).then_inc(*absx_ok.up(b))
                        act.wait_ge(absx_ok.sem, absx_ok.at(b, 2))
                        act.activation(absx[:, :, 0:n], absx[:, :, 0:n], ACT.Exp, scale=-1.0).then_inc(*ln_ok.up(b))
                        act.wait_ge(ln_ok.sem, ln_ok.at(b, 1))
                        act.activation(absx[:, :, 0:n], absx[:, :, 0:n], ACT.Ln, bias=const(K_ONE))\
                           .then_inc(*ln_ok.up(b))
                    elif kind in ("zg", "zr"):
                        k = g0 // 2 + (2 if kind == "zr" else 0)
                        if k == 0:
                            act.wait_ge(cum_ok.sem, cum_ok.at(b, 3))
                            act.activation(eb[:, :, 0:n], absx[:, :, 0:n], ACT.Exp, scale=1.0 / GLA_TEMP)\
                               .then_inc(*eb_ok.up(b))
                            act.activation(enb[:, :, 0:n], absx[:, :, 0:n], ACT.Exp, scale=-1.0 / GLA_TEMP)\
                               .then_inc(*eb_ok.up(b))
                            cview = cum[:, :, :].rearrange("p g t -> p (g t)")[:, 0:2 * n]\
                                .rearrange("p (g s l) -> p g s l", g=2, l=L)
                            aview = absx[:, :, 0:n].rearrange("p g (s l) -> p g s l", l=L)
                            ns = n // L
                            act.activation(dmid[:, :, 0:ns], cview[:, :, :, mid], ACT.Exp,
                                           scale=1.0 / GLA_TEMP).then_inc(*eb_ok.up(b))
                            act.activation(dlast[:, :, 0:ns], aview[:, :, :, L - 1], ACT.Exp,
                                           scale=1.0 / GLA_TEMP).then_inc(*eb_ok.up(b))
                        if k:
                            act.wait_ge(z_ok.sem, z_ok.at(b, k))
                        act.activation(th[:, :, 0:n], pair, ACT.Tanh, scale=0.5 * UNSCALE).then_inc(*th_ok.up(b))
                    elif kind == "v":
                        act.activation(v_tok[:, g0, :], bk[:, :], ACT.Copy, scale=UNSCALE).then_inc(*v_ok.up(b))

            def keys(b, i):
                act.wait_ge(g1_full.sem, g1_full.at(b, i + 1))
                act.activation(k_tok[:, :, :], kbank[:, 0], ACT.Copy).then_inc(*ktok_ok.up(b))

            def outputs(b, i):
                act.wait_ge(o_full.sem, o_full.at(b, i + 1))
                if i or not is_sample(b):
                    act.wait_ge(m_ok.sem, m_ok.at(b, 2 * i))
                act.activation(o_sq[:, :, :], obank, ACT.Square).then_inc(*o_ok.up(b))
                act.activation(o_sb[:, :, :], obank, ACT.Copy).then_inc(*o_ok.up(b))

            def rnorm(b, i):
                act.wait_ge(ms_full.sem, ms_full.at(b, i + 1))
                act.activation(r_o[:, :, :], d_bank[1 + i].rearrange("p (h t) -> p h t", h=4), ACT.Ln,
                               bias=const(K_RMS)).then_inc(*r_ok.up(b))
                act.wait_ge(r_ok.sem, r_ok.at(b, 2 * i + 1))
                act.activation(r_o[:, :, :], r_o[:, :, :], ACT.Exp, scale=-0.5).then_inc(*r_ok.up(b))

            def m_high(b, i):
                act.wait_ge(m_ok.sem, m_ok.at(b, 2 * i + 2))
                if i:
                    act.wait_ge(mg_out.sem, mg_out.at(b, i))
                elif not is_sample(b):
                    act.wait_ge(mg_out.sem, mg_out.at(b, 0))
                act.activation(m_hl[:, 0, :, :], mg[:, :, :], ACT.Copy).then_inc(*mh_ok.up(b))

            def body(b, has_next=True):
                projection(b)
                keys(b, 0)
                if has_next:
                    x_stats(b + 1)
                    high_part(b + 1, 0)
                outputs(b, 0)
                if has_next:
                    high_part(b + 1, 1)
                if not is_sample(b):
                    keys(b, 1)
                if has_next:
                    high_part(b + 1, 2)
                rnorm(b, 0)
                m_high(b, 0)
                if not is_sample(b):
                    outputs(b, 1)
                if has_next:
                    high_part(b + 1, 3)
                if not is_sample(b):
                    rnorm(b, 1)
                    m_high(b, 1)

            x_stats(0)
            high_part(0, 0)
            high_part(0, 1)
            body(0)
            with act.Fori(1, LAST) as b:
                body(b)
            body(LAST, has_next=False)

        @block.vector
        def _(dve):
            def make_diag(b):
                for i in range(tiles(b)):
                    dve.wait_ge(x_stat.sem, x_stat.at(b, 3 * i + 3))
                    if not is_sample(b):
                        dve.wait_ge(tr_full.sem, tr_full.at(b, 0))
                    dve.tensor_scalar(diag[:, i, :], ident[:, :], rstd[:, i:i + 1], None,
                                      ALU.mult).then_inc(*diag_ok.up(b))

            def low_part(b, r):
                i, half = r // 2, r % 2
                dve.wait_ge(h_high.sem, h_high.at(b, r + 1))
                view = (slice(None), slice(4 * half, 4 * half + 4), slice(i * P, (i + 1) * P))
                dve.tensor_tensor(hT[:, 1, 4 * half:4 * half + 4, i * P:(i + 1) * P],
                                  tr_bank[r % 2].rearrange("p (k t) -> p k t", k=4),
                                  hT[:, 0, 4 * half:4 * half + 4, i * P:(i + 1) * P],
                                  ALU.subtract).then_inc(*h_low.up(b))

            def projection(b):
                n = tiles(b) * P
                L, mid = seg(b)
                ns = 2 * n // L
                for r, (kind, g0) in enumerate(rounds(b)):
                    bk = d_bank[r % 3]
                    pair = bk[:, 0:2 * n].rearrange("p (g t) -> p g t", g=2)
                    if kind == "k":
                        dve.wait_ge(d_full.sem, d_full.at(b, r + 1))
                        dve.tensor_scalar(k_sb[:, :, 0:n], pair, UNSCALE, None, ALU.mult).then_inc(*k_sb_ok.up(b))
                    elif kind == "up":
                        dve.wait_ge(absx_ok.sem, absx_ok.at(b, 2))
                        for g in range(2):
                            dve.tensor_scalar(minx[:, g, 0:n], pair[:, g, :], pcol("gla_bias", g), 0.0,
                                              ALU.add, ALU.min)\
                               .then_inc(*minx_ok.up(b))
                        dve.wait_ge(minx_ok.sem, minx_ok.at(b, 2))
                        dve.wait_ge(ln_ok.sem, ln_ok.at(b, 2))
                        dve.tensor_tensor(minx[:, :, 0:n], minx[:, :, 0:n], absx[:, :, 0:n],
                                          ALU.subtract).then_inc(*minx_ok.up(b))
                        dve.wait_ge(minx_ok.sem, minx_ok.at(b, 3))
                        for g in range(2):
                            run = run_sample if is_sample(b) else run_prompt
                            dve.tensor_tensor_scan(cum[:, :, :].rearrange("p g t -> p (g t)")[:, g * n:(g + 1) * n],
                                                   run[:, 0:n], minx[:, g, 0:n], 0.0, ALU.mult,
                                                   ALU.add).then_inc(*cum_ok.up(b))
                        dve.wait_ge(cum_ok.sem, cum_ok.at(b, 2))
                        cview = cum[:, :, :].rearrange("p g t -> p (g t)")[:, 0:2 * n]\
                            .rearrange("p (g s l) -> p g s l", g=2, l=L)
                        aview = absx[:, :, 0:n].rearrange("p g (s l) -> p g s l", l=L)
                        dve.tensor_tensor(aview, cview, cview[:, :, :, mid:mid + 1].to_broadcast([P, 2, ns // 2, L]),
                                          ALU.subtract).then_inc(*cum_ok.up(b))
                    elif kind in ("zg", "zr"):
                        k = g0 // 2 + (2 if kind == "zr" else 0)
                        z = zg if kind == "zg" else zr
                        dve.wait_ge(th_ok.sem, th_ok.at(b, k + 1))
                        if kind == "zr" and not is_sample(b):
                            dve.wait_ge(zr_out.sem, zr_out.at(b, 0))
                        dve.scalar_tensor_tensor(out=z[:, g0:g0 + 2, 0:n], in0=th[:, :, 0:n], scalar=1.0, in1=pair,
                                                 op0=ALU.add, op1=ALU.mult).then_inc(*z_ok.up(b))
                        if k == 0:
                            dve.wait_ge(eb_ok.sem, eb_ok.at(b, 4))
                            dve.wait_ge(q_sb_ok.sem, q_sb_ok.at(b, 1))
                            dve.wait_ge(k_sb_ok.sem, k_sb_ok.at(b, 1))
                            for h in range(2):
                                rows = slice(64 * h, 64 * h + 64)
                                dve.tensor_tensor(qd[rows, h, :, 0:n], q_sb[rows, :, 0:n], eb[rows, :, 0:n],
                                                  ALU.mult).then_inc(*qk_ok.up(b))
                            dve.tensor_tensor(kd[:, :, 0:n], k_sb[:, :, 0:n], enb[:, :, 0:n],
                                              ALU.mult).then_inc(*qk_ok.up(b))
                            if is_sample(b):
                                for j in range(STREAMS):
                                    for g in range(2):
                                        dve.tensor_scalar(Ss[:, j, g, :], Ss[:, j, g, :], dmid[:, g, j:j + 1], None,
                                                          ALU.mult).then_inc(*sd_ok.up(b))

            def state_mid(b, i):
                for g in range(2):
                    dve.tensor_scalar(Sd[:, g, :], S[:, g, :], dmid[:, g, i:i + 1], None,
                                      ALU.mult).then_inc(*sd_ok.up(b))

            def mask(b, i):
                dve.wait_ge(g1_full.sem, g1_full.at(b, i + 1))
                m = mask_sample if is_sample(b) else mask_prompt
                dve.tensor_tensor(att_m[:, :, :], att, m[:, :].unsqueeze(1).to_broadcast([P, 4, P]),
                                  ALU.mult).then_inc(*att_ok.up(b))

            def state(b, i):
                if is_sample(b):
                    dve.wait_ge(ktok_ok.sem, ktok_ok.at(b, 1))
                    dve.wait_ge(o_full.sem, o_full.at(b, 1))
                    for j in range(STREAMS):
                        if j:
                            dve.wait_ge(s_full.sem, s_full.at(b, j))
                        dve.tensor_scalar(k_seg[:, :, :], k_tok[:, :, :], seg_rows[:, j:j + 1], None,
                                          ALU.mult).then_inc(*kseg_ok.up(b))
                        dve.wait_ge(s_full.sem, s_full.at(b, j + 1))
                        dve.tensor_tensor(Ss[:, j], kbank[:, 1], Ss[:, j], ALU.add).then_inc(*ssum_ok.up(b))
                        dve.wait_ge(ssum_ok.sem, ssum_ok.at(b, j + 1))
                        for g in range(2):
                            dve.tensor_scalar(Ss[:, j, g, :], Ss[:, j, g, :], dlast[:, g, j:j + 1], None,
                                              ALU.mult).then_inc(*s_ok.up(b))
                    return
                dve.wait_ge(s_full.sem, s_full.at(b, i + 1))
                dve.tensor_tensor(S[:, :, :], kbank[:, 1], Sd[:, :, :], ALU.add).then_inc(*ssum_ok.up(b))
                dve.wait_ge(ssum_ok.sem, ssum_ok.at(b, i + 1))
                for g in range(2):
                    dve.tensor_scalar(S[:, g, :], S[:, g, :], dlast[:, g, i:i + 1], None,
                                      ALU.mult).then_inc(*s_ok.up(b))
                dve.wait_ge(s_ok.sem, s_ok.at(b, 2 * i + 2))

            def gate(b, i):
                dve.wait_ge(r_ok.sem, r_ok.at(b, 2 * i + 2))
                if i or not is_sample(b):
                    dve.wait_ge(ml_ok.sem, ml_ok.at(b, i))
                dve.scalar_tensor_tensor(out=mg[:, :, :], in0=o_sb[:, :, :], scalar=g_norm[:, 0:1], in1=r_o[:, :, :],
                                         op0=ALU.mult, op1=ALU.mult).then_inc(*m_ok.up(b))
                dve.wait_ge(m_ok.sem, m_ok.at(b, 2 * i + 1))
                dve.tensor_tensor(mg[:, :, :], mg[:, :, :], zg[:, :, i * P:(i + 1) * P],
                                  ALU.mult).then_inc(*m_ok.up(b))
                dve.wait_ge(mh_ok.sem, mh_ok.at(b, i + 1))
                dve.tensor_tensor(m_hl[:, 1, :, :], mg[:, :, :], m_hl[:, 0, :, :],
                                  ALU.subtract).then_inc(*ml_ok.up(b))

            def body(b, has_next=True):
                projection(b)
                if not is_sample(b):
                    state_mid(b, 0)
                mask(b, 0)
                if has_next:
                    make_diag(b + 1)
                    low_part(b + 1, 0)
                state(b, 0)
                if has_next:
                    low_part(b + 1, 1)
                if not is_sample(b):
                    mask(b, 1)
                    state_mid(b, 1)
                if has_next:
                    low_part(b + 1, 2)
                gate(b, 0)
                if not is_sample(b):
                    state(b, 1)
                if has_next:
                    low_part(b + 1, 3)
                if not is_sample(b):
                    gate(b, 1)

            make_diag(0)
            low_part(0, 0)
            low_part(0, 1)
            body(0)
            with dve.Fori(1, LAST) as b:
                body(b)
            body(LAST, has_next=False)

        for s in signals:
            s.check()


CH = 64
INV = F32
N_RUN, N_MASKS = 3, 16

PE_HEAD = ["turn", "scores", "sq1", "sq2", "sq3", "sq4", "sq5", "sq6", "Z", "U"]
PE_STEPS = (PE_HEAD + ["state", "y"], PE_HEAD + ["y0", "y1", "y2", "y", "s0", "s1", "s2", "state"])
DVE_HEAD = ["B", "BT", "Y0a", "Y0", "Aqb", "Aak", "Aqk", "B1", "B2", "Y2", "B3", "Y3", "B4", "Y4", "Y5", "Y6a", "Y6b"]
DVE_STEPS = (DVE_HEAD + ["Z", "U", "Ssum", "S"],
             DVE_HEAD + ["Za", "Z0", "Z1", "Z2", "Z", "U"] + [f"e{j}{h}" for j in range(4) for h in "ab"]
             + [f"{k}{j}" for j in range(3) for k in ("u", "v", "sum", "S")] + ["u3", "v3", "Ssum", "S"])
ACT_STEPS = (["Vc", "Vt0", "Vt1", "betaT", "kappaT", "BT1", "BT2", "BT3", "BT4", "BT5", "U0", "U1", "y", "bdS0",
              "bdS1"],) * 2
SLOTS = 10

ROUNDS = ["x12", "x4", "x6", "lw0", "la0", "lw2", "la2", "kn0", "kn2", "x0", "x2", "x8", "x10"]
PIECES = [(r, h) for r, kind in enumerate(ROUNDS) for h in range(2 if kind[0] == "x" and kind != "x12" else 1)]


def rwkv_phase(nc, t, c):
    par, ident, consts = c["par"], c["ident"], c["consts"]

    def pcol(name, g=0):
        return par[:, PAR[name][0] + g:PAR[name][0] + g + 1]

    def const(k):
        return consts[:, k:k + 1]

    with ExitStack() as ctx:
        def sb(name, shape, dt=F32):
            return ctx.enter_context(nc.sbuf_tensor("r_" + name, shape, dt))

        def bank(name):
            return ctx.enter_context(nc.psum_tensor("r_" + name, [P, 512], F32))

        signals = []

        def sig(name, first, rest, step=1):
            s = Signal(ctx.enter_context(nc.semaphore("r_" + name)), name, first, rest, step)
            signals.append(s)
            return s

        w_hi = sb("w2_hi", [P, KT, W2_COLS], F16)
        w_lo = sb("w2_lo", [P, KT, W2_COLS], F16)
        o_hi = sb("wout_hi", [P, KT, D], F16)
        o_lo = sb("wout_lo", [P, KT, D], F16)
        up = sb("up", [P, 512])
        npost = sb("npost", [P, D])
        centre = sb("centre", [P, P])
        headsum = sb("headsum", [P, P])
        headmean = sb("headmean", [P, P])
        ident2 = sb("ident2", [P, CH])
        lt_bd = sb("lt_bd", [P, P], F16)
        gt_bd = sb("gt_bd", [P, P], F16)
        lt_c = sb("lt_c", [P, CH], F16)
        le_c = sb("le_c", [P, CH], F16)
        seg_rows = sb("seg_rows4", [P, 4])
        run = sb("run", [P, BLK], F16)
        sc = sb("sc", [P, 28])
        SC = {"w0h": 0, "a0h": 4, "nkk": 8, "kah": 12, "ka1": 16, "rk": 20, "lnw": 24}

        hT = sb("hT", [P, 2, KT, BLK], F16)
        praw = sb("praw", [P, 2, BLK + STREAMS])
        carry = sb("carry", [P, 13])
        carry_s = sb("carry_s", [P, 13, STREAMS])
        lor = sb("lor", [P, BLK])
        xm = sb("xm", [P, 12, BLK])
        scr = sb("scr", [P, 4, BLK])
        ta = sb("ta", [P, 4, BLK])
        kk = sb("kk", [P, 4, BLK])
        gam = sb("gam", [P, 4 * (BLK + 8)])
        gin = sb("gin", [P, 4, BLK])
        ar = sb("ar", [P, 4, 2, BLK])
        beta = sb("beta", [P, 4, BLK])
        kappa = sb("kappa", [P, 4, BLK])
        vv = sb("vv", [P, 4, BLK])
        bonus = sb("bonus", [P, 4, BLK])
        gL = sb("gL", [P, 4, 8])
        bdx = sb("bdx", [P, 4, 4, P])
        Aq = sb("Aq", [P, 2, 4, CH])
        bdAak = sb("bdAak", [P, 4, P])
        bdB = sb("bdB", [P, 4, P], INV)
        bdBT = sb("bdBT", [P, 4, P], INV)
        Yc = sb("Yc", [P, 4, CH], INV)
        bdY = bdBT
        bT = sb("bT", [P, 4, P])
        kT = sb("kT", [P, 4, P])
        Vc = sb("Vc", [P, 4, CH])
        bdV = sb("bdV", [P, 4, P])
        Zc = Yc
        Uc = sb("Uc", [P, 4, CH])
        bdU = bdAak
        S = sb("S", [P, 4, CH])
        bdS = sb("bdS", [P, 4, P])
        yT = sb("yT", [P, 2, 4, P])
        zr = sb("zr", [P, 4, P])
        m_hl = sb("m_hl", [P, 2, 2, 2, 4, P], F16)
        x_y = sb("x_y", [P, D])
        st = sb("st", [P, 8])

        d_bank = [bank("d0"), bank("d1")]
        R = [bank(f"R{i}") for i in range(5)]
        G = bank("G")
        Ss = x_y[:, :].rearrange("p (j g v) -> p j g v", j=4, g=4)

        def b4(ap, w=P):
            return ap.rearrange("p (g t) -> p g t", g=4)

        def half(r, k):
            return r[:, 256 * k:256 * k + 256].rearrange("p (g t) -> p g t", g=4)

        def blocks2(ap4):
            return ap4.rearrange("p g (a t) -> p g a t", a=2)

        def bc(ap, shape, at):
            return ap.unsqueeze(at).to_broadcast(shape)

        def par_s(name, g):
            return sc[:, SC[name] + g:SC[name] + g + 1]

        lnb_s = sb("lnb_s", [P, 4])

        def make_run(pool, done, l):
            done(pool.memset(run[:, :], 1.0))
            done(pool.memset(run[:, :].rearrange("p (c t) -> p c t", t=l)[:, :, 0:1], 0.0))

        def make_masks(pool, done, sample):
            for m in (lt_bd, gt_bd, lt_c, le_c):
                done(pool.memset(m[:, :], 1.0))
            for m in (lt_bd, gt_bd):
                done(pool.memset(m[0:64, 64:128], 0.0))
                done(pool.memset(m[64:128, 0:64], 0.0))
            for h in range(2):
                rows = slice(64 * h, 64 * h + 64)
                every = slice(0, CH)
                for m, cols, op, step in ((lt_bd, rows, ALU.is_gt, 1), (lt_c, every, ALU.is_gt, 1),
                                          (le_c, every, ALU.is_ge, 1), (gt_bd, rows, ALU.is_gt, -1)):
                    done(pool.affine_select(out=m[rows, cols], in_=m[rows, cols], compare_op=op, fill=0.0, base=0,
                                            pattern=[[step, CH]], channel_multiplier=-step))
            if not sample:
                return
            for h in range(2):
                rows = slice(64 * h, 64 * h + 64)
                for m, cols, base, step in ((lt_bd, rows, 0, -1), (lt_c, slice(0, CH), 0, -1),
                                            (le_c, slice(0, CH), 0, -1), (gt_bd, rows, SLEN - 1, 1)):
                    done(pool.affine_select(out=m[rows, cols], in_=m[rows, cols], compare_op=ALU.is_ge, fill=0.0,
                                            base=base, pattern=[[step * SLEN, 4], [0, SLEN]],
                                            channel_multiplier=-step))

        with ExitStack() as pre:
            w_in = [pre.enter_context(nc.semaphore(f"s_w2_in{i}")) for i in range(2)]
            w_high = pre.enter_context(nc.semaphore("s_w2_high"))
            w_split = pre.enter_context(nc.semaphore("s_w2_split"))
            small = pre.enter_context(nc.semaphore("s_small2"))
            scaled = pre.enter_context(nc.semaphore("s_scaled2"))
            pset = pre.enter_context(nc.semaphore("s_pool_set2"))
            nset = [0]
            stage = [xm[:, :, :].rearrange("p g t -> p (g t)"), ar[:, :, :, :].rearrange("p g a t -> p (g a t)")]
            gscale = carry_s[:, 0, :]
            block = pre.enter_context(nc.Block())

            @block.sync
            def _(sp):
                sp.dma_start(up[0:64, :], t["rwkv_w_up"]).then_inc(small, 16)
                sp.dma_start(up[64:128, :], t["rwkv_a_up"]).then_inc(small, 16)
                sp.dma_start(npost[:, :], t["norm_post"].to_broadcast([P, D])).then_inc(small, 16)
                for k in range(2 * KT):
                    if k >= 2:
                        sp.wait_ge(w_split, k - 1)
                    if k < KT:
                        src, n = t["w_in"][k * P:(k + 1) * P, GLA_COLS:GLA_COLS + SHIFT_W], W2_COLS
                    else:
                        src, n = t["w_out"][(k - KT) * P:(k - KT + 1) * P, :], D
                    sp.dma_start(stage[k % 2][:, 0:n], src).then_inc(w_in[k % 2], 16)
                sp.wait_ge(small, 48)

            @block.scalar
            def _(act):
                act.wait_ge(scaled, 1)
                for k in range(2 * KT):
                    act.wait_ge(w_in[k % 2], 16 * (k // 2 + 1))
                    if k < KT:
                        act.activation(w_hi[:, k, :], stage[k % 2][:, 0:W2_COLS], ACT.Identity,
                                       scale=gscale[:, k:k + 1]).then_inc(w_high, 1)
                    else:
                        act.activation(o_hi[:, k - KT, :], stage[k % 2][:, 0:D], ACT.Copy,
                                       scale=W_SCALE).then_inc(w_high, 1)

            @block.vector
            def _(dve):
                dve.tensor_scalar(gscale, par[:, 0:KT], W_SCALE, None, ALU.mult).then_inc(scaled, 1)
                dve.wait_ge(scaled, 1)
                n = 1
                cm = M_SCALE * UNSCALE * 0.5
                for dst, src, a, o in (("w0h", "w0", 0.5, None), ("a0h", "a0", 0.5, None), ("nkk", "k_k", -1.0, None),
                                       ("kah", "k_a", 0.5, None), ("ka1", "k_a", -0.5, 1.0), ("rk", "r_k", cm, None),
                                       ("lnw", "ln_w", cm, None)):
                    src = par[:, PAR[src][0]:PAR[src][0] + 4]
                    dst = sc[:, SC[dst]:SC[dst] + 4]
                    if o is None:
                        dve.tensor_scalar(dst, src, a, None, ALU.mult).then_inc(scaled, 1)
                    else:
                        dve.tensor_scalar(dst, src, a, o, ALU.mult, ALU.add).then_inc(scaled, 1)
                    n += 1
                dve.tensor_scalar(lnb_s[:, :], par[:, PAR["ln_b"][0]:PAR["ln_b"][0] + 4], cm, None,
                                  ALU.mult).then_inc(scaled, 1)
                for k in range(2 * KT):
                    dve.wait_ge(w_high, k + 1)
                    if k < KT:
                        dve.scalar_tensor_tensor(out=w_lo[:, k, :], in0=stage[k % 2][:, 0:W2_COLS],
                                                 scalar=gscale[:, k:k + 1], in1=w_hi[:, k, :],
                                                 op0=ALU.mult, op1=ALU.subtract).then_inc(w_split, 1)
                    else:
                        dve.scalar_tensor_tensor(out=o_lo[:, k - KT, :], in0=stage[k % 2][:, 0:D],
                                                 scalar=W_SCALE, in1=o_hi[:, k - KT, :],
                                                 op0=ALU.mult, op1=ALU.subtract).then_inc(w_split, 1)

            @block.gpsimd
            def _(pool):
                def done(ins):
                    ins.then_inc(pset, 1)
                    nset[0] += 1
                    pool.wait_ge(pset, nset[0])

                for m, v in ((headsum, 1.0), (headmean, 1.0 / CH), (ident2, 0.0), (seg_rows, 1.0), (carry, 0.0)):
                    done(pool.memset(m[:, :], v))
                for m in (bdV, bdS, S):
                    done(pool.memset(m[:, :, :], 0.0))
                done(pool.memset(gam[:, :], 1.0))
                for m in (headsum, headmean):
                    done(pool.memset(m[0:64, 64:128], 0.0))
                    done(pool.memset(m[64:128, 0:64], 0.0))
                done(pool.tensor_tensor(centre[:, :], ident[:, :], headmean[:, :], ALU.subtract))
                for h in range(2):
                    rows = slice(64 * h, 64 * h + 64)
                    done(pool.affine_select(out=ident2[rows, :], in_=ident2[rows, :], compare_op=ALU.not_equal,
                                            fill=1.0, base=0, pattern=[[-1, CH]], channel_multiplier=1))
                    done(pool.affine_select(out=seg_rows[rows, :], in_=seg_rows[rows, :], compare_op=ALU.is_ge,
                                            fill=0.0, base=0, pattern=[[-SLEN, 4]], channel_multiplier=1))
                for h in range(2):
                    rows = slice(64 * h, 64 * h + 64)
                    done(pool.affine_select(out=seg_rows[rows, :], in_=seg_rows[rows, :], compare_op=ALU.is_ge,
                                            fill=0.0, base=SLEN - 1, pattern=[[SLEN, 4]], channel_multiplier=-1))
                make_run(pool, done, SLEN)
                make_masks(pool, done, True)


        class Steps:

            def __init__(self, name, steps):
                self.steps = steps
                self.s = sig(name, 2 * len(steps[1]), 4 * len(steps[0]))

            def wait(self, eng, b, ch, step):
                steps = self.steps[is_sample(b)]
                eng.wait_ge(self.s.sem, self.s.at(b, ch * len(steps) + steps.index(step) + 1))

            def wait_prev(self, eng, b, ch, step):
                if ch:
                    self.wait(eng, b, ch - 1, step)
                elif not is_sample(b):
                    eng.wait_ge(self.s.sem, self.s.at(b, 0))

            def up(self, b):
                return self.s.up(b)

        pe_s = Steps("rec_pe", PE_STEPS)
        dve_s = Steps("rec_dve", DVE_STEPS)
        act_s = Steps("rec_act", ACT_STEPS)

        h_in = sig("h_in", 1, 1, 16)
        zr_in = sig("zr_in", 1, 2, 16)
        mg_in = [sig("mg_in0", 1, 1, 16), sig("mg_in1", 0, 1, 16)]
        xy_in = sig("xy_in", 1, 2, 16)
        y_out = sig("y_out", 1, 2, 16)
        ss_in = sig("ss_in", 2, 0, 16)
        ss_out = sig("ss_out", 2, 0, 16)
        sh_in = sig("sh_in", 1, 0, 16)
        ends = sig("ends_out", 0, 0, 16)
        remade = sig("remade", 0, 0)
        d_full = sig("d_full", 13, 13)
        praw_ok = sig("praw", 7, 7)
        mix_ok = sig("mix", 20, 20)
        carry_ok = sig("carry", 14, 14)
        th_ok = sig("th", 9, 9)
        dec_ok = sig("decay", 5, 5)
        gam_ok = sig("gamma", 2, 2)
        sq_ok = sig("kk_sq", 4, 4)
        clamp_ok = sig("clamp", 2, 2)
        rn_ok = sig("rnorm", 4, 4)
        kk_ok = sig("kk", 4, 4)
        kf_ok = sig("k_factor", 4, 4)
        kp_ok = sig("k_prime", 2, 2)
        rkk_ok = sig("rkk", 4, 4)
        op_ok = sig("operands", 4, 4)
        vv_ok = sig("v_operand", 2, 2)
        bd_ok = sig("bd", 8, 16)
        gc_full = sig("gc_full", 2, 4)
        gb_full = sig("gb_full", 2, 2)
        yc_ok = sig("y_centred", 2, 4)
        gr_ok = sig("y_rstd", 2, 4)
        post_ok = sig("post", 7, 14)
        mh_ok = sig("m_high", 1, 2)
        ml_ok = sig("m_low", 1, 2)
        bonus_ok = sig("bonus", 2, 2)
        o_full = sig("o_full", 1, 2)
        ss_ok = sig("y_stats", 4, 8)
        st_ok = sig("y_stat_sum", 1, 2)
        fin_ok = sig("y_done", 4, 8)

        def nchunks(b):
            return 2 if is_sample(b) else 4

        def L(b):
            return SLEN if is_sample(b) else CH

        def pieces_at(b, slot):
            n = SLOTS * nchunks(b) - 2
            return [p for p in range(len(PIECES)) if p * n // len(PIECES) == slot]

        def last_piece(p):
            return p + 1 == len(PIECES) or PIECES[p + 1][0] != PIECES[p][0]

        def gview(b, prev):
            n, l = tiles(b) * P, L(b)
            ns = n // l
            v = gam[:, 0:4 * ns * (l + 1)].rearrange("p (g s l) -> p g s l", g=4, l=l + 1)
            return v[:, :, :, 0:l] if prev else v[:, :, :, 1:l + 1]

        def segs(ap, l):
            return ap.rearrange("p g (s l) -> p g s l", l=l)

        junk = praw[:, :, :].rearrange("p g t -> p (g t)").bitcast(F16)

        def sq_view(i):
            return m_hl[:, i, 1].rearrange("p a k t -> p (a k t)").bitcast(F32)

        XROUNDS = [q for q in ROUNDS if q[0] == "x"]

        block = ctx.enter_context(nc.Block())

        @block.sync
        def _(sp):
            def load_h(b):
                n = tiles(b) * P
                if not is_sample(b):
                    sp.wait_ge(d_full.sem, d_full.at(b, 0))
                sp.dma_start(hT[:, :, :, 0:n], t["hT"][b][:, :, :, 0:n]).then_inc(*h_in.up(b))

            def load_zr(b, i):
                if i or not is_sample(b):
                    sp.wait_ge(post_ok.sem, post_ok.at(b, 7 * i))
                sp.dma_start(zr[:, :, :], t["zr"][b][:, :, i * P:(i + 1) * P]).then_inc(*zr_in.up(b))

            def load_x(b, i):
                if i or not is_sample(b):
                    sp.wait_ge(y_out.sem, y_out.at(b, i))
                src = t["x_sample"] if is_sample(b) else t["x_prompt"][(b - 1) * 2 + i]
                sp.dma_start(x_y[:, :], src).then_inc(*xy_in.up(b))

            def store_y(b, i):
                sp.wait_ge(fin_ok.sem, fin_ok.at(b, 4 * i + 4))
                dst = t["y_sample"] if is_sample(b) else t["y_prompt"][(b - 1) * 2 + i]
                sp.dma_start(dst, x_y[:, :]).then_inc(*y_out.up(b))

            def body(b, has_next=True):
                if has_next:
                    load_h(b + 1)
                for i in range(tiles(b)):
                    if not is_sample(b):
                        sp.wait_ge(o_full.sem, o_full.at(b, 0))
                    sp.dma_start(m_hl[:, i, 0], t["mg"][b][:, i]).then_inc(*mg_in[i].up(b))
                load_zr(b, 0)
                if is_sample(b):
                    for ch in range(2):
                        sp.dma_start(Ss, t["state_rwkv"][:, 4 * ch:4 * ch + 4]).then_inc(*ss_in.up(b))
                        dve_s.wait(sp, b, ch, "S")
                        sp.dma_start(t["rwkv_sample"][:, 4 * ch:4 * ch + 4], Ss).then_inc(*ss_out.up(b))
                        sp.wait_ge(ss_out.sem, ss_out.at(b, ch + 1))
                load_x(b, 0)
                if not is_sample(b):
                    load_zr(b, 1)
                store_y(b, 0)
                if not is_sample(b):
                    load_x(b, 1)
                    store_y(b, 1)

            sp.dma_start(carry_s[:, :, :], t["state_shift"]).then_inc(*sh_in.up(0))
            load_h(0)
            body(0)
            sp.wait_ge(carry_ok.sem, carry_ok.at(0, 14))
            sp.dma_start(t["shift_sample"], carry_s[:, :, :]).then_inc(ends.sem, 16)
            with sp.Fori(1, LAST) as b:
                body(b)
            body(LAST, has_next=False)
            sp.wait_ge(carry_ok.sem, carry_ok.at(LAST, 14))
            sp.dma_start(t["shift_prompt"], carry[:, :]).then_inc(ends.sem, 16)
            dve_s.wait(sp, LAST, 3, "S")
            sp.dma_start(t["rwkv_prompt"], S[:, :, :]).then_inc(ends.sem, 16)
            sp.wait_ge(ends.sem, 48)
            sp.wait_ge(y_out.sem, y_out.at(LAST, 2))

        @block.gpsimd
        def _(pool):
            def copies(b, ch):
                cols = slice(ch * CH, (ch + 1) * CH)
                if ch == 0:
                    pool.wait_ge(op_ok.sem, op_ok.at(b, 4))
                    pool.wait_ge(vv_ok.sem, vv_ok.at(b, 2))
                pe_s.wait_prev(pool, b, ch, "scores")
                for k, src in ((1, beta), (2, kappa), (3, vv), (0, ar)):
                    if k == 0:
                        pe_s.wait_prev(pool, b, ch, "Z")
                    s = src[:, :, 0, cols] if k == 0 else src[:, :, cols]
                    pool.tensor_tensor(blocks2(bdx[:, k]), bc(s, [P, 4, 2, CH], 2),
                                       bc(headsum[:, :].rearrange("p (a t) -> p a t", a=2), [P, 4, 2, CH], 1),
                                       ALU.mult).then_inc(*bd_ok.up(b))

            def body(b):
                for ch in range(nchunks(b)):
                    copies(b, ch)

            count = [0]

            def done(ins):
                ins.then_inc(remade.sem, 1)
                count[0] += 1
                pool.wait_ge(remade.sem, count[0])

            pool.wait_ge(dec_ok.sem, dec_ok.at(0, 5))
            make_run(pool, done, CH)
            pool.wait_ge(op_ok.sem, op_ok.at(0, 4))
            pool.wait_ge(vv_ok.sem, vv_ok.at(0, 2))
            ones = gam[:, 0:4 * 4 * (CH + 1)].rearrange("p (s l) -> p s l", l=CH + 1)[:, :, 0:1]
            done(pool.memset(ones, 1.0))
            REMADE_RUN = count[0]
            assert REMADE_RUN == N_RUN
            body(0)
            dve_s.wait(pool, 0, 1, "Aqk")
            make_masks(pool, done, False)
            assert count[0] == N_RUN + N_MASKS, count
            with pool.Fori(1, LAST) as b:
                body(b)
            body(LAST)

        @block.tensor
        def _(pe):
            def product(out, lhs, rhs):
                for k in range(KT):
                    for n, (a, w) in enumerate(((0, 0), (1, 0), (0, 1))):
                        mm = pe.matmul(out, lhs(k, a, w), rhs(k, a, w),
                                       start=(k == 0 and n == 0), stop=(k == KT - 1 and n == 2))
                return mm

            READER = {"x12": (praw_ok, 1), "x4": (praw_ok, 2), "x6": (praw_ok, 3), "lw0": (th_ok, 3),
                      "la0": (th_ok, 5), "lw2": (th_ok, 7), "la2": (th_ok, 9), "kn0": (kk_ok, 2), "kn2": (kk_ok, 4),
                      "x0": (praw_ok, 4), "x2": (praw_ok, 5), "x8": (praw_ok, 6), "x10": (praw_ok, 7)}

            def piece(b, p):
                r, h = PIECES[p]
                kind = ROUNDS[r]
                out = d_bank[r % 2]
                n = tiles(b) * P
                if r >= 2:
                    s, k = READER[ROUNDS[r - 2]]
                    pe.wait_ge(s.sem, s.at(b, k))
                elif not (isinstance(b, int) and b <= 1):
                    pe.wait_ge(fin_ok.sem, fin_ok.at(b - 1, 0))
                elif b == 1:
                    pe.wait_ge(praw_ok.sem, praw_ok.at(b, 0))
                if kind[0] == "x":
                    if r == 0:
                        pe.wait_ge(h_in.sem, h_in.at(b, 1))
                    g = int(kind[1:]) + h
                    mm = product(out[:, h * n:(h + 1) * n],
                                 lambda k, a, w: (w_hi, w_lo)[w][:, k, g * P:(g + 1) * P],
                                 lambda k, a, w: hT[:, a, k, 0:n])
                elif kind[0] == "l":
                    pe.wait_ge(th_ok.sem, th_ok.at(b, 1))
                    rows = slice(0, 64) if kind[1] == "w" else slice(64, 128)
                    g0 = int(kind[2])
                    for g in range(2):
                        mm = pe.matmul(out[:, g * n:(g + 1) * n], up[rows, (g0 + g) * P:(g0 + g + 1) * P],
                                       lor[rows, 0:n], start=True, stop=True)
                else:
                    g0 = int(kind[2])
                    pe.wait_ge(sq_ok.sem, sq_ok.at(b, g0 + 2))
                    for g in range(2):
                        mm = pe.matmul(out[:, g * n:(g + 1) * n], headsum[:, :], scr[:, g0 + g, 0:n],
                                       start=True, stop=True)
                if last_piece(p):
                    mm.then_inc(*d_full.up(b))

            def bd(k, g):
                return bdx[:, k, g, :]

            def turn(b, ch):
                pe.wait_ge(bd_ok.sem, bd_ok.at(b, 4 * ch + 3))
                dve_s.wait_prev(pe, b, ch, "U")
                act_s.wait_prev(pe, b, ch, "kappaT")
                for g in range(4):
                    pe.matmul(half(R[2], 0)[:, g, :], bd(3, g), ident2[:, :], start=True, stop=True)
                for g in range(4):
                    pe.transpose(R[0][:, g * P:(g + 1) * P], bd(1, g), ident[:, :])
                for g in range(4):
                    mm = pe.transpose(R[1][:, g * P:(g + 1) * P], bd(2, g), ident[:, :])
                mm.then_inc(*pe_s.up(b))

            def scores(b, ch):
                dve_s.wait_prev(pe, b, ch, "Ssum")
                act_s.wait_prev(pe, b, ch, "y")
                pe.wait_ge(bd_ok.sem, bd_ok.at(b, 4 * ch + 4))
                cols = slice(ch * CH, (ch + 1) * CH)
                for g in range(4):
                    pe.matmul(R[3][:, g * P:(g + 1) * P], bd(1, g), ar[:, g, :, cols], start=True, stop=True)
                for g in range(4):
                    pe.matmul(R[4][:, g * P:(g + 1) * P], bd(2, g), ar[:, g, :, cols], start=True, stop=True)
                act_s.wait(pe, b, ch, "Vc")
                for g in range(4):
                    mm = pe.matmul(half(R[2], 1)[:, g, :], bd(0, g), beta[:, g, cols], start=True, stop=True)
                mm.then_inc(*pe_s.up(b))

            def square(b, ch, j):
                if j == 1:
                    dve_s.wait(pe, b, ch, "Aqk")
                else:
                    if j <= 5:
                        dve_s.wait(pe, b, ch, "B%d" % (j - 1))
                    act_s.wait(pe, b, ch, "BT%d" % (j - 1))
                    if j >= 3:
                        dve_s.wait(pe, b, ch, "Y%d" % (j - 1))
                for g in range(4):
                    if j <= 4:
                        mm = pe.matmul(R[3][:, g * P:(g + 1) * P], bdBT[:, g, :], bdB[:, g, :], start=True, stop=True)
                    if j <= 5:
                        mm = pe.matmul(R[4][:, g * P:(g + 1) * P], bdB[:, g, :], bdBT[:, g, :], start=True, stop=True)
                    if j >= 2:
                        mm = pe.matmul(half(R[2], 1)[:, g, :], bdBT[:, g, :], Yc[:, g, :], start=True, stop=True)
                mm.then_inc(*pe_s.up(b))

            def solve(b, ch):
                act_s.wait(pe, b, ch, "kappaT")
                if is_sample(b):
                    act_s.wait(pe, b, ch, "BT5")
                    for g in range(4):
                        pe.matmul(half(R[0], 0)[:, g, :], bdAak[:, g, :], Vc[:, g, :], start=True, stop=True)
                    pe.wait_ge(ss_in.sem, ss_in.at(b, ch + 1))
                    for j in range(4):
                        for g in range(4):
                            mm = pe.matmul(half(R[3 + j // 2], j % 2)[:, g, :], bd(0, g), Ss[:, j, g, :],
                                           start=True, stop=True)
                else:
                    dve_s.wait_prev(pe, b, ch, "S")
                    for g in range(4):
                        pe.matmul(half(R[0], 0)[:, g, :], bdAak[:, g, :], Vc[:, g, :], start=True, stop=False)
                        mm = pe.matmul(half(R[0], 0)[:, g, :], bd(0, g), S[:, g, :], start=False, stop=True)
                mm.then_inc(*pe_s.up(b))

            def unknowns(b, ch):
                dve_s.wait(pe, b, ch, "Z")
                for g in range(4):
                    mm = pe.matmul(half(R[0], 1)[:, g, :], bdY[:, g, :], Zc[:, g, :], start=True, stop=True)
                mm.then_inc(*pe_s.up(b))

            def state(b, ch):
                dve_s.wait(pe, b, ch, "U")
                for j in range(4 if is_sample(b) else 1):
                    if is_sample(b):
                        dve_s.wait(pe, b, ch, "v%d" % j)
                    for g in range(4):
                        u = bdAak[:, g, 0:CH] if is_sample(b) else Uc[:, g, :]
                        v = bdAak[:, g, CH:P] if is_sample(b) else Vc[:, g, :]
                        pe.matmul(half(R[3], 0)[:, g, :], bT[:, g, :], u, start=True, stop=False)
                        mm = pe.matmul(half(R[3], 0)[:, g, :], kT[:, g, :], v, start=False, stop=True)
                    mm.then_inc(*pe_s.up(b))

            def outputs(b, ch):
                act_s.wait(pe, b, ch, "U1")
                if not is_sample(b):
                    act_s.wait_prev(pe, b, ch, "bdS1")
                for j in range(4 if is_sample(b) else 1):
                    if is_sample(b):
                        dve_s.wait(pe, b, ch, "e%db" % j)
                    w = SLEN if is_sample(b) else CH
                    cols = slice(j * w, (j + 1) * w)
                    for g in range(4):
                        out = half(R[4], 0)[:, g, cols]
                        pe.matmul(out, bdU[:, g, :], Aq[:, 0, g, cols], start=True, stop=False)
                        pe.matmul(out, bdV[:, g, :], Aq[:, 1, g, cols], start=False, stop=False)
                        mm = pe.matmul(out, bdS[:, g, :], ar[:, g, 1, ch * CH + cols.start:ch * CH + cols.stop],
                                       start=False, stop=True)
                    mm.then_inc(*pe_s.up(b))

            def group_norm(b, i):
                act_s.wait(pe, b, 2 * i + 1, "y")
                if i:
                    pe.wait_ge(post_ok.sem, post_ok.at(b, 1))
                else:
                    pe.wait_ge(bonus_ok.sem, bonus_ok.at(b, 2))
                pe.matmul(G[:, :], centre[:, :], yT[:, i], start=True, stop=True).then_inc(*gc_full.up(b))
                pe.wait_ge(yc_ok.sem, yc_ok.at(b, 2 * i + 2))
                pe.matmul(G[:, :], headmean[:, :], sq_view(i), start=True, stop=True).then_inc(*gc_full.up(b))

            def bonus_sums(b):
                n = tiles(b) * P
                for k in range(2):
                    pe.wait_ge(rkk_ok.sem, rkk_ok.at(b, 2 * k + 2))
                    if k:
                        pe.wait_ge(bonus_ok.sem, bonus_ok.at(b, 1))
                    elif not is_sample(b):
                        pe.wait_ge(post_ok.sem, post_ok.at(b, 0))
                    for g in range(2):
                        mm = pe.matmul(G[:, g * n:(g + 1) * n], headsum[:, :], scr[:, 2 * k + g, 0:n],
                                       start=True, stop=True)
                    mm.then_inc(*gb_full.up(b))

            def project_out(b, i, has_next):
                pe.wait_ge(mg_in[i].sem, mg_in[i].at(b, 1))
                pe.wait_ge(ml_ok.sem, ml_ok.at(b, i + 1))
                if i:
                    pe.wait_ge(fin_ok.sem, fin_ok.at(b, 3))
                elif has_next:
                    pe.wait_ge(praw_ok.sem, praw_ok.at(b + 1, 7))
                elif not is_sample(b):
                    pe.wait_ge(fin_ok.sem, fin_ok.at(b, 0))
                for col in range(2):
                    mm = product(d_bank[col][:, :], lambda k, a, w: m_hl[:, i, k // 4, a, k % 4, :],
                                 lambda k, a, w: (o_hi, o_lo)[w][:, k, col * 512:(col + 1) * 512])
                mm.then_inc(*o_full.up(b))

            def body(b, has_next=True):
                def fill(ch, k):
                    if has_next:
                        for p in pieces_at(b, ch * SLOTS + k):
                            piece(b + 1, p)

                for ch in range(nchunks(b)):
                    turn(b, ch)
                    fill(ch, 0)
                    scores(b, ch)
                    fill(ch, 1)
                    for j in range(1, 7):
                        square(b, ch, j)
                        fill(ch, 1 + j)
                    solve(b, ch)
                    fill(ch, 8)
                    unknowns(b, ch)
                    fill(ch, 9)
                    if is_sample(b):
                        outputs(b, ch)
                        state(b, ch)
                    else:
                        state(b, ch)
                        outputs(b, ch)
                    if ch % 2 == 1 and ch < nchunks(b) - 1:
                        group_norm(b, ch // 2)
                group_norm(b, tiles(b) - 1)
                if has_next:
                    bonus_sums(b + 1)
                for i in range(tiles(b)):
                    project_out(b, i, has_next)

            for p in range(len(PIECES)):
                piece(0, p)
            bonus_sums(0)
            body(0)
            with pe.Fori(1, LAST) as b:
                body(b)
            body(LAST, has_next=False)

        @block.scalar
        def _(act):
            def projected(b, r):
                kind = ROUNDS[r]
                n, l = tiles(b) * P, L(b)
                pair = d_bank[r % 2][:, 0:2 * n].rearrange("p (g t) -> p g t", g=2)
                if kind[0] == "x":
                    ng = 1 if kind == "x12" else 2
                    k = XROUNDS.index(kind)
                    act.wait_ge(d_full.sem, d_full.at(b, r + 1))
                    if k:
                        act.wait_ge(carry_ok.sem, carry_ok.at(b, 2 * k))
                    elif not is_sample(b):
                        act.wait_ge(carry_ok.sem, carry_ok.at(b, 0))
                        act.wait_ge(op_ok.sem, op_ok.at(b, 0))
                        act.wait_ge(bonus_ok.sem, bonus_ok.at(b, 0))
                        act.wait_ge(d_full.sem, d_full.at(b, 1))
                    if is_sample(b):
                        out = praw[:, 0:ng, 0:STREAMS * (SLEN + 1)].rearrange("p g (s l) -> p g s l", l=SLEN + 1)
                        out, src = out[:, :, :, 1:SLEN + 1], segs(pair[:, 0:ng, :], SLEN)
                    else:
                        out, src = praw[:, 0:ng, 1:n + 1], pair[:, 0:ng, :]
                    act.activation(out, src, ACT.Copy, scale=UNSCALE).then_inc(*praw_ok.up(b))
                    if kind == "x12":
                        act.wait_ge(mix_ok.sem, mix_ok.at(b, 2))
                        act.activation(lor[0:64, 0:n], lor[0:64, 0:n], ACT.Tanh).then_inc(*th_ok.up(b))
                elif kind[0] == "l":
                    act.wait_ge(d_full.sem, d_full.at(b, r + 1))
                    g0 = int(kind[2])
                    out, bias = (gin, "w0h") if kind[1] == "w" else (ta, "a0h")
                    for g in range(2):
                        act.activation(out[:, g0 + g, 0:n], pair[:, g, :], ACT.Tanh, scale=0.5,
                                       bias=par_s(bias, g0 + g)).then_inc(*th_ok.up(b))
                else:
                    g0 = int(kind[2])
                    act.wait_ge(clamp_ok.sem, clamp_ok.at(b, g0 // 2 + 1))
                    act.activation(pair, pair, ACT.Ln, scale=float(2 ** 20)).then_inc(*rn_ok.up(b))
                    act.wait_ge(rn_ok.sem, rn_ok.at(b, g0 + 1))
                    act.activation(pair, pair, ACT.Exp, scale=-0.5, bias=const(K_KK)).then_inc(*rn_ok.up(b))
                if kind in ("x4", "x6"):
                    g0 = int(kind[1]) - 4
                    for g in range(2):
                        act.wait_ge(mix_ok.sem, mix_ok.at(b, 2 + 3 * (g0 // 2) + 2 + g))
                        act.activation(scr[:, g0 + g, 0:n], xm[:, 4 + g0 + g, 0:n], ACT.Square,
                                       scale=pcol("k_k", g0 + g)).then_inc(*sq_ok.up(b))
                if kind == "la2":
                    act.wait_ge(dec_ok.sem, dec_ok.at(b, 5))
                    act.activation(gview(b, False), segs(gin[:, :, 0:n], l), ACT.Exp,
                                   scale=-0.5 * DECAY).then_inc(*gam_ok.up(b))
                    act.wait_ge(gam_ok.sem, gam_ok.at(b, 1))
                    act.activation(gin[:, :, 0:n], gin[:, :, 0:n], ACT.Exp, scale=0.5 * DECAY).then_inc(*gam_ok.up(b))

            def operands(b):
                n, l = tiles(b) * P, L(b)
                if not is_sample(b):
                    act.wait_ge(bd_ok.sem, bd_ok.at(b, 0))
                    dve_s.wait_prev(act, b, 0, "S")
                act.wait_ge(mix_ok.sem, mix_ok.at(b, 20))
                act.activation(vv[:, :, 0:n], xm[:, 8:12, 0:n], ACT.Copy).then_inc(*vv_ok.up(b))
                act.wait_ge(gam_ok.sem, gam_ok.at(b, 2))
                act.activation(gL[:, :, 0:n // l], gview(b, False)[:, :, :, l - 1], ACT.Copy).then_inc(*vv_ok.up(b))

            def turned(b, ch):
                pe_s.wait_prev(act, b, ch, "y")
                pe_s.wait(act, b, ch, "turn")
                act.activation(Vc[:, :, :], half(R[2], 0), ACT.Copy).then_inc(*act_s.up(b))
                act_s.wait(act, b, ch, "Vc")
                for h in range(2):
                    rows = slice(64 * h, 64 * h + 64)
                    act.activation(bdV[rows, :, rows], Vc[rows, :, :], ACT.Copy).then_inc(*act_s.up(b))
                act.activation(bT[:, :, :], b4(R[0]), ACT.Copy).then_inc(*act_s.up(b))
                act.activation(kT[:, :, :], b4(R[1]), ACT.Copy).then_inc(*act_s.up(b))

            def squared(b, ch, j):
                if j <= 5:
                    pe_s.wait(act, b, ch, "sq%d" % j)
                    act.activation(bdBT[:, :, :], b4(R[4]), ACT.Copy).then_inc(*act_s.up(b))

            def spread_u(b, ch):
                dve_s.wait(act, b, ch, "U")
                for h in range(2):
                    rows = slice(64 * h, 64 * h + 64)
                    act.activation(bdU[rows, :, rows], Uc[rows, :, :], ACT.Copy).then_inc(*act_s.up(b))

            def output(b, ch):
                pe_s.wait(act, b, ch, "y")
                i = ch // 2
                if ch % 2 == 0 and not is_sample(b):
                    act.wait_ge(ml_ok.sem, ml_ok.at(b, 0))
                act.activation(yT[:, i, :, (ch % 2) * CH:(ch % 2 + 1) * CH], half(R[4], 0), ACT.Copy)\
                    .then_inc(*act_s.up(b))
                dve_s.wait(act, b, ch, "S")
                for h in range(2):
                    rows = slice(64 * h, 64 * h + 64)
                    act.activation(bdS[rows, :, rows], S[rows, :, :], ACT.Copy).then_inc(*act_s.up(b))

            def group_norm(b, i):
                act.wait_ge(gc_full.sem, gc_full.at(b, 2 * i + 1))
                if not is_sample(b):
                    act.wait_ge(o_full.sem, o_full.at(b, 0))
                act.activation(sq_view(i), G[:, :], ACT.Square).then_inc(*yc_ok.up(b))
                act.activation(yT[:, i], b4(G), ACT.Copy).then_inc(*yc_ok.up(b))
                act.wait_ge(gc_full.sem, gc_full.at(b, 2 * i + 2))
                act.activation(G[:, :], G[:, :], ACT.Ln, bias=const(K_GN)).then_inc(*gr_ok.up(b))
                act.wait_ge(gr_ok.sem, gr_ok.at(b, 2 * i + 1))
                act.activation(G[:, :], G[:, :], ACT.Exp, scale=-0.5).then_inc(*gr_ok.up(b))
                act.wait_ge(post_ok.sem, post_ok.at(b, 7 * i + 7))
                act.activation(m_hl[:, i, 1, 0], yT[:, i], ACT.Copy).then_inc(*mh_ok.up(b))

            def out_stats(b, i, has_next):
                act.wait_ge(o_full.sem, o_full.at(b, i + 1))
                if i:
                    act.wait_ge(ss_ok.sem, ss_ok.at(b, 4))
                elif has_next:
                    act.wait_ge(carry_ok.sem, carry_ok.at(b + 1, 14))
                for h in range(2):
                    act.activation(junk[:, h * 512:(h + 1) * 512], d_bank[h][:, :], ACT.Square,
                                   accum_out=st[:, h:h + 1]).then_inc(*ss_ok.up(b))
                act.wait_ge(st_ok.sem, st_ok.at(b, i + 1))
                act.activation(st[:, 4:5], st[:, 4:5], ACT.Ln, scale=1.0 / (D * (M_SCALE * W_SCALE) ** 2),
                               bias=const(K_RMS)).then_inc(*ss_ok.up(b))
                act.wait_ge(ss_ok.sem, ss_ok.at(b, 4 * i + 3))
                act.activation(st[:, 5:6], st[:, 4:5], ACT.Exp, scale=-0.5, bias=const(K_LNM)).then_inc(*ss_ok.up(b))

            def body(b, has_next=True):
                def fill(ch, k):
                    if has_next:
                        for p in pieces_at(b, ch * SLOTS + k):
                            if last_piece(p):
                                projected(b + 1, PIECES[p][0])

                for ch in range(nchunks(b)):
                    turned(b, ch)
                    fill(ch, 0)
                    fill(ch, 1)
                    for j in range(1, 7):
                        squared(b, ch, j)
                        fill(ch, 1 + j)
                    fill(ch, 8)
                    spread_u(b, ch)
                    fill(ch, 9)
                    output(b, ch)
                    if ch % 2 == 1 and ch < nchunks(b) - 1:
                        group_norm(b, ch // 2)
                if has_next:
                    operands(b + 1)
                group_norm(b, tiles(b) - 1)
                for i in range(tiles(b)):
                    out_stats(b, i, has_next)

            for r in range(len(ROUNDS)):
                projected(0, r)
            operands(0)
            body(0)
            with act.Fori(1, LAST) as b:
                body(b)
            body(LAST, has_next=False)

        @block.vector
        def _(dve):
            def projected(b, r):
                kind = ROUNDS[r]
                n, l = tiles(b) * P, L(b)
                pair = d_bank[r % 2][:, 0:2 * n].rearrange("p (g t) -> p g t", g=2)
                if kind[0] == "x":
                    k = XROUNDS.index(kind)
                    ng, g0 = (1, 12) if kind == "x12" else (2, int(kind[1:]))
                    m0 = 0 if kind == "x12" else 2 + 3 * (k - 1)
                    out = lor[:, 0:n].unsqueeze(1) if kind == "x12" else xm[:, g0:g0 + 2, 0:n]
                    if is_sample(b):
                        raw = praw[:, 0:ng, 0:STREAMS * (SLEN + 1)].rearrange("p g (s l) -> p g s l", l=SLEN + 1)
                        front, last = raw[:, :, :, 0], raw[:, :, :, SLEN]
                        before, now = raw[:, :, :, 0:SLEN], raw[:, :, :, 1:SLEN + 1]
                        kept = carry_s[:, g0:g0 + ng, :]
                        out = segs(out, SLEN)
                        if k == 0:
                            dve.wait_ge(sh_in.sem, 16)
                    else:
                        front, last = praw[:, 0:ng, 0:1], praw[:, 0:ng, n:n + 1]
                        before, now = praw[:, 0:ng, 0:n], praw[:, 0:ng, 1:n + 1]
                        kept = carry[:, g0:g0 + ng].unsqueeze(2)
                    if k == 0 and not is_sample(b):
                        dve.wait_ge(d_full.sem, d_full.at(b, 0))
                        if not (isinstance(b, int) and b == 1):
                            dve.wait_ge(ss_ok.sem, ss_ok.at(b - 1, 0))
                    dve.tensor_copy(front, kept).then_inc(*carry_ok.up(b))
                    dve.wait_ge(carry_ok.sem, carry_ok.at(b, 2 * k + 1))
                    dve.wait_ge(praw_ok.sem, praw_ok.at(b, k + 1))
                    dve.tensor_tensor(out, before, now, ALU.subtract).then_inc(*mix_ok.up(b))
                    dve.wait_ge(mix_ok.sem, mix_ok.at(b, m0 + 1))
                    for g in range(ng):
                        dve.scalar_tensor_tensor(out=out[:, g], in0=out[:, g], scalar=pcol("mu", g0 + g),
                                                 in1=now[:, g], op0=ALU.mult, op1=ALU.add).then_inc(*mix_ok.up(b))
                    dve.wait_ge(mix_ok.sem, mix_ok.at(b, m0 + 1 + ng))
                    dve.tensor_copy(kept, last).then_inc(*carry_ok.up(b))
                elif kind[0] == "k":
                    g0 = int(kind[2])
                    dve.wait_ge(d_full.sem, d_full.at(b, r + 1))
                    dve.tensor_scalar(pair, pair, 1e-24, None, ALU.max).then_inc(*clamp_ok.up(b))
                    dve.wait_ge(rn_ok.sem, rn_ok.at(b, g0 + 2))
                    for g in range(2):
                        dve.scalar_tensor_tensor(out=kk[:, g0 + g, 0:n], in0=xm[:, 4 + g0 + g, 0:n],
                                                 scalar=par_s("nkk", g0 + g), in1=pair[:, g, :],
                                                 op0=ALU.mult, op1=ALU.mult).then_inc(*kk_ok.up(b))
                if kind == "la2":
                    dve.wait_ge(th_ok.sem, th_ok.at(b, 9))
                    dve.tensor_scalar(gin[:, :, 0:n], gin[:, :, 0:n], 1.0, None, ALU.add).then_inc(*dec_ok.up(b))
                    dve.wait_ge(dec_ok.sem, dec_ok.at(b, 1))
                    if isinstance(b, int) and b == 1:
                        dve.wait_ge(remade.sem, N_RUN)
                    for g in range(4):
                        dve.tensor_tensor_scan(gin[:, g, 0:n], run[:, 0:n], gin[:, g, 0:n], 0.0, ALU.mult,
                                               ALU.add).then_inc(*dec_ok.up(b))
                if kind == "kn2":
                    for g in range(4):
                        dve.tensor_scalar(scr[:, g, 0:n], ta[:, g, 0:n], par_s("kah", g), par_s("ka1", g),
                                          ALU.mult, ALU.add).then_inc(*kf_ok.up(b))
                    dve.wait_ge(kf_ok.sem, kf_ok.at(b, 4))
                    dve.wait_ge(kk_ok.sem, kk_ok.at(b, 4))
                    dve.tensor_tensor(xm[:, 4:8, 0:n], xm[:, 4:8, 0:n], scr[:, :, 0:n],
                                      ALU.mult).then_inc(*kp_ok.up(b))
                    dve.scalar_tensor_tensor(out=ta[:, :, 0:n], in0=ta[:, :, 0:n], scalar=1.0, in1=kk[:, :, 0:n],
                                             op0=ALU.add, op1=ALU.mult).then_inc(*kp_ok.up(b))
                if kind in ("x0", "x2"):
                    g0 = int(kind[1])
                    dve.wait_ge(kp_ok.sem, kp_ok.at(b, 2))
                    for g in (g0, g0 + 1):
                        dve.scalar_tensor_tensor(out=scr[:, g, 0:n], in0=xm[:, g, 0:n], scalar=par_s("rk", g),
                                                 in1=xm[:, 4 + g, 0:n], op0=ALU.mult, op1=ALU.mult)\
                           .then_inc(*rkk_ok.up(b))

            def operands(b):
                n, l = tiles(b) * P, L(b)
                dve.wait_ge(gam_ok.sem, gam_ok.at(b, 2))
                if not is_sample(b):
                    pe_s.wait_prev(dve, b, 0, "y")
                    dve.wait_ge(bd_ok.sem, bd_ok.at(b, 0))
                dve.wait_ge(mix_ok.sem, mix_ok.at(b, 20))
                dve.tensor_tensor(segs(ar[:, :, 0, 0:n], l), segs(kk[:, :, 0:n], l), gview(b, True),
                                  ALU.mult).then_inc(*op_ok.up(b))
                dve.tensor_tensor(segs(ar[:, :, 1, 0:n], l), segs(xm[:, 0:4, 0:n], l), gview(b, False),
                                  ALU.mult).then_inc(*op_ok.up(b))
                dve.tensor_tensor(kappa[:, :, 0:n], xm[:, 4:8, 0:n], gin[:, :, 0:n], ALU.mult).then_inc(*op_ok.up(b))
                dve.scalar_tensor_tensor(out=beta[:, :, 0:n], in0=ta[:, :, 0:n], scalar=-0.5, in1=gin[:, :, 0:n],
                                         op0=ALU.mult, op1=ALU.mult).then_inc(*op_ok.up(b))

            def masked(b, ch):
                pe_s.wait(dve, b, ch, "scores")
                if isinstance(b, int) and b == 1 or not isinstance(b, int):
                    if ch == 0:
                        dve.wait_ge(remade.sem, N_RUN + N_MASKS)

                def spread(out, src, mask):
                    return dve.tensor_tensor(blocks2(out[:, :, :]), bc(src, [P, 4, 2, CH], 2),
                                             bc(mask[:, :].rearrange("p (a t) -> p a t", a=2), [P, 4, 2, CH], 1),
                                             ALU.mult)

                spread(bdB, b4(R[3])[:, :, 0:CH], lt_bd).then_inc(*dve_s.up(b))
                spread(bdBT, half(R[2], 1), gt_bd).then_inc(*dve_s.up(b))
                dve.tensor_tensor(Yc[:, :, :], b4(R[3])[:, :, 0:CH], bc(lt_c[:, :], [P, 4, CH], 1),
                                  ALU.mult).then_inc(*dve_s.up(b))
                dve_s.wait(dve, b, ch, "Y0a")
                dve.tensor_tensor(Yc[:, :, :], Yc[:, :, :], bc(ident2[:, :], [P, 4, CH], 1),
                                  ALU.add).then_inc(*dve_s.up(b))
                dve.tensor_tensor(Aq[:, 0], b4(R[3])[:, :, CH:P], bc(le_c[:, :], [P, 4, CH], 1),
                                  ALU.mult).then_inc(*dve_s.up(b))
                spread(bdAak, b4(R[4])[:, :, 0:CH], lt_bd).then_inc(*dve_s.up(b))
                dve.tensor_tensor(Aq[:, 1], b4(R[4])[:, :, CH:P], bc(le_c[:, :], [P, 4, CH], 1),
                                  ALU.mult).then_inc(*dve_s.up(b))

            def squared(b, ch, j):
                pe_s.wait(dve, b, ch, "sq%d" % j)
                if j <= 4:
                    dve.tensor_copy(bdB[:, :, :], b4(R[3])).then_inc(*dve_s.up(b))
                if 2 <= j <= 5:
                    dve.tensor_tensor(Yc[:, :, :], half(R[2], 1), Yc[:, :, :], ALU.add).then_inc(*dve_s.up(b))
                if j == 6:
                    dve_s.wait(dve, b, ch, "Y5")
                    for h in range(2):
                        rows = slice(64 * h, 64 * h + 64)
                        dve.tensor_tensor(bdY[rows, :, rows], half(R[2], 1)[rows, :, :], Yc[rows, :, :],
                                          ALU.add).then_inc(*dve_s.up(b))

            def solved(b, ch):
                pe_s.wait(dve, b, ch, "Z")
                dve_s.wait(dve, b, ch, "Y6b")
                dve.tensor_copy(Zc[:, :, :], half(R[0], 0)).then_inc(*dve_s.up(b))
                if is_sample(b):
                    for j in range(4):
                        dve_s.wait(dve, b, ch, "Z%d" % (j - 1) if j else "Za")
                        dve.scalar_tensor_tensor(out=Zc[:, :, :], in0=half(R[3 + j // 2], j % 2),
                                                 scalar=seg_rows[:, j:j + 1], in1=Zc[:, :, :], op0=ALU.mult,
                                                 op1=ALU.add).then_inc(*dve_s.up(b))

            def states(b, ch):
                pe_s.wait(dve, b, ch, "U")
                dve.tensor_copy(Uc[:, :, :], half(R[0], 1)).then_inc(*dve_s.up(b))
                if not is_sample(b):
                    pe_s.wait(dve, b, ch, "state")
                    dve.tensor_tensor(S[:, :, :], half(R[3], 0), S[:, :, :], ALU.add).then_inc(*dve_s.up(b))
                    dve_s.wait(dve, b, ch, "Ssum")
                    if ch == 0:
                        dve.wait_ge(vv_ok.sem, vv_ok.at(b, 2))
                    if ch:
                        act_s.wait(dve, b, ch - 1, "bdS1")
                    dve.tensor_tensor(S[:, :, :], S[:, :, :], bc(gL[:, :, ch], [P, 4, CH], 2),
                                      ALU.mult).then_inc(*dve_s.up(b))
                    return
                for j in range(4):
                    if j:
                        pe_s.wait(dve, b, ch, "y%d" % (j - 1))
                    for h in range(2):
                        rows = slice(64 * h, 64 * h + 64)
                        dve.tensor_copy(bdS[rows, :, rows], Ss[rows, j]).then_inc(*dve_s.up(b))
                pe_s.wait(dve, b, ch, "y")
                dve.wait_ge(vv_ok.sem, vv_ok.at(b, 2))
                for j in range(4):
                    if j:
                        pe_s.wait(dve, b, ch, "s%d" % (j - 1))
                    dve_s.wait(dve, b, ch, "U")
                    for src, at in ((Uc, 0), (Vc, CH)):
                        dve.tensor_scalar(bdAak[:, :, at:at + CH], src[:, :, :], seg_rows[:, j:j + 1], None,
                                          ALU.mult).then_inc(*dve_s.up(b))
                    pe_s.wait(dve, b, ch, "s%d" % j if j < 3 else "state")
                    dve.tensor_tensor(Ss[:, j], half(R[3], 0), Ss[:, j], ALU.add).then_inc(*dve_s.up(b))
                    dve_s.wait(dve, b, ch, "sum%d" % j if j < 3 else "Ssum")
                    dve.tensor_tensor(Ss[:, j], Ss[:, j], bc(gL[:, :, 4 * ch + j], [P, 4, CH], 2),
                                      ALU.mult).then_inc(*dve_s.up(b))

            def gated(b, i):
                k = 7 * i
                y = yT[:, i]
                dve.wait_ge(gr_ok.sem, gr_ok.at(b, 2 * i + 2))
                dve.tensor_tensor(y, y, b4(G), ALU.mult).then_inc(*post_ok.up(b))
                dve.wait_ge(post_ok.sem, post_ok.at(b, k + 1))
                for g in range(4):
                    dve.tensor_scalar(y[:, g, :], y[:, g, :], par_s("lnw", g), lnb_s[:, g:g + 1], ALU.mult,
                                      ALU.add).then_inc(*post_ok.up(b))
                dve.wait_ge(post_ok.sem, post_ok.at(b, k + 5))
                dve.wait_ge(bonus_ok.sem, bonus_ok.at(b, 2))
                dve.tensor_tensor(y, y, bonus[:, :, i * P:(i + 1) * P], ALU.add).then_inc(*post_ok.up(b))
                dve.wait_ge(post_ok.sem, post_ok.at(b, k + 6))
                dve.wait_ge(zr_in.sem, zr_in.at(b, i + 1))
                dve.tensor_tensor(y, y, zr[:, :, :], ALU.mult).then_inc(*post_ok.up(b))
                dve.wait_ge(mh_ok.sem, mh_ok.at(b, i + 1))
                dve.tensor_tensor(m_hl[:, i, 1, 1], y, m_hl[:, i, 1, 0], ALU.subtract).then_inc(*ml_ok.up(b))

            def bonuses(b):
                n = tiles(b) * P
                for k in range(2):
                    dve.wait_ge(gb_full.sem, gb_full.at(b, k + 1))
                    dve.tensor_tensor(bonus[:, 2 * k:2 * k + 2, 0:n],
                                      G[:, 0:2 * n].rearrange("p (g t) -> p g t", g=2),
                                      xm[:, 8 + 2 * k:10 + 2 * k, 0:n], ALU.mult).then_inc(*bonus_ok.up(b))

            def finish(b, i):
                dve.wait_ge(ss_ok.sem, ss_ok.at(b, 4 * i + 2))
                dve.tensor_reduce(st[:, 4:5], st[:, 0:2], mybir.AxisListType.X, ALU.add).then_inc(*st_ok.up(b))
                dve.wait_ge(xy_in.sem, xy_in.at(b, i + 1))
                dve.wait_ge(ss_ok.sem, ss_ok.at(b, 4 * i + 4))
                for h in range(2):
                    tmp = scr[:, 2 * h:2 * h + 2, :].rearrange("p g t -> p (g t)")
                    dve.scalar_tensor_tensor(out=tmp, in0=d_bank[h][:, :], scalar=st[:, 5:6],
                                             in1=npost[:, h * 512:(h + 1) * 512], op0=ALU.mult,
                                             op1=ALU.mult).then_inc(*fin_ok.up(b))
                    dve.wait_ge(fin_ok.sem, fin_ok.at(b, 4 * i + 2 * h + 1))
                    dve.tensor_tensor(x_y[:, h * 512:(h + 1) * 512], tmp, x_y[:, h * 512:(h + 1) * 512],
                                      ALU.add).then_inc(*fin_ok.up(b))

            def body(b, has_next=True):
                def fill(ch, k):
                    if has_next:
                        for p in pieces_at(b, ch * SLOTS + k):
                            if last_piece(p):
                                projected(b + 1, PIECES[p][0])

                for ch in range(nchunks(b)):
                    fill(ch, 0)
                    masked(b, ch)
                    fill(ch, 1)
                    for j in range(1, 7):
                        squared(b, ch, j)
                        fill(ch, 1 + j)
                    solved(b, ch)
                    fill(ch, 8)
                    states(b, ch)
                    fill(ch, 9)
                    if ch % 2 == 1 and ch < nchunks(b) - 1:
                        gated(b, ch // 2)
                if has_next:
                    operands(b + 1)
                gated(b, tiles(b) - 1)
                if has_next:
                    bonuses(b + 1)
                for i in range(tiles(b)):
                    finish(b, i)

            for r in range(len(ROUNDS)):
                projected(0, r)
            operands(0)
            bonuses(0)
            body(0)
            with dve.Fori(1, LAST) as b:
                body(b)
            body(LAST, has_next=False)

        for s in signals:
            s.check()



def channels(a):
    return np.ascontiguousarray(a.reshape(-1, P).T)


def kernel(**inputs):
    from concourse import bacc
    from concourse.bass_utils import run_bass_kernel_spmd

    a = {k: np.asarray(v) for k, v in inputs.items()}
    mu = a["rwkv_mu"][0]
    ins = {
        "x_prompt": a["x_prompt"].reshape(SEQ // P, P, D),
        "x_sample": a["x_sample"].reshape(P, D),
        "w_in": a["w_in"][0],
        "w_out": a["w_out"][0],
        "gla_a_up": a["gla_a_up"][0],
        "rwkv_w_up": a["rwkv_w_up"][0],
        "rwkv_a_up": a["rwkv_a_up"][0],
        "norm_post": a["norm_post"],
        "state_gla": a["state_gla"][0].reshape(8, 2, 2, 64, 128).transpose(2, 3, 0, 1, 4).reshape(P, 8, 2, 128),
        "state_rwkv": a["state_rwkv"][0].reshape(8, 4, 2, 64, 64).transpose(2, 4, 0, 1, 3).reshape(P, 8, 4, 64),
        "state_shift": a["state_shift"][0].reshape(8, 13, P).transpose(2, 1, 0),
        "par": np.concatenate([channels(a[k]) for k in (
            "norm_pre", "gla_a_bias", "gla_norm", "rwkv_mu", "rwkv_w0", "rwkv_a0", "rwkv_k_k", "rwkv_k_a",
            "rwkv_r_k", "rwkv_ln_w", "rwkv_ln_b")], axis=1),
    }
    outs = {
        "y_prompt": (SEQ // P, P, D), "y_sample": (P, D),
        "gla_prompt": (P, 2, P), "gla_sample": (P, 8, 2, P),
        "rwkv_prompt": (P, 4, 64), "rwkv_sample": (P, 8, 4, 64),
        "shift_prompt": (P, 13), "shift_sample": (P, 13, 8),
    }
    scratch = {"hT": ((NB, P, 2, KT, BLK), F16), "zr": ((NB, P, 4, BLK), F32), "mg": ((NB, P, 2, 2, 4, P), F16)}
    nc = bacc.Bacc("TRN2", target_bir_lowering=False, num_devices=1)
    t, arrays = {}, {}
    for name, v in ins.items():
        arrays["in_" + name] = np.ascontiguousarray(v)
        t[name] = nc.dram_tensor("in_" + name, v.shape, mybir.dt.from_np(v.dtype), kind="ExternalInput").ap()
    for name, shape in outs.items():
        t[name] = nc.dram_tensor("out_" + name, shape, F32, kind="ExternalOutput").ap()
    for name, (shape, dt) in scratch.items():
        t[name] = nc.dram_tensor("scratch_" + name, shape, dt, kind="Internal").ap()
    build(nc, t)
    r = run_bass_kernel_spmd(nc, [arrays], core_ids=[0]).results[0]

    def heads(o, n):
        return o.reshape((2, 64) + o.shape[1:])

    gp = heads(r["out_gla_prompt"], 0).transpose(2, 0, 1, 3).reshape(1, 1, 4, 64, 128)
    gs = heads(r["out_gla_sample"], 0).transpose(2, 3, 0, 1, 4).reshape(1, 8, 4, 64, 128)
    rp = heads(r["out_rwkv_prompt"], 0).transpose(2, 0, 3, 1).reshape(1, 1, 8, 64, 64)
    rs = heads(r["out_rwkv_sample"], 0).transpose(2, 3, 0, 4, 1).reshape(1, 8, 8, 64, 64)
    return (r["out_y_prompt"].reshape(1, SEQ, D), r["out_y_sample"].reshape(8, 16, D), gp, gs, rp, rs,
            r["out_shift_prompt"].T.reshape(1, 1, SHIFT_W), r["out_shift_sample"].transpose(2, 1, 0).reshape(1, 8, SHIFT_W))
```

```python
from contextlib import ExitStack

import numpy as np

import concourse.bass as bass
from concourse import mybir

ALU = mybir.AluOpType
ACT = mybir.ActivationFunctionType
F32 = mybir.dt.float32
F16 = mybir.dt.float16

P = 128
D = 1024
KT = D // P
SEQ = 4096
BLK = 256
NB = 1 + SEQ // BLK
LAST = NB - 1
STREAMS, SLEN = 8, 16
SHIFT_W = 1664
GLA_COLS = 1552
RMS_EPS = 1e-6
GN_EPS = 64e-5
DECAY = 0.606531
GLA_TEMP = 16.0

H_SCALE = 64.0
W_SCALE = 256.0
M_SCALE = 16.0
UNSCALE = 1.0 / (H_SCALE * W_SCALE)

PAR = {}
for _name, _n in (("npre", 8), ("gla_bias", 2), ("gla_norm", 1), ("mu", 13), ("w0", 4), ("a0", 4),
                  ("k_k", 4), ("k_a", 4), ("r_k", 4), ("ln_w", 4), ("ln_b", 4)):
    PAR[_name] = (sum(n for _, n in PAR.values()), _n)
NPAR = sum(n for _, n in PAR.values())

C_Q, C_K, C_V, C_ZG, C_GD, C_ZR, W1_COLS = 0, 256, 512, 1024, 1536, 1552, 2064
W2_COLS = SHIFT_W


class Signal:

    def __init__(self, sem, name, first, rest, step=1):
        self.sem, self.name, self.first, self.rest, self.step = sem, name, first, rest, step
        self.seen = {}

    def at(self, b, k):
        if isinstance(b, int) and b == 0:
            return k * self.step
        return b * (self.rest * self.step) + (self.first - self.rest + k) * self.step

    def up(self, b):
        key = b if isinstance(b, int) else "loop"
        self.seen[key] = self.seen.get(key, 0) + 1
        return self.sem, self.step

    def check(self):
        for key, n in self.seen.items():
            assert n == (self.first if key == 0 else self.rest), (self.name, key, n)


def tiles(b):
    return 1 if isinstance(b, int) and b == 0 else BLK // P


def is_sample(b):
    return isinstance(b, int) and b == 0


def build(nc, t):
    with ExitStack() as ctx:
        def sb(name, shape, dt=F32):
            return ctx.enter_context(nc.sbuf_tensor(name, shape, dt))

        def sem(name):
            return ctx.enter_context(nc.semaphore(name))

        c = {}
        c["par"] = sb("par", [P, NPAR])
        c["ident"] = sb("ident", [P, P])
        c["consts"] = sb("consts", [P, 8])
        c["bar"] = sem("s_phase")
        setup(nc, t, c)
        gla_phase(nc, t, c)
        rwkv_phase(nc, t, c)


K_ONE, K_RMS, K_LNH, K_GN, K_LNM, K_KK = range(6)


def setup(nc, t, c):
    par, ident, consts = c["par"], c["ident"], c["consts"]
    with ExitStack() as ctx:
        loaded = ctx.enter_context(nc.semaphore("s_par_loaded"))
        zeroed = ctx.enter_context(nc.semaphore("s_ident_zeroed"))
        made = ctx.enter_context(nc.semaphore("s_ident_made"))
        block = ctx.enter_context(nc.Block())

        @block.sync
        def _(sp):
            sp.dma_start(par[:, :], t["par"]).then_inc(loaded, 16)
            sp.wait_ge(loaded, 16)

        @block.gpsimd
        def _(pool):
            pool.memset(ident[:, :], 0.0).then_inc(zeroed, 1)
            pool.wait_ge(zeroed, 1)
            pool.affine_select(out=ident[:, :], in_=ident[:, :], compare_op=ALU.not_equal, fill=1.0,
                               base=0, pattern=[[-1, P]], channel_multiplier=1).then_inc(made, 1)
            for k, v in ((K_ONE, 1.0), (K_RMS, RMS_EPS), (K_LNH, float(np.log(H_SCALE))), (K_GN, GN_EPS),
                         (K_LNM, -float(np.log(M_SCALE * W_SCALE))), (K_KK, 10 * float(np.log(2.0)))):
                pool.memset(consts[:, k:k + 1], v).then_inc(made, 1)
            pool.wait_ge(made, 7)


def gla_phase(nc, t, c):
    par, ident, consts = c["par"], c["ident"], c["consts"]

    def pcol(name, g=0):
        return par[:, PAR[name][0] + g:PAR[name][0] + g + 1]

    def const(k):
        return consts[:, k:k + 1]

    with ExitStack() as ctx:
        def sb(name, shape, dt=F32):
            return ctx.enter_context(nc.sbuf_tensor(name, shape, dt))

        def bank(name):
            return ctx.enter_context(nc.psum_tensor(name, [P, 512], F32))

        signals = []

        def sig(name, first, rest, step=1):
            s = Signal(ctx.enter_context(nc.semaphore("s_" + name)), name, first, rest, step)
            signals.append(s)
            return s

        w_hi = sb("w1_hi", [P, KT, W1_COLS], F16)
        w_lo = sb("w1_lo", [P, KT, W1_COLS], F16)
        stage = sb("w1_stage", [P, 2, W1_COLS])
        gscale = sb("gscale", [P, KT])
        a_up = sb("a_up", [16, 256])
        g_norm = sb("g_norm", [P, 1])
        ones_dv = sb("ones_dv", [P, P])
        mask_prompt = sb("mask_prompt", [P, P])
        mask_sample = sb("mask_sample", [P, P])
        seg_rows = sb("seg_rows", [P, STREAMS])
        run_prompt = sb("run_prompt", [P, 2 * BLK])
        run_sample = sb("run_sample", [P, 2 * P])
        x_tok = sb("x_tok", [P, 2, D])
        junk = sb("junk", [P, D], F16)
        ssq = sb("ssq", [P, 2])
        lnx = sb("lnx", [P, 2])
        rstd = sb("rstd", [P, 2])
        diag = sb("diag", [P, 2, P])
        hT = sb("hT", [P, 2, KT, BLK], F16)
        gd_sb = sb("gd_sb", [16, BLK])
        q_sb = sb("q_sb", [P, 2, BLK])
        k_sb = sb("k_sb", [P, 2, BLK])
        qd = sb("qd", [P, 2, 2, BLK])
        kd = sb("kd", [P, 2, BLK])
        v_tok = sb("v_tok", [P, 2, 512])
        zg = sb("zg", [P, 4, BLK])
        zr = sb("zr", [P, 4, BLK])
        th = sb("th", [P, 2, BLK])
        absx = sb("absx", [P, 2, BLK])
        minx = sb("minx", [P, 2, BLK])
        cum = sb("cum", [P, 2, BLK])
        eb = sb("eb", [P, 2, BLK])
        enb = sb("enb", [P, 2, BLK])
        dmid = sb("dmid", [P, 2, 8])
        dlast = sb("dlast", [P, 2, 8])
        S = sb("S", [P, 2, P])
        Sd = sb("Sd", [P, 2, P])
        Ss = sb("Ss", [P, STREAMS, 2, P])
        att_m = sb("att_m", [P, 4, P])
        k_tok = sb("k_tok", [P, 2, P])
        k_seg = sb("k_seg", [P, 2, P])
        o_sb = sb("o_sb", [P, 4, P])
        o_sq = sb("o_sq", [P, 4, P])
        r_o = sb("r_o", [P, 4, P])
        mg = sb("mg", [P, 4, P])
        m_hl = sb("m_hl", [P, 2, 4, P], F16)

        tr_bank = [bank("tr0"), bank("tr1")]
        d_bank = [bank("d0"), bank("d1"), bank("d2")]
        att = bank("att").rearrange("p (h t) -> p h t", h=4)
        obank = bank("obank").rearrange("p (h t) -> p h t", h=4)
        kbank = bank("kbank").rearrange("p (a g t) -> p a g t", a=2, g=2)

        with ExitStack() as pre:
            w_in = [pre.enter_context(nc.semaphore(f"s_w1_in{i}")) for i in range(2)]
            w_split = pre.enter_context(nc.semaphore("s_w1_split"))
            w_high = pre.enter_context(nc.semaphore("s_w1_high"))
            small = pre.enter_context(nc.semaphore("s_small_in"))
            scaled = pre.enter_context(nc.semaphore("s_scaled"))
            pset = pre.enter_context(nc.semaphore("s_pool_set"))
            block = pre.enter_context(nc.Block())

            @block.sync
            def _(sp):
                sp.dma_start(a_up[:, :], t["gla_a_up"]).then_inc(small, 16)
                sp.dma_start(Ss[:, :, :, :], t["state_gla"]).then_inc(small, 16)
                for k in range(KT):
                    if k >= 2:
                        sp.wait_ge(w_split, k - 1)
                    rows = t["w_in"][k * P:(k + 1) * P, :]
                    sp.dma_start(stage[:, k % 2, 0:GLA_COLS], rows[:, 0:GLA_COLS]).then_inc(w_in[k % 2], 16)
                    sp.dma_start(stage[:, k % 2, GLA_COLS:W1_COLS],
                                 rows[:, GLA_COLS + SHIFT_W:]).then_inc(w_in[k % 2], 16)
                sp.wait_ge(small, 32)

            @block.scalar
            def _(act):
                act.wait_ge(scaled, 1)
                for k in range(KT):
                    act.wait_ge(w_in[k % 2], 32 * (k // 2 + 1))
                    act.activation(w_hi[:, k, :], stage[:, k % 2, :], ACT.Identity,
                                   scale=gscale[:, k:k + 1]).then_inc(w_high, 1)

            @block.vector
            def _(dve):
                dve.tensor_scalar(gscale[:, :], par[:, 0:KT], W_SCALE, None, ALU.mult).then_inc(scaled, 1)
                dve.wait_ge(scaled, 1)
                dve.tensor_scalar(g_norm[:, :], pcol("gla_norm"), M_SCALE * UNSCALE * 0.5, None,
                                  ALU.mult).then_inc(scaled, 1)
                for k in range(KT):
                    dve.wait_ge(w_high, k + 1)
                    dve.scalar_tensor_tensor(out=w_lo[:, k, :], in0=stage[:, k % 2, :],
                                             scalar=gscale[:, k:k + 1], in1=w_hi[:, k, :],
                                             op0=ALU.mult, op1=ALU.subtract).then_inc(w_split, 1)

            @block.gpsimd
            def _(pool):
                n = 0
                for m, v in ((ones_dv, 1.0 / P), (mask_prompt, 1.0), (mask_sample, 1.0), (seg_rows, 1.0),
                             (run_prompt, 1.0), (run_sample, 1.0), (S, 0.0), (qd, 0.0)):
                    ap = m[:, :, :] if m is S else m[:, :, :, :] if m is qd else m[:, :]
                    pool.memset(ap, v).then_inc(pset, 1)
                    n += 1
                pool.wait_ge(pset, n)
                pool.affine_select(out=mask_prompt[:, :], in_=mask_prompt[:, :], compare_op=ALU.is_ge, fill=0.0,
                                   base=0, pattern=[[1, P]], channel_multiplier=-1).then_inc(pset, 1)
                pool.affine_select(out=mask_sample[:, :], in_=mask_sample[:, :], compare_op=ALU.is_ge, fill=0.0,
                                   base=0, pattern=[[1, P]], channel_multiplier=-1).then_inc(pset, 1)
                pool.affine_select(out=seg_rows[:, :], in_=seg_rows[:, :], compare_op=ALU.is_ge, fill=0.0,
                                   base=0, pattern=[[-SLEN, STREAMS]], channel_multiplier=1).then_inc(pset, 1)
                pool.memset(run_prompt[:, :].rearrange("p (c t) -> p c t", t=P)[:, :, 0:1], 0.0).then_inc(pset, 1)
                pool.memset(run_sample[:, :].rearrange("p (c t) -> p c t", t=SLEN)[:, :, 0:1], 0.0).then_inc(pset, 1)
                n += 5
                pool.wait_ge(pset, n)
                pool.affine_select(out=mask_sample[:, :], in_=mask_sample[:, :], compare_op=ALU.is_ge, fill=0.0,
                                   base=0, pattern=[[-SLEN, STREAMS], [0, SLEN]],
                                   channel_multiplier=1).then_inc(pset, 1)
                pool.affine_select(out=seg_rows[:, :], in_=seg_rows[:, :], compare_op=ALU.is_ge, fill=0.0,
                                   base=SLEN - 1, pattern=[[SLEN, STREAMS]], channel_multiplier=-1).then_inc(pset, 1)
                n += 2
                pool.wait_ge(pset, n)

        x_in = [sig("x_in0", 1, 1, 16), sig("x_in1", 0, 1, 16)]
        h_out = sig("h_out", 1, 1, 16)
        zr_out = sig("zr_out", 1, 1, 16)
        mg_out = sig("mg_out", 1, 2, 16)
        st_out = sig("gla_state_out", 1, 0, 16)
        x_stat = sig("x_stat", 3, 6)
        diag_ok = sig("diag", 1, 2)
        tr_full = sig("tr_full", 2, 4)
        h_high = sig("h_high", 2, 4)
        h_low = sig("h_low", 2, 4)
        d_full = sig("d_full", 9, 10)
        ms_full = sig("ms_full", 1, 2)
        gd_ok = sig("gd", 1, 1)
        absx_ok = sig("absx", 2, 2)
        minx_ok = sig("minx", 3, 3)
        ln_ok = sig("logsig", 2, 2)
        cum_ok = sig("cum", 3, 3)
        eb_ok = sig("eb", 4, 4)
        qk_ok = sig("qk_decayed", 3, 3)
        k_sb_ok = sig("k_sb", 1, 1)
        q_sb_ok = sig("q_sb", 1, 1)
        th_ok = sig("tanh", 4, 4)
        z_ok = sig("z_gated", 4, 4)
        v_ok = sig("v_tok", 1, 2)
        g1_full = sig("g1_full", 1, 2)
        att_ok = sig("att_masked", 1, 2)
        ktok_ok = sig("k_tok", 1, 2)
        sd_ok = sig("state_mid", 2 * STREAMS, 4)
        o_full = sig("o_full", 1, 2)
        s_full = sig("state_full", STREAMS, 2)
        kseg_ok = sig("k_seg", STREAMS, 0)
        ssum_ok = sig("state_sum", STREAMS, 2)
        s_ok = sig("state_ok", 2 * STREAMS, 4)
        o_ok = sig("o_sb", 2, 4)
        r_ok = sig("r_o", 2, 4)
        m_ok = sig("m_steps", 2, 4)
        mh_ok = sig("m_high", 1, 2)
        ml_ok = sig("m_low", 1, 2)

        def rounds(b):
            r = [("gd", 0), ("q", 0), ("k", 0), ("up", 0), ("zg", 0), ("zg", 2), ("zr", 0), ("zr", 2), ("v", 0)]
            return r if is_sample(b) else r + [("v", 1)]

        READER = {0: (gd_ok, 1), 1: (q_sb_ok, 1), 2: (k_sb_ok, 1), 3: (minx_ok, 2), 4: (z_ok, 1), 5: (z_ok, 2),
                  6: (z_ok, 3), 7: (z_ok, 4), 8: (v_ok, 1), 9: (v_ok, 2)}

        def wait_slot(pe, b, r):
            if r >= 3:
                s, k = READER[r - 3]
                pe.wait_ge(s.sem, s.at(b, k))
            elif not is_sample(b):
                for s in (v_ok, z_ok if r == 0 else r_ok):
                    pe.wait_ge(s.sem, s.at(b, 0))

        W_COL = {"q": C_Q, "k": C_K, "zg": C_ZG, "zr": C_ZR}

        def seg(b):
            return (SLEN, SLEN // 2 - 1) if is_sample(b) else (P, P // 2 - 1)

        block = ctx.enter_context(nc.Block())

        @block.sync
        def _(sp):
            def load_x(b, after_tr):
                for i in range(tiles(b)):
                    if is_sample(b):
                        src = t["x"][0]
                    else:
                        if after_tr:
                            sp.wait_ge(tr_full.sem, tr_full.at(b - 1, 2 * (i + 1) if not is_sample(b - 1) else 2))
                        src = t["x"][2 * b - 1 + i]
                    sp.dma_start(x_tok[:, i, :], src).then_inc(*x_in[i].up(b))

            def body(b, has_next=True):
                n = tiles(b) * P
                sp.wait_ge(h_low.sem, h_low.at(b, 2 * tiles(b)))
                sp.dma_start(t["hT"][b][:, :, :, 0:n], hT[:, :, :, 0:n]).then_inc(*h_out.up(b))
                if has_next:
                    load_x(b + 1, True)
                sp.wait_ge(z_ok.sem, z_ok.at(b, 4))
                sp.dma_start(t["zr"][b][:, :, 0:n], zr[:, :, 0:n]).then_inc(*zr_out.up(b))
                for i in range(tiles(b)):
                    sp.wait_ge(ml_ok.sem, ml_ok.at(b, i + 1))
                    sp.dma_start(t["mg"][b][:, i], m_hl[:, :, :, :]).then_inc(*mg_out.up(b))
                if is_sample(b):
                    sp.wait_ge(s_ok.sem, s_ok.at(b, 2 * STREAMS))
                    sp.dma_start(t["gla_sample"], Ss[:, :, :, :]).then_inc(*st_out.up(b))

            load_x(0, False)
            body(0)
            with sp.Fori(1, LAST) as b:
                body(b)
            body(LAST, has_next=False)
            sp.wait_ge(s_ok.sem, s_ok.at(LAST, 4))
            sp.dma_start(t["gla_prompt"], S[:, :, :]).then_inc(st_out.sem, 16)
            sp.wait_ge(st_out.sem, 32)
            sp.wait_ge(h_out.sem, h_out.at(LAST, 1))
            sp.wait_ge(zr_out.sem, zr_out.at(LAST, 1))
            sp.wait_ge(mg_out.sem, mg_out.at(LAST, 2))

        @block.tensor
        def _(pe):
            def transpose_round(b, r):
                i, half = r // 2, r % 2
                pe.wait_ge(diag_ok.sem, diag_ok.at(b, i + 1))
                pe.wait_ge(x_in[i].sem, x_in[i].at(b, 1))
                if r >= 2:
                    pe.wait_ge(h_low.sem, h_low.at(b, r - 1))
                elif not is_sample(b):
                    pe.wait_ge(h_low.sem, h_low.at(b, 0))
                for k in range(4):
                    mm = pe.matmul(tr_bank[r % 2][:, k * P:(k + 1) * P],
                                   x_tok[:, i, (4 * half + k) * P:(4 * half + k + 1) * P], diag[:, i, :],
                                   start=True, stop=True)
                mm.then_inc(*tr_full.up(b))

            def product(out, lhs, rhs):
                for k in range(KT):
                    for n, (a, w) in enumerate(((0, 0), (1, 0), (0, 1))):
                        mm = pe.matmul(out, lhs(k, a, w), rhs(k, a, w),
                                       start=(k == 0 and n == 0), stop=(k == KT - 1 and n == 2))
                return mm

            def wcols(k, w, c0, n):
                return (w_hi, w_lo)[w][:, k, c0:c0 + n]

            def projection(b):
                n = tiles(b) * P
                pe.wait_ge(h_low.sem, h_low.at(b, 2 * tiles(b)))
                for r, (kind, g0) in enumerate(rounds(b)):
                    slot = r % 3
                    wait_slot(pe, b, r)
                    out = d_bank[slot]
                    if kind == "gd":
                        mm = product(out[0:16, 0:n], lambda k, a, w: wcols(k, w, C_GD, 16),
                                     lambda k, a, w: hT[:, a, k, 0:n])
                    elif kind == "up":
                        pe.wait_ge(gd_ok.sem, gd_ok.at(b, 1))
                        for g in range(2):
                            mm = pe.matmul(out[:, g * n:(g + 1) * n], a_up[:, g * P:(g + 1) * P], gd_sb[:, 0:n],
                                           start=True, stop=True)
                    elif kind == "v":
                        mm = product(out[:, :], lambda k, a, w: hT[:, a, k, g0 * P:(g0 + 1) * P],
                                     lambda k, a, w: wcols(k, w, C_V, 512))
                    else:
                        for g in range(2):
                            mm = product(out[:, g * n:(g + 1) * n],
                                         lambda k, a, w: wcols(k, w, W_COL[kind] + (g0 + g) * P, P),
                                         lambda k, a, w: hT[:, a, k, 0:n])
                    mm.then_inc(*d_full.up(b))

            def attention(b, i):
                pe.wait_ge(qk_ok.sem, qk_ok.at(b, 3))
                if i:
                    pe.wait_ge(att_ok.sem, att_ok.at(b, i))
                    pe.wait_ge(ssum_ok.sem, ssum_ok.at(b, i))
                elif not is_sample(b):
                    pe.wait_ge(att_ok.sem, att_ok.at(b, 0))
                    pe.wait_ge(ssum_ok.sem, ssum_ok.at(b, 0))
                for h in range(4):
                    pe.matmul(att[:, h, :], kd[:, h // 2, i * P:(i + 1) * P],
                              qd[:, h % 2, h // 2, i * P:(i + 1) * P], start=True, stop=True)
                for g in range(2):
                    mm = pe.transpose(kbank[:, 0, g, :], kd[:, g, i * P:(i + 1) * P], ident[:, :])
                mm.then_inc(*g1_full.up(b))

            def outputs(b, i):
                pe.wait_ge(att_ok.sem, att_ok.at(b, i + 1))
                pe.wait_ge(v_ok.sem, v_ok.at(b, i + 1))
                if i:
                    pe.wait_ge(o_ok.sem, o_ok.at(b, 2 * i))
                elif not is_sample(b):
                    pe.wait_ge(o_ok.sem, o_ok.at(b, 0))
                if is_sample(b):
                    pe.wait_ge(sd_ok.sem, sd_ok.at(b, 2 * STREAMS))
                else:
                    pe.wait_ge(sd_ok.sem, sd_ok.at(b, 2 * (i + 1)))
                for h in range(4):
                    for j in range(STREAMS if is_sample(b) else 1):
                        cols = slice(j * SLEN, (j + 1) * SLEN) if is_sample(b) else slice(0, P)
                        qcols = slice(i * P + cols.start, i * P + cols.stop)
                        start = Ss[:, j, h // 2, :] if is_sample(b) else Sd[:, h // 2, :]
                        pe.matmul(obank[:, h, cols], v_tok[:, i, h * P:(h + 1) * P], att_m[:, h, cols],
                                  start=True, stop=False)
                        mm = pe.matmul(obank[:, h, cols], start, qd[:, h % 2, h // 2, qcols],
                                       start=False, stop=True)
                mm.then_inc(*o_full.up(b))
                if not is_sample(b):
                    pe.wait_ge(ktok_ok.sem, ktok_ok.at(b, i + 1))
                for j in range(STREAMS if is_sample(b) else 1):
                    if is_sample(b):
                        pe.wait_ge(kseg_ok.sem, kseg_ok.at(b, j + 1))
                        if j:
                            pe.wait_ge(ssum_ok.sem, ssum_ok.at(b, j))
                    keys = k_seg if is_sample(b) else k_tok
                    for h in range(4):
                        rows = slice((h % 2) * 64, (h % 2) * 64 + 64)
                        mm = pe.matmul(kbank[rows, 1, h // 2, :], keys[:, h // 2, rows],
                                       v_tok[:, i, h * P:(h + 1) * P], start=True, stop=True)
                    mm.then_inc(*s_full.up(b))

            def mean_squares(b, i):
                slot = 1 + i
                s, k = READER[7 + i]
                pe.wait_ge(s.sem, s.at(b, k))
                pe.wait_ge(o_ok.sem, o_ok.at(b, 2 * i + 2))
                pe.matmul(d_bank[slot][:, :], ones_dv[:, :], o_sq[:, :, :], start=True,
                          stop=True).then_inc(*ms_full.up(b))

            def body(b, has_next=True):
                projection(b)
                attention(b, 0)
                if has_next:
                    transpose_round(b + 1, 0)
                outputs(b, 0)
                if has_next:
                    transpose_round(b + 1, 1)
                if not is_sample(b):
                    attention(b, 1)
                if has_next:
                    transpose_round(b + 1, 2)
                mean_squares(b, 0)
                if not is_sample(b):
                    outputs(b, 1)
                if has_next:
                    transpose_round(b + 1, 3)
                if not is_sample(b):
                    mean_squares(b, 1)

            transpose_round(0, 0)
            transpose_round(0, 1)
            body(0)
            with pe.Fori(1, LAST) as b:
                body(b)
            body(LAST, has_next=False)

        @block.scalar
        def _(act):
            def x_stats(b):
                for i in range(tiles(b)):
                    act.wait_ge(x_in[i].sem, x_in[i].at(b, 1))
                    act.activation(junk[:, :], x_tok[:, i, :], ACT.Square,
                                   accum_out=ssq[:, i:i + 1]).then_inc(*x_stat.up(b))
                    act.wait_ge(x_stat.sem, x_stat.at(b, 3 * i + 1))
                    act.activation(lnx[:, i:i + 1], ssq[:, i:i + 1], ACT.Ln, bias=const(K_RMS),
                                   scale=1.0 / D).then_inc(*x_stat.up(b))
                    act.wait_ge(x_stat.sem, x_stat.at(b, 3 * i + 2))
                    act.activation(rstd[:, i:i + 1], lnx[:, i:i + 1], ACT.Exp, bias=const(K_LNH),
                                   scale=-0.5).then_inc(*x_stat.up(b))

            def high_part(b, r):
                i, half = r // 2, r % 2
                act.wait_ge(tr_full.sem, tr_full.at(b, r + 1))
                if r == 0 and not is_sample(b):
                    act.wait_ge(h_out.sem, h_out.at(b, 0))
                act.activation(hT[:, 0, 4 * half:4 * half + 4, i * P:(i + 1) * P],
                               tr_bank[r % 2].rearrange("p (k t) -> p k t", k=4), ACT.Copy).then_inc(*h_high.up(b))

            def projection(b):
                n = tiles(b) * P
                L, mid = seg(b)
                for r, (kind, g0) in enumerate(rounds(b)):
                    bk = d_bank[r % 3]
                    pair = bk[:, 0:2 * n].rearrange("p (g t) -> p g t", g=2)
                    if kind != "k":
                        act.wait_ge(d_full.sem, d_full.at(b, r + 1))
                    if kind == "gd":
                        act.activation(gd_sb[:, 0:n], bk[0:16, 0:n], ACT.Copy, scale=UNSCALE).then_inc(*gd_ok.up(b))
                    elif kind == "q":
                        act.activation(q_sb[:, :, 0:n], pair, ACT.Copy, scale=UNSCALE * 0.125)\
                           .then_inc(*q_sb_ok.up(b))
                    elif kind == "up":
                        for g in range(2):
                            act.activation(absx[:, g, 0:n], pair[:, g, :], ACT.Abs,
                                           bias=pcol("gla_bias", g)).then_inc(*absx_ok.up(b))
                        act.wait_ge(absx_ok.sem, absx_ok.at(b, 2))
                        act.activation(absx[:, :, 0:n], absx[:, :, 0:n], ACT.Exp, scale=-1.0).then_inc(*ln_ok.up(b))
                        act.wait_ge(ln_ok.sem, ln_ok.at(b, 1))
                        act.activation(absx[:, :, 0:n], absx[:, :, 0:n], ACT.Ln, bias=const(K_ONE))\
                           .then_inc(*ln_ok.up(b))
                    elif kind in ("zg", "zr"):
                        k = g0 // 2 + (2 if kind == "zr" else 0)
                        if k == 0:
                            act.wait_ge(cum_ok.sem, cum_ok.at(b, 3))
                            act.activation(eb[:, :, 0:n], absx[:, :, 0:n], ACT.Exp, scale=1.0 / GLA_TEMP)\
                               .then_inc(*eb_ok.up(b))
                            act.activation(enb[:, :, 0:n], absx[:, :, 0:n], ACT.Exp, scale=-1.0 / GLA_TEMP)\
                               .then_inc(*eb_ok.up(b))
                            cview = cum[:, :, :].rearrange("p g t -> p (g t)")[:, 0:2 * n]\
                                .rearrange("p (g s l) -> p g s l", g=2, l=L)
                            aview = absx[:, :, 0:n].rearrange("p g (s l) -> p g s l", l=L)
                            ns = n // L
                            act.activation(dmid[:, :, 0:ns], cview[:, :, :, mid], ACT.Exp,
                                           scale=1.0 / GLA_TEMP).then_inc(*eb_ok.up(b))
                            act.activation(dlast[:, :, 0:ns], aview[:, :, :, L - 1], ACT.Exp,
                                           scale=1.0 / GLA_TEMP).then_inc(*eb_ok.up(b))
                        if k:
                            act.wait_ge(z_ok.sem, z_ok.at(b, k))
                        act.activation(th[:, :, 0:n], pair, ACT.Tanh, scale=0.5 * UNSCALE).then_inc(*th_ok.up(b))
                    elif kind == "v":
                        act.activation(v_tok[:, g0, :], bk[:, :], ACT.Copy, scale=UNSCALE).then_inc(*v_ok.up(b))

            def keys(b, i):
                act.wait_ge(g1_full.sem, g1_full.at(b, i + 1))
                act.activation(k_tok[:, :, :], kbank[:, 0], ACT.Copy).then_inc(*ktok_ok.up(b))

            def outputs(b, i):
                act.wait_ge(o_full.sem, o_full.at(b, i + 1))
                if i or not is_sample(b):
                    act.wait_ge(m_ok.sem, m_ok.at(b, 2 * i))
                act.activation(o_sq[:, :, :], obank, ACT.Square).then_inc(*o_ok.up(b))
                act.activation(o_sb[:, :, :], obank, ACT.Copy).then_inc(*o_ok.up(b))

            def rnorm(b, i):
                act.wait_ge(ms_full.sem, ms_full.at(b, i + 1))
                act.activation(r_o[:, :, :], d_bank[1 + i].rearrange("p (h t) -> p h t", h=4), ACT.Ln,
                               bias=const(K_RMS)).then_inc(*r_ok.up(b))
                act.wait_ge(r_ok.sem, r_ok.at(b, 2 * i + 1))
                act.activation(r_o[:, :, :], r_o[:, :, :], ACT.Exp, scale=-0.5).then_inc(*r_ok.up(b))

            def m_high(b, i):
                act.wait_ge(m_ok.sem, m_ok.at(b, 2 * i + 2))
                if i:
                    act.wait_ge(mg_out.sem, mg_out.at(b, i))
                elif not is_sample(b):
                    act.wait_ge(mg_out.sem, mg_out.at(b, 0))
                act.activation(m_hl[:, 0, :, :], mg[:, :, :], ACT.Copy).then_inc(*mh_ok.up(b))

            def body(b, has_next=True):
                projection(b)
                keys(b, 0)
                if has_next:
                    x_stats(b + 1)
                    high_part(b + 1, 0)
                outputs(b, 0)
                if has_next:
                    high_part(b + 1, 1)
                if not is_sample(b):
                    keys(b, 1)
                if has_next:
                    high_part(b + 1, 2)
                rnorm(b, 0)
                m_high(b, 0)
                if not is_sample(b):
                    outputs(b, 1)
                if has_next:
                    high_part(b + 1, 3)
                if not is_sample(b):
                    rnorm(b, 1)
                    m_high(b, 1)

            x_stats(0)
            high_part(0, 0)
            high_part(0, 1)
            body(0)
            with act.Fori(1, LAST) as b:
                body(b)
            body(LAST, has_next=False)

        @block.vector
        def _(dve):
            def make_diag(b):
                for i in range(tiles(b)):
                    dve.wait_ge(x_stat.sem, x_stat.at(b, 3 * i + 3))
                    if not is_sample(b):
                        dve.wait_ge(tr_full.sem, tr_full.at(b, 0))
                    dve.tensor_scalar(diag[:, i, :], ident[:, :], rstd[:, i:i + 1], None,
                                      ALU.mult).then_inc(*diag_ok.up(b))

            def low_part(b, r):
                i, half = r // 2, r % 2
                dve.wait_ge(h_high.sem, h_high.at(b, r + 1))
                view = (slice(None), slice(4 * half, 4 * half + 4), slice(i * P, (i + 1) * P))
                dve.tensor_tensor(hT[:, 1, 4 * half:4 * half + 4, i * P:(i + 1) * P],
                                  tr_bank[r % 2].rearrange("p (k t) -> p k t", k=4),
                                  hT[:, 0, 4 * half:4 * half + 4, i * P:(i + 1) * P],
                                  ALU.subtract).then_inc(*h_low.up(b))

            def projection(b):
                n = tiles(b) * P
                L, mid = seg(b)
                ns = 2 * n // L
                for r, (kind, g0) in enumerate(rounds(b)):
                    bk = d_bank[r % 3]
                    pair = bk[:, 0:2 * n].rearrange("p (g t) -> p g t", g=2)
                    if kind == "k":
                        dve.wait_ge(d_full.sem, d_full.at(b, r + 1))
                        dve.tensor_scalar(k_sb[:, :, 0:n], pair, UNSCALE, None, ALU.mult).then_inc(*k_sb_ok.up(b))
                    elif kind == "up":
                        dve.wait_ge(absx_ok.sem, absx_ok.at(b, 2))
                        for g in range(2):
                            dve.tensor_scalar(minx[:, g, 0:n], pair[:, g, :], pcol("gla_bias", g), 0.0,
                                              ALU.add, ALU.min)\
                               .then_inc(*minx_ok.up(b))
                        dve.wait_ge(minx_ok.sem, minx_ok.at(b, 2))
                        dve.wait_ge(ln_ok.sem, ln_ok.at(b, 2))
                        dve.tensor_tensor(minx[:, :, 0:n], minx[:, :, 0:n], absx[:, :, 0:n],
                                          ALU.subtract).then_inc(*minx_ok.up(b))
                        dve.wait_ge(minx_ok.sem, minx_ok.at(b, 3))
                        for g in range(2):
                            run = run_sample if is_sample(b) else run_prompt
                            dve.tensor_tensor_scan(cum[:, :, :].rearrange("p g t -> p (g t)")[:, g * n:(g + 1) * n],
                                                   run[:, 0:n], minx[:, g, 0:n], 0.0, ALU.mult,
                                                   ALU.add).then_inc(*cum_ok.up(b))
                        dve.wait_ge(cum_ok.sem, cum_ok.at(b, 2))
                        cview = cum[:, :, :].rearrange("p g t -> p (g t)")[:, 0:2 * n]\
                            .rearrange("p (g s l) -> p g s l", g=2, l=L)
                        aview = absx[:, :, 0:n].rearrange("p g (s l) -> p g s l", l=L)
                        dve.tensor_tensor(aview, cview, cview[:, :, :, mid:mid + 1].to_broadcast([P, 2, ns // 2, L]),
                                          ALU.subtract).then_inc(*cum_ok.up(b))
                    elif kind in ("zg", "zr"):
                        k = g0 // 2 + (2 if kind == "zr" else 0)
                        z = zg if kind == "zg" else zr
                        dve.wait_ge(th_ok.sem, th_ok.at(b, k + 1))
                        if kind == "zr" and not is_sample(b):
                            dve.wait_ge(zr_out.sem, zr_out.at(b, 0))
                        dve.scalar_tensor_tensor(out=z[:, g0:g0 + 2, 0:n], in0=th[:, :, 0:n], scalar=1.0, in1=pair,
                                                 op0=ALU.add, op1=ALU.mult).then_inc(*z_ok.up(b))
                        if k == 0:
                            dve.wait_ge(eb_ok.sem, eb_ok.at(b, 4))
                            dve.wait_ge(q_sb_ok.sem, q_sb_ok.at(b, 1))
                            dve.wait_ge(k_sb_ok.sem, k_sb_ok.at(b, 1))
                            for h in range(2):
                                rows = slice(64 * h, 64 * h + 64)
                                dve.tensor_tensor(qd[rows, h, :, 0:n], q_sb[rows, :, 0:n], eb[rows, :, 0:n],
                                                  ALU.mult).then_inc(*qk_ok.up(b))
                            dve.tensor_tensor(kd[:, :, 0:n], k_sb[:, :, 0:n], enb[:, :, 0:n],
                                              ALU.mult).then_inc(*qk_ok.up(b))
                            if is_sample(b):
                                for j in range(STREAMS):
                                    for g in range(2):
                                        dve.tensor_scalar(Ss[:, j, g, :], Ss[:, j, g, :], dmid[:, g, j:j + 1], None,
                                                          ALU.mult).then_inc(*sd_ok.up(b))

            def state_mid(b, i):
                for g in range(2):
                    dve.tensor_scalar(Sd[:, g, :], S[:, g, :], dmid[:, g, i:i + 1], None,
                                      ALU.mult).then_inc(*sd_ok.up(b))

            def mask(b, i):
                dve.wait_ge(g1_full.sem, g1_full.at(b, i + 1))
                m = mask_sample if is_sample(b) else mask_prompt
                dve.tensor_tensor(att_m[:, :, :], att, m[:, :].unsqueeze(1).to_broadcast([P, 4, P]),
                                  ALU.mult).then_inc(*att_ok.up(b))

            def state(b, i):
                if is_sample(b):
                    dve.wait_ge(ktok_ok.sem, ktok_ok.at(b, 1))
                    dve.wait_ge(o_full.sem, o_full.at(b, 1))
                    for j in range(STREAMS):
                        if j:
                            dve.wait_ge(s_full.sem, s_full.at(b, j))
                        dve.tensor_scalar(k_seg[:, :, :], k_tok[:, :, :], seg_rows[:, j:j + 1], None,
                                          ALU.mult).then_inc(*kseg_ok.up(b))
                        dve.wait_ge(s_full.sem, s_full.at(b, j + 1))
                        dve.tensor_tensor(Ss[:, j], kbank[:, 1], Ss[:, j], ALU.add).then_inc(*ssum_ok.up(b))
                        dve.wait_ge(ssum_ok.sem, ssum_ok.at(b, j + 1))
                        for g in range(2):
                            dve.tensor_scalar(Ss[:, j, g, :], Ss[:, j, g, :], dlast[:, g, j:j + 1], None,
                                              ALU.mult).then_inc(*s_ok.up(b))
                    return
                dve.wait_ge(s_full.sem, s_full.at(b, i + 1))
                dve.tensor_tensor(S[:, :, :], kbank[:, 1], Sd[:, :, :], ALU.add).then_inc(*ssum_ok.up(b))
                dve.wait_ge(ssum_ok.sem, ssum_ok.at(b, i + 1))
                for g in range(2):
                    dve.tensor_scalar(S[:, g, :], S[:, g, :], dlast[:, g, i:i + 1], None,
                                      ALU.mult).then_inc(*s_ok.up(b))
                dve.wait_ge(s_ok.sem, s_ok.at(b, 2 * i + 2))

            def gate(b, i):
                dve.wait_ge(r_ok.sem, r_ok.at(b, 2 * i + 2))
                if i or not is_sample(b):
                    dve.wait_ge(ml_ok.sem, ml_ok.at(b, i))
                dve.scalar_tensor_tensor(out=mg[:, :, :], in0=o_sb[:, :, :], scalar=g_norm[:, 0:1], in1=r_o[:, :, :],
                                         op0=ALU.mult, op1=ALU.mult).then_inc(*m_ok.up(b))
                dve.wait_ge(m_ok.sem, m_ok.at(b, 2 * i + 1))
                dve.tensor_tensor(mg[:, :, :], mg[:, :, :], zg[:, :, i * P:(i + 1) * P],
                                  ALU.mult).then_inc(*m_ok.up(b))
                dve.wait_ge(mh_ok.sem, mh_ok.at(b, i + 1))
                dve.tensor_tensor(m_hl[:, 1, :, :], mg[:, :, :], m_hl[:, 0, :, :],
                                  ALU.subtract).then_inc(*ml_ok.up(b))

            def body(b, has_next=True):
                projection(b)
                if not is_sample(b):
                    state_mid(b, 0)
                mask(b, 0)
                if has_next:
                    make_diag(b + 1)
                    low_part(b + 1, 0)
                state(b, 0)
                if has_next:
                    low_part(b + 1, 1)
                if not is_sample(b):
                    mask(b, 1)
                    state_mid(b, 1)
                if has_next:
                    low_part(b + 1, 2)
                gate(b, 0)
                if not is_sample(b):
                    state(b, 1)
                if has_next:
                    low_part(b + 1, 3)
                if not is_sample(b):
                    gate(b, 1)

            make_diag(0)
            low_part(0, 0)
            low_part(0, 1)
            body(0)
            with dve.Fori(1, LAST) as b:
                body(b)
            body(LAST, has_next=False)

        for s in signals:
            s.check()


CH = 64
INV = F32
N_RUN, N_MASKS = 3, 19

PE_HEAD = ["turn", "scores", "turnk", "sq1", "sq2", "sq3", "sq4", "sq5", "sq6", "Z", "U"]
PE_STEPS = (PE_HEAD + ["state", "y"], PE_HEAD + ["y0", "y1", "y2", "y", "s0", "s1", "s2", "state"])
DVE_HEAD = ["BT", "PT", "B", "PB", "Y0", "Aqb", "Aak", "Aqk", "B1", "P1", "B2", "P2", "Y2", "B3", "P3", "Y3",
            "B4", "P4", "Y4", "Y5", "Y6a", "Y6b"]
DVE_STEPS = (DVE_HEAD + ["Z", "U", "Ssum", "S"],
             DVE_HEAD + ["Za", "Z0", "Z1", "Z2", "Z", "U"] + [f"e{j}{h}" for j in range(4) for h in "ab"]
             + [f"{k}{j}" for j in range(3) for k in ("u", "v", "sum", "S")] + ["u3", "v3", "Ssum", "S"])
ACT_STEPS = (["Vc", "Vt0", "Vt1", "betaT", "kappaT"] + [f"BT{j}{h}" for j in range(1, 6) for h in "abp"]
             + ["U0", "U1", "y", "bdS0", "bdS1"],) * 2
LN_SET = "natural_log_exp_and_others"
SLOTS = 11
LIGHT = (0, 1)
PE_JOBS = ("centre", "variance", "out", "bonus_sum0", "bonus_sum1", "piece")

ROUNDS = ["x12", "x4", "lw0", "x6", "la0", "lw2", "la2", "x0", "kn0", "x2", "kn2", "x8", "x10"]
PIECES = []
for _r, _kind in enumerate(ROUNDS):
    if _kind[0] == "x":
        _n = 1 if _kind == "x12" else 2
        PIECES += [(_r, _h, _third, _h == _n - 1 and _third == 2) for _h in range(_n) for _third in range(3)]
    else:
        PIECES.append((_r, 0, 0, True))


class Tile:

    def __init__(self, b, off):
        self.b, self.off, self.i = b, off, 1 - off % 2

    def index(self):
        return 2 * self.b + self.off


class TileSignal(Signal):

    def __init__(self, sem, name, n, step=1):
        super().__init__(sem, name, n, 2 * n, step)
        self.n = n

    def at(self, tile, k):
        return tile.b * (2 * self.n * self.step) + (tile.off * self.n + k) * self.step

    def up(self, tile):
        key = (tile.b if isinstance(tile.b, int) else "loop", tile.off)
        self.seen[key] = self.seen.get(key, 0) + 1
        return self.sem, self.step

    def check(self):
        for key, n in self.seen.items():
            assert n == self.n, (self.name, key, n)


def rwkv_phase(nc, t, c):
    par, ident, consts = c["par"], c["ident"], c["consts"]

    def pcol(name, g=0):
        return par[:, PAR[name][0] + g:PAR[name][0] + g + 1]

    def const(k):
        return consts[:, k:k + 1]

    with ExitStack() as ctx:
        def sb(name, shape, dt=F32):
            return ctx.enter_context(nc.sbuf_tensor("r_" + name, shape, dt))

        def bank(name):
            return ctx.enter_context(nc.psum_tensor("r_" + name, [P, 512], F32))

        signals = []

        def sig(name, first, rest, step=1):
            s = Signal(ctx.enter_context(nc.semaphore("r_" + name)), name, first, rest, step)
            signals.append(s)
            return s

        w_hi = sb("w2_hi", [P, KT, W2_COLS], F16)
        w_lo = sb("w2_lo", [P, KT, W2_COLS], F16)
        o_hi = sb("wout_hi", [P, KT, D], F16)
        o_lo = sb("wout_lo", [P, KT, D], F16)
        up = sb("up", [P, 512])
        npost = sb("npost", [P, D])
        centre = sb("centre", [P, P])
        headsum = sb("headsum", [P, P])
        headmean = sb("headmean", [P, P])
        ident2 = sb("ident2", [P, CH])
        lt_bd = sb("lt_bd", [P, P], F16)
        gt_bd = sb("gt_bd", [P, P], F16)
        lt_c = sb("lt_c", [P, CH], F16)
        le_c = sb("le_c", [P, CH], F16)
        gt_c = sb("gt_c", [P, CH], F16)
        seg_rows = sb("seg_rows4", [P, 4])
        run = sb("run", [P, BLK], F16)
        sc = sb("sc", [P, 28])
        SC = {"w0h": 0, "a0h": 4, "nkk": 8, "kah": 12, "ka1": 16, "rk": 20, "lnw": 24}

        hT = sb("hT", [P, 2, KT, BLK], F16)
        praw = sb("praw", [P, 2, BLK + STREAMS])
        carry = sb("carry", [P, 13])
        carry_s = sb("carry_s", [P, 13, STREAMS])
        lor = sb("lor", [P, BLK])
        xm = sb("xm", [P, 12, BLK])
        scr = sb("scr", [P, 4, BLK])
        ta = sb("ta", [P, 4, BLK])
        kk = sb("kk", [P, 4, BLK])
        gam = sb("gam", [P, 4 * (BLK + 8)])
        gin = sb("gin", [P, 4, BLK])
        ar = sb("ar", [P, 4, 2, BLK])
        beta = sb("beta", [P, 4, BLK])
        kappa = sb("kappa", [P, 4, BLK])
        vv = sb("vv", [P, 4, BLK])
        bonus = sb("bonus", [P, 4, BLK])
        gL = sb("gL", [P, 4, 8])
        bdx = sb("bdx", [P, 4, 4, P])
        Aq = sb("Aq", [P, 2, 4, CH])
        bdAak = sb("bdAak", [P, 4, P])
        bdB = sb("bdB", [P, 4, P], INV)
        bdBT = sb("bdBT", [P, 4, P], INV)
        PT = sb("PT", [P, 4, CH], INV)
        PBY = sb("PBY", [P, 4, P], INV)
        PB, Yc = PBY[:, :, 0:CH], PBY[:, :, CH:P]
        bdY = bdBT
        bT = sb("bT", [P, 4, P])
        kT = sb("kT", [P, 4, P])
        Vc = sb("Vc", [P, 4, CH])
        bdV = sb("bdV", [P, 4, P])
        Zc = Yc
        Uc = sb("Uc", [P, 4, CH])
        bdU = bdAak
        S = sb("S", [P, 4, CH])
        bdS = sb("bdS", [P, 4, P])
        yT = sb("yT", [P, 2, 4, P])
        zr = sb("zr", [P, 4, P])
        m_hl = sb("m_hl", [P, 2, 2, 4, P], F16)
        x_y = sb("x_y", [P, D])
        st = sb("st", [P, 8])

        d_bank = [bank("d0"), bank("d1")]
        o_bank = [bank("o0"), bank("o1")]
        R = {i: bank(f"R{i}") for i in (0, 2, 3, 4)}
        Ss = x_y[:, :].rearrange("p (j g v) -> p j g v", j=4, g=4)

        def b4(ap, w=P):
            return ap.rearrange("p (g t) -> p g t", g=4)

        def half(r, k):
            return r[:, 256 * k:256 * k + 256].rearrange("p (g t) -> p g t", g=4)

        def blocks2(ap4):
            return ap4.rearrange("p g (a t) -> p g a t", a=2)

        def bc(ap, shape, at):
            return ap.unsqueeze(at).to_broadcast(shape)

        def par_s(name, g):
            return sc[:, SC[name] + g:SC[name] + g + 1]

        lnb_s = sb("lnb_s", [P, 4])

        def make_run(pool, done, l):
            done(pool.memset(run[:, :], 1.0))
            done(pool.memset(run[:, :].rearrange("p (c t) -> p c t", t=l)[:, :, 0:1], 0.0))

        def make_masks(pool, done, sample):
            for m in (lt_bd, gt_bd, lt_c, le_c, gt_c):
                done(pool.memset(m[:, :], 1.0))
            for m in (lt_bd, gt_bd):
                done(pool.memset(m[0:64, 64:128], 0.0))
                done(pool.memset(m[64:128, 0:64], 0.0))
            for h in range(2):
                rows = slice(64 * h, 64 * h + 64)
                every = slice(0, CH)
                for m, cols, op, step in ((lt_bd, rows, ALU.is_gt, 1), (lt_c, every, ALU.is_gt, 1),
                                          (le_c, every, ALU.is_ge, 1), (gt_bd, rows, ALU.is_gt, -1),
                                          (gt_c, every, ALU.is_gt, -1)):
                    done(pool.affine_select(out=m[rows, cols], in_=m[rows, cols], compare_op=op, fill=0.0, base=0,
                                            pattern=[[step, CH]], channel_multiplier=-step))
            if not sample:
                return
            for h in range(2):
                rows = slice(64 * h, 64 * h + 64)
                for m, cols, base, step in ((lt_bd, rows, 0, -1), (lt_c, slice(0, CH), 0, -1),
                                            (le_c, slice(0, CH), 0, -1), (gt_bd, rows, SLEN - 1, 1),
                                            (gt_c, slice(0, CH), SLEN - 1, 1)):
                    done(pool.affine_select(out=m[rows, cols], in_=m[rows, cols], compare_op=ALU.is_ge, fill=0.0,
                                            base=base, pattern=[[step * SLEN, 4], [0, SLEN]],
                                            channel_multiplier=-step))

        with ExitStack() as pre:
            w_in = [pre.enter_context(nc.semaphore(f"s_w2_in{i}")) for i in range(2)]
            w_high = pre.enter_context(nc.semaphore("s_w2_high"))
            w_split = pre.enter_context(nc.semaphore("s_w2_split"))
            small = pre.enter_context(nc.semaphore("s_small2"))
            scaled = pre.enter_context(nc.semaphore("s_scaled2"))
            pset = pre.enter_context(nc.semaphore("s_pool_set2"))
            nset = [0]
            stage = [xm[:, :, :].rearrange("p g t -> p (g t)"), ar[:, :, :, :].rearrange("p g a t -> p (g a t)")]
            gscale = carry_s[:, 0, :]
            block = pre.enter_context(nc.Block())

            @block.sync
            def _(sp):
                sp.dma_start(up[0:64, :], t["rwkv_w_up"]).then_inc(small, 16)
                sp.dma_start(up[64:128, :], t["rwkv_a_up"]).then_inc(small, 16)
                sp.dma_start(npost[:, :], t["norm_post"].to_broadcast([P, D])).then_inc(small, 16)
                for k in range(2 * KT):
                    if k >= 2:
                        sp.wait_ge(w_split, k - 1)
                    if k < KT:
                        src, n = t["w_in"][k * P:(k + 1) * P, GLA_COLS:GLA_COLS + SHIFT_W], W2_COLS
                    else:
                        src, n = t["w_out"][(k - KT) * P:(k - KT + 1) * P, :], D
                    sp.dma_start(stage[k % 2][:, 0:n], src).then_inc(w_in[k % 2], 16)
                sp.wait_ge(small, 48)

            @block.scalar
            def _(act):
                act.wait_ge(scaled, 1)
                for k in range(2 * KT):
                    act.wait_ge(w_in[k % 2], 16 * (k // 2 + 1))
                    if k < KT:
                        act.activation(w_hi[:, k, :], stage[k % 2][:, 0:W2_COLS], ACT.Identity,
                                       scale=gscale[:, k:k + 1]).then_inc(w_high, 1)
                    else:
                        act.activation(o_hi[:, k - KT, :], stage[k % 2][:, 0:D], ACT.Copy,
                                       scale=W_SCALE).then_inc(w_high, 1)

            @block.vector
            def _(dve):
                dve.tensor_scalar(gscale, par[:, 0:KT], W_SCALE, None, ALU.mult).then_inc(scaled, 1)
                dve.wait_ge(scaled, 1)
                n = 1
                cm = M_SCALE * UNSCALE * 0.5
                for dst, src, a, o in (("w0h", "w0", 0.5, None), ("a0h", "a0", 0.5, None), ("nkk", "k_k", -1.0, None),
                                       ("kah", "k_a", 0.5, None), ("ka1", "k_a", -0.5, 1.0), ("rk", "r_k", cm, None),
                                       ("lnw", "ln_w", cm, None)):
                    src = par[:, PAR[src][0]:PAR[src][0] + 4]
                    dst = sc[:, SC[dst]:SC[dst] + 4]
                    if o is None:
                        dve.tensor_scalar(dst, src, a, None, ALU.mult).then_inc(scaled, 1)
                    else:
                        dve.tensor_scalar(dst, src, a, o, ALU.mult, ALU.add).then_inc(scaled, 1)
                    n += 1
                dve.tensor_scalar(lnb_s[:, :], par[:, PAR["ln_b"][0]:PAR["ln_b"][0] + 4], cm, None,
                                  ALU.mult).then_inc(scaled, 1)
                for k in range(2 * KT):
                    dve.wait_ge(w_high, k + 1)
                    if k < KT:
                        dve.scalar_tensor_tensor(out=w_lo[:, k, :], in0=stage[k % 2][:, 0:W2_COLS],
                                                 scalar=gscale[:, k:k + 1], in1=w_hi[:, k, :],
                                                 op0=ALU.mult, op1=ALU.subtract).then_inc(w_split, 1)
                    else:
                        dve.scalar_tensor_tensor(out=o_lo[:, k - KT, :], in0=stage[k % 2][:, 0:D],
                                                 scalar=W_SCALE, in1=o_hi[:, k - KT, :],
                                                 op0=ALU.mult, op1=ALU.subtract).then_inc(w_split, 1)

            @block.gpsimd
            def _(pool):
                def done(ins):
                    ins.then_inc(pset, 1)
                    nset[0] += 1
                    pool.wait_ge(pset, nset[0])

                for m, v in ((headsum, 1.0), (headmean, 1.0 / CH), (ident2, 0.0), (seg_rows, 1.0), (carry, 0.0)):
                    done(pool.memset(m[:, :], v))
                for m in (bdV, bdS, S):
                    done(pool.memset(m[:, :, :], 0.0))
                done(pool.memset(gam[:, :], 1.0))
                for m in (headsum, headmean):
                    done(pool.memset(m[0:64, 64:128], 0.0))
                    done(pool.memset(m[64:128, 0:64], 0.0))
                done(pool.tensor_tensor(centre[:, :], ident[:, :], headmean[:, :], ALU.subtract))
                for h in range(2):
                    rows = slice(64 * h, 64 * h + 64)
                    done(pool.affine_select(out=ident2[rows, :], in_=ident2[rows, :], compare_op=ALU.not_equal,
                                            fill=1.0, base=0, pattern=[[-1, CH]], channel_multiplier=1))
                    done(pool.affine_select(out=seg_rows[rows, :], in_=seg_rows[rows, :], compare_op=ALU.is_ge,
                                            fill=0.0, base=0, pattern=[[-SLEN, 4]], channel_multiplier=1))
                for h in range(2):
                    rows = slice(64 * h, 64 * h + 64)
                    done(pool.affine_select(out=seg_rows[rows, :], in_=seg_rows[rows, :], compare_op=ALU.is_ge,
                                            fill=0.0, base=SLEN - 1, pattern=[[SLEN, 4]], channel_multiplier=-1))
                make_run(pool, done, SLEN)
                make_masks(pool, done, True)


        class Steps:

            def __init__(self, name, steps):
                self.steps = steps
                self.s = sig(name, 2 * len(steps[1]), 4 * len(steps[0]))

            def wait(self, eng, b, ch, step):
                steps = self.steps[is_sample(b)]
                eng.wait_ge(self.s.sem, self.s.at(b, ch * len(steps) + steps.index(step) + 1))

            def wait_prev(self, eng, b, ch, step):
                if ch:
                    self.wait(eng, b, ch - 1, step)
                elif not is_sample(b):
                    eng.wait_ge(self.s.sem, self.s.at(b, 1 + self.steps[0].index(step) - len(self.steps[0])))

            def up(self, b):
                return self.s.up(b)

        def tile_sig(name, n, step=1):
            s = TileSignal(ctx.enter_context(nc.semaphore("r_" + name)), name, n, step)
            signals.append(s)
            return s

        pe_s = Steps("rec_pe", PE_STEPS)
        dve_s = Steps("rec_dve", DVE_STEPS)
        act_s = Steps("rec_act", ACT_STEPS)

        h_in = sig("h_in", 1, 1, 16)
        mg_in = tile_sig("mg_in", 1, 16)
        zr_in = tile_sig("zr_in", 1, 16)
        xy_in = tile_sig("xy_in", 1, 16)
        y_out = tile_sig("y_out", 1, 16)
        ss_in = sig("ss_in", 2, 0, 16)
        ss_out = sig("ss_out", 2, 0, 16)
        sh_in = sig("sh_in", 1, 0, 16)
        ends = sig("ends_out", 0, 0, 16)
        remade = sig("remade", 0, 0)
        d_full = sig("d_full", 13, 13)
        praw_ok = sig("praw", 7, 7)
        mix_ok = sig("mix", 20, 20)
        carry_ok = sig("carry", 14, 14)
        th_ok = sig("th", 9, 9)
        dec_ok = sig("decay", 5, 5)
        gam_ok = sig("gamma", 2, 2)
        sq_ok = sig("kk_sq", 4, 4)
        clamp_ok = sig("clamp", 2, 2)
        rn_ok = sig("rnorm", 4, 4)
        kk_ok = sig("kk", 4, 4)
        kf_ok = sig("k_factor", 4, 4)
        kp_ok = sig("k_prime", 2, 2)
        rkk_ok = sig("rkk", 4, 4)
        op_ok = sig("operands", 5, 5)
        vv_ok = sig("v_operand", 2, 2)
        bd_ok = sig("bd", 8, 16)
        gb_full = sig("gb_full", 2, 2)
        bonus_ok = sig("bonus", 2, 2)
        gc_full = tile_sig("gc_full", 2)
        yc_ok = tile_sig("y_centred", 2)
        gr_ok = tile_sig("y_rstd", 2)
        post_ok = tile_sig("post", 7)
        mh_ok = tile_sig("m_high", 1)
        ml_ok = tile_sig("m_low", 1)
        o_full = tile_sig("o_full", 2)
        ss_ok = tile_sig("y_stats", 4)
        st_ok = tile_sig("y_stat_sum", 1)
        fin_ok = tile_sig("y_done", 4)

        def nchunks(b):
            return 2 if is_sample(b) else 4

        def L(b):
            return SLEN if is_sample(b) else CH

        def plan(b, has_next=True):
            slots = [[] for _ in range(SLOTS * nchunks(b))]
            for half_b, tile in enumerate(() if is_sample(b) else (Tile(b, -2), Tile(b, -1))):
                first = 2 * SLOTS * half_b
                for at, job in ((3, "centre"), (4, "variance"), (5, "gate0"), (6, "gate1"), (7, "high"), (8, "low")):
                    slots[first + at].append((job, tile))
                out = [s for s in range(first + 9, first + 2 * SLOTS) if s % SLOTS not in LIGHT]
                out = sorted(out + out[-1:] * (12 - len(out)))
                for n in range(12):
                    slots[out[n]].append(("out", (tile, n)))
                slots[out[7]].append(("squares0", tile))
                for job in ("squares1", "sum", "rstd", "finish"):
                    slots[first + 2 * SLOTS - 1].append((job, tile))
            for at, job in ((4, "bonus_sum0"), (6, "bonus0"), (7, "bonus_sum1"), (8, "bonus1")):
                slots[at].append((job, b))
            if has_next:
                room = [s for s in range(2, len(slots) - 4) if s % SLOTS not in LIGHT]
                load = {s: sum(job in PE_JOBS for job, _ in slots[s]) for s in room}
                per_slot = (len(PIECES) + sum(load.values())) / len(room)
                p = done = 0
                for n, s in enumerate(room):
                    done += load[s]
                    while p < len(PIECES) and (done < per_slot * (n + 1) or s == room[-1]):
                        slots[s].append(("piece", p))
                        if PIECES[p][3]:
                            for round_, steps in (("la2", ("decay", "gamma")), ("kn2", ("k_factor", "k_prime", "rkk"))):
                                if ROUNDS[PIECES[p][0]] == round_:
                                    for later, job in enumerate(steps):
                                        slots[s + 1 + later].append((job, b + 1))
                        p, done = p + 1, done + 1
                slots[-3].append(("operands0", b + 1))
                slots[-2].append(("operands1", b + 1))
                slots[-2].append(("v_operand", b + 1))
            return slots

        def run_plan(slots, at, does):
            for job, arg in slots[at]:
                if job in does:
                    does[job](arg)

        def gview(b, prev):
            n, l = tiles(b) * P, L(b)
            ns = n // l
            v = gam[:, 0:4 * ns * (l + 1)].rearrange("p (g s l) -> p g s l", g=4, l=l + 1)
            return v[:, :, :, 0:l] if prev else v[:, :, :, 1:l + 1]

        def segs(ap, l):
            return ap.rearrange("p g (s l) -> p g s l", l=l)

        y_squares = m_hl[:, 1].rearrange("p a k t -> p (a k t)").bitcast(F32)

        XROUNDS = [q for q in ROUNDS if q[0] == "x"]

        block = ctx.enter_context(nc.Block())

        @block.sync
        def _(sp):
            def load_zr(tile, src):
                sp.dma_start(zr[:, :, :], src).then_inc(*zr_in.up(tile))

            def load_gla(tile, src):
                sp.dma_start(m_hl[:, 0], src).then_inc(*mg_in.up(tile))

            def load_x(tile):
                sp.dma_start(x_y[:, :], t["x"][tile.index()]).then_inc(*xy_in.up(tile))

            def store_y(tile):
                sp.wait_ge(fin_ok.sem, fin_ok.at(tile, 4))
                sp.dma_start(t["y"][tile.index()], x_y[:, :]).then_inc(*y_out.up(tile))
                sp.wait_ge(y_out.sem, y_out.at(tile, 1))

            def body(b, has_next=True):
                before, first, second = Tile(b, -2), Tile(b, -1), Tile(b, 0)
                sp.wait_ge(post_ok.sem, post_ok.at(before, 7))
                load_zr(first, t["zr"][b][:, :, 0:P])
                sp.wait_ge(o_full.sem, o_full.at(before, 2))
                load_gla(first, t["mg"][b][:, 0])
                store_y(before)
                load_x(first)
                sp.wait_ge(post_ok.sem, post_ok.at(first, 7))
                load_zr(second, t["zr"][b][:, :, P:2 * P])
                sp.wait_ge(o_full.sem, o_full.at(first, 2))
                load_gla(second, t["mg"][b][:, 1])
                store_y(first)
                load_x(second)

            sp.dma_start(carry_s[:, :, :], t["state_shift"]).then_inc(*sh_in.up(0))
            load_gla(Tile(0, 0), t["mg"][0][:, 0])
            load_zr(Tile(0, 0), t["zr"][0][:, :, 0:P])
            for ch in range(2):
                sp.dma_start(Ss, t["state_rwkv"][:, 4 * ch:4 * ch + 4]).then_inc(*ss_in.up(0))
                dve_s.wait(sp, 0, ch, "S")
                sp.dma_start(t["rwkv_sample"][:, 4 * ch:4 * ch + 4], Ss).then_inc(*ss_out.up(0))
                sp.wait_ge(ss_out.sem, ss_out.at(0, ch + 1))
            load_x(Tile(0, 0))
            sp.wait_ge(carry_ok.sem, carry_ok.at(0, 14))
            sp.dma_start(t["shift_sample"], carry_s[:, :, :]).then_inc(ends.sem, 16)
            with sp.Fori(1, LAST) as b:
                body(b)
            body(LAST, has_next=False)
            sp.wait_ge(carry_ok.sem, carry_ok.at(LAST, 14))
            sp.dma_start(t["shift_prompt"], carry[:, :]).then_inc(ends.sem, 16)
            dve_s.wait(sp, LAST, 3, "S")
            sp.dma_start(t["rwkv_prompt"], S[:, :, :]).then_inc(ends.sem, 16)
            store_y(Tile(LAST, 0))
            sp.wait_ge(ends.sem, 48)

        @block.gpsimd
        def _(pool):
            def copies(b, ch):
                cols = slice(ch * CH, (ch + 1) * CH)
                if ch == 0:
                    pool.wait_ge(op_ok.sem, op_ok.at(b, 3))
                    pool.wait_ge(vv_ok.sem, vv_ok.at(b, 1))
                pe_s.wait_prev(pool, b, ch, "turnk")
                for k, src in ((1, beta), (2, kappa), (3, vv), (0, ar)):
                    if k == 0:
                        pe_s.wait_prev(pool, b, ch, "Z")
                    s = src[:, :, 0, cols] if k == 0 else src[:, :, cols]
                    pool.tensor_tensor(blocks2(bdx[:, k]), bc(s, [P, 4, 2, CH], 2),
                                       bc(headsum[:, :].rearrange("p (a t) -> p a t", a=2), [P, 4, 2, CH], 1),
                                       ALU.mult).then_inc(*bd_ok.up(b))

            def body(b):
                for ch in range(nchunks(b)):
                    copies(b, ch)

            count = [0]

            def done(ins):
                ins.then_inc(remade.sem, 1)
                count[0] += 1
                pool.wait_ge(remade.sem, count[0])

            pool.wait_ge(dec_ok.sem, dec_ok.at(0, 5))
            make_run(pool, done, CH)
            pool.wait_ge(op_ok.sem, op_ok.at(0, 5))
            pool.wait_ge(vv_ok.sem, vv_ok.at(0, 2))
            ones = gam[:, 0:4 * 4 * (CH + 1)].rearrange("p (s l) -> p s l", l=CH + 1)[:, :, 0:1]
            done(pool.memset(ones, 1.0))
            REMADE_RUN = count[0]
            assert REMADE_RUN == N_RUN
            body(0)
            dve_s.wait(pool, 0, 1, "Aqk")
            make_masks(pool, done, False)
            assert count[0] == N_RUN + N_MASKS, count
            with pool.Fori(1, LAST) as b:
                body(b)
            body(LAST)

        @block.tensor
        def _(pe):
            def product(out, lhs, rhs, third):
                for m in range(8 * third, 8 * third + 8):
                    k, (a, w) = m // 3, ((0, 0), (1, 0), (0, 1))[m % 3]
                    mm = pe.matmul(out, lhs(k, a, w), rhs(k, a, w), start=(m == 0), stop=(m == 3 * KT - 1))
                return mm

            READER = {"x12": (praw_ok, 1), "x4": (praw_ok, 2), "x6": (praw_ok, 3), "lw0": (th_ok, 3),
                      "la0": (th_ok, 5), "lw2": (th_ok, 7), "la2": (th_ok, 9), "kn0": (kk_ok, 2), "kn2": (kk_ok, 4),
                      "x0": (praw_ok, 4), "x2": (praw_ok, 5), "x8": (praw_ok, 6), "x10": (praw_ok, 7)}

            def piece(b, p):
                r, h, third, last = PIECES[p]
                kind = ROUNDS[r]
                out = d_bank[r % 2]
                n = tiles(b) * P
                if h or third:
                    pass
                elif r >= 2:
                    s, k = READER[ROUNDS[r - 2]]
                    pe.wait_ge(s.sem, s.at(b, k))
                elif not is_sample(b):
                    pe.wait_ge(praw_ok.sem, praw_ok.at(b, 0))
                if kind[0] == "x":
                    if p == 0:
                        pe.wait_ge(h_in.sem, h_in.at(b, 1))
                    g = int(kind[1:]) + h
                    mm = product(out[:, h * n:(h + 1) * n],
                                 lambda k, a, w: (w_hi, w_lo)[w][:, k, g * P:(g + 1) * P],
                                 lambda k, a, w: hT[:, a, k, 0:n], third)
                elif kind[0] == "l":
                    pe.wait_ge(th_ok.sem, th_ok.at(b, 1))
                    rows = slice(0, 64) if kind[1] == "w" else slice(64, 128)
                    g0 = int(kind[2])
                    for g in range(2):
                        mm = pe.matmul(out[:, g * n:(g + 1) * n], up[rows, (g0 + g) * P:(g0 + g + 1) * P],
                                       lor[rows, 0:n], start=True, stop=True)
                else:
                    g0 = int(kind[2])
                    pe.wait_ge(sq_ok.sem, sq_ok.at(b, g0 + 2))
                    for g in range(2):
                        mm = pe.matmul(out[:, g * n:(g + 1) * n], headsum[:, :], scr[:, g0 + g, 0:n],
                                       start=True, stop=True)
                if last:
                    mm.then_inc(*d_full.up(b))

            def bd(k, g):
                return bdx[:, k, g, :]

            def turn(b, ch):
                pe.wait_ge(bd_ok.sem, bd_ok.at(b, 4 * ch + 3))
                for g in range(4):
                    pe.matmul(half(R[2], 0)[:, g, :], bd(3, g), ident2[:, :], start=True, stop=True)
                for g in range(4):
                    mm = pe.transpose(R[0][:, g * P:(g + 1) * P], bd(1, g), ident[:, :])
                mm.then_inc(*pe_s.up(b))

            def turn_kappa(b, ch):
                act_s.wait(pe, b, ch, "betaT")
                for g in range(4):
                    mm = pe.transpose(R[0][:, g * P:(g + 1) * P], bd(2, g), ident[:, :])
                mm.then_inc(*pe_s.up(b))

            def scores(b, ch):
                dve_s.wait_prev(pe, b, ch, "Ssum")
                act_s.wait_prev(pe, b, ch, "y")
                pe.wait_ge(bd_ok.sem, bd_ok.at(b, 4 * ch + 4))
                if ch == 0:
                    pe.wait_ge(op_ok.sem, op_ok.at(b, 4))
                elif ch == nchunks(b) - 1:
                    pe.wait_ge(op_ok.sem, op_ok.at(b, 5))
                cols = slice(ch * CH, (ch + 1) * CH)
                for g in range(4):
                    pe.matmul(R[3][:, g * P:(g + 1) * P], bd(1, g), ar[:, g, :, cols], start=True, stop=True)
                act_s.wait(pe, b, ch, "Vc")
                for g in range(4):
                    pe.matmul(half(R[2], 1)[:, g, :], bd(0, g), beta[:, g, cols], start=True, stop=True)
                for g in range(4):
                    mm = pe.matmul(R[4][:, g * P:(g + 1) * P], bd(2, g), ar[:, g, :, cols], start=True, stop=True)
                mm.then_inc(*pe_s.up(b))

            def square(b, ch, j):
                if j == 1:
                    dve_s.wait(pe, b, ch, "PB")
                    act_s.wait(pe, b, ch, "kappaT")
                else:
                    dve_s.wait(pe, b, ch, "P1" if j == 2 else "Y%d" % (j - 1))
                    act_s.wait(pe, b, ch, "BT%dp" % (j - 1))
                for g in range(4):
                    if j <= 5:
                        mm = pe.matmul(half(R[0], 0)[:, g, :], bdB[:, g, :], PT[:, g, :], start=True, stop=True)
                    cols = slice(0 if j <= 4 else CH, CH if j == 1 else P)
                    mm = pe.matmul(b4(R[2])[:, g, cols], bdBT[:, g, :], PBY[:, g, cols], start=True, stop=True)
                mm.then_inc(*pe_s.up(b))

            def solve(b, ch):
                dve_s.wait(pe, b, ch, "Aqk")
                if is_sample(b):
                    for g in range(4):
                        pe.matmul(half(R[0], 0)[:, g, :], bdAak[:, g, :], Vc[:, g, :], start=True, stop=True)
                    pe.wait_ge(ss_in.sem, ss_in.at(b, ch + 1))
                    for j in range(4):
                        for g in range(4):
                            mm = pe.matmul(half(R[3 + j // 2], j % 2)[:, g, :], bd(0, g), Ss[:, j, g, :],
                                           start=True, stop=True)
                else:
                    dve_s.wait_prev(pe, b, ch, "S")
                    for g in range(4):
                        pe.matmul(half(R[0], 0)[:, g, :], bdAak[:, g, :], Vc[:, g, :], start=True, stop=False)
                        mm = pe.matmul(half(R[0], 0)[:, g, :], bd(0, g), S[:, g, :], start=False, stop=True)
                mm.then_inc(*pe_s.up(b))

            def unknowns(b, ch):
                dve_s.wait(pe, b, ch, "Z")
                for g in range(4):
                    mm = pe.matmul(half(R[0], 1)[:, g, :], bdY[:, g, :], Zc[:, g, :], start=True, stop=True)
                mm.then_inc(*pe_s.up(b))

            def state(b, ch):
                dve_s.wait(pe, b, ch, "U")
                for j in range(4 if is_sample(b) else 1):
                    if is_sample(b):
                        dve_s.wait(pe, b, ch, "v%d" % j)
                    for g in range(4):
                        u = bdAak[:, g, 0:CH] if is_sample(b) else Uc[:, g, :]
                        v = bdAak[:, g, CH:P] if is_sample(b) else Vc[:, g, :]
                        pe.matmul(half(R[3], 0)[:, g, :], bT[:, g, :], u, start=True, stop=False)
                        mm = pe.matmul(half(R[3], 0)[:, g, :], kT[:, g, :], v, start=False, stop=True)
                    mm.then_inc(*pe_s.up(b))

            def outputs(b, ch):
                act_s.wait(pe, b, ch, "U1")
                if not is_sample(b):
                    act_s.wait_prev(pe, b, ch, "bdS1")
                for j in range(4 if is_sample(b) else 1):
                    if is_sample(b):
                        dve_s.wait(pe, b, ch, "e%db" % j)
                    w = SLEN if is_sample(b) else CH
                    cols = slice(j * w, (j + 1) * w)
                    for g in range(4):
                        out = half(R[4], 0)[:, g, cols]
                        pe.matmul(out, bdU[:, g, :], Aq[:, 0, g, cols], start=True, stop=False)
                        pe.matmul(out, bdV[:, g, :], Aq[:, 1, g, cols], start=False, stop=False)
                        mm = pe.matmul(out, bdS[:, g, :], ar[:, g, 1, ch * CH + cols.start:ch * CH + cols.stop],
                                       start=False, stop=True)
                    mm.then_inc(*pe_s.up(b))

            def centre_y(tile):
                if tile.off == -1:
                    act_s.wait(pe, tile.b, 1, "y")
                elif tile.off == -2:
                    act_s.wait_prev(pe, tile.b, 0, "y")
                else:
                    act_s.wait(pe, tile.b, 3, "y")
                pe.matmul(o_bank[0][:, :], centre[:, :], yT[:, tile.i], start=True, stop=True)\
                  .then_inc(*gc_full.up(tile))

            def variance(tile):
                pe.wait_ge(yc_ok.sem, yc_ok.at(tile, 2))
                pe.matmul(o_bank[0][:, :], headmean[:, :], y_squares, start=True, stop=True)\
                  .then_inc(*gc_full.up(tile))

            def bonus_sums(b, k):
                n = tiles(b) * P
                pe.wait_ge(rkk_ok.sem, rkk_ok.at(b, 2 * k + 2))
                if k:
                    pe.wait_ge(bonus_ok.sem, bonus_ok.at(b, 1))
                for g in range(2):
                    mm = pe.matmul(o_bank[1][:, g * n:(g + 1) * n], headsum[:, :], scr[:, 2 * k + g, 0:n],
                                   start=True, stop=True)
                mm.then_inc(*gb_full.up(b))

            def project_out(tile, n):
                q, third = n // 3, n % 3
                if n == 0:
                    pe.wait_ge(mg_in.sem, mg_in.at(tile, 1))
                    pe.wait_ge(ml_ok.sem, ml_ok.at(tile, 1))
                if n == 6 and tile.off == -2:
                    pe.wait_ge(bonus_ok.sem, bonus_ok.at(tile.b, 2))
                mm = product(o_bank[q // 2][:, q % 2 * 256:q % 2 * 256 + 256],
                             lambda k, a, w: m_hl[:, k // 4, a, k % 4, :],
                             lambda k, a, w: (o_hi, o_lo)[w][:, k, q * 256:(q + 1) * 256], third)
                if n % 6 == 5:
                    mm.then_inc(*o_full.up(tile))

            does = {"centre": centre_y, "variance": variance, "out": lambda arg: project_out(*arg),
                    "bonus_sum0": lambda b: bonus_sums(b, 0), "bonus_sum1": lambda b: bonus_sums(b, 1)}

            def body(b, has_next=True):
                slots = plan(b, has_next)
                does["piece"] = lambda p: piece(b + 1, p)

                def fill(ch, k):
                    run_plan(slots, ch * SLOTS + k, does)

                for ch in range(nchunks(b)):
                    turn(b, ch)
                    fill(ch, 0)
                    scores(b, ch)
                    fill(ch, 1)
                    turn_kappa(b, ch)
                    fill(ch, 2)
                    for j in range(1, 7):
                        square(b, ch, j)
                        fill(ch, 2 + j)
                    solve(b, ch)
                    fill(ch, 9)
                    unknowns(b, ch)
                    fill(ch, 10)
                    if is_sample(b):
                        outputs(b, ch)
                        state(b, ch)
                    else:
                        state(b, ch)
                        outputs(b, ch)

            for p in range(len(PIECES)):
                piece(0, p)
            body(0)
            with pe.Fori(1, LAST) as b:
                body(b)
            body(LAST, has_next=False)
            tile = Tile(LAST, 0)
            pe.wait_ge(fin_ok.sem, fin_ok.at(Tile(LAST, -1), 4))
            centre_y(tile)
            variance(tile)
            for n in range(12):
                project_out(tile, n)

        @block.scalar
        def _(act):
            def load_h(b):
                n = tiles(b) * P
                if not is_sample(b):
                    act.wait_ge(d_full.sem, d_full.at(b, 0))
                act.dma_start(hT[:, :, :, 0:n], t["hT"][b][:, :, :, 0:n]).then_inc(*h_in.up(b))

            def projected(b, r):
                kind = ROUNDS[r]
                n, l = tiles(b) * P, L(b)
                pair = d_bank[r % 2][:, 0:2 * n].rearrange("p (g t) -> p g t", g=2)
                if kind[0] == "x":
                    ng = 1 if kind == "x12" else 2
                    k = XROUNDS.index(kind)
                    act.wait_ge(d_full.sem, d_full.at(b, r + 1))
                    if k:
                        act.wait_ge(carry_ok.sem, carry_ok.at(b, 2 * k))
                    elif not is_sample(b):
                        act.wait_ge(carry_ok.sem, carry_ok.at(b, 0))
                        act.wait_ge(op_ok.sem, op_ok.at(b, 0))
                    if is_sample(b):
                        out = praw[:, 0:ng, 0:STREAMS * (SLEN + 1)].rearrange("p g (s l) -> p g s l", l=SLEN + 1)
                        out, src = out[:, :, :, 1:SLEN + 1], segs(pair[:, 0:ng, :], SLEN)
                    else:
                        out, src = praw[:, 0:ng, 1:n + 1], pair[:, 0:ng, :]
                    act.activation(out, src, ACT.Copy, scale=UNSCALE).then_inc(*praw_ok.up(b))
                    if kind == "x12":
                        act.wait_ge(mix_ok.sem, mix_ok.at(b, 2))
                        act.activation(lor[0:64, 0:n], lor[0:64, 0:n], ACT.Tanh).then_inc(*th_ok.up(b))
                elif kind[0] == "l":
                    act.wait_ge(d_full.sem, d_full.at(b, r + 1))
                    g0 = int(kind[2])
                    out, bias = (gin, "w0h") if kind[1] == "w" else (ta, "a0h")
                    for g in range(2):
                        act.activation(out[:, g0 + g, 0:n], pair[:, g, :], ACT.Tanh, scale=0.5,
                                       bias=par_s(bias, g0 + g)).then_inc(*th_ok.up(b))
                else:
                    g0 = int(kind[2])
                    act.wait_ge(clamp_ok.sem, clamp_ok.at(b, g0 // 2 + 1))
                    act.activation(pair, pair, ACT.Ln, scale=float(2 ** 20)).then_inc(*rn_ok.up(b))
                    act.wait_ge(rn_ok.sem, rn_ok.at(b, g0 + 1))
                    act.activation(pair, pair, ACT.Exp, scale=-0.5, bias=const(K_KK)).then_inc(*rn_ok.up(b))
                if kind in ("lw0", "la0"):
                    g0 = 0 if kind == "lw0" else 2
                    act.wait_ge(mix_ok.sem, mix_ok.at(b, 2 + 3 * (g0 // 2) + 3))
                    if not is_sample(b):
                        act.wait_ge(gb_full.sem, gb_full.at(b - 1, g0 // 2 + 1))
                    for g in range(2):
                        act.activation(scr[:, g0 + g, 0:n], xm[:, 4 + g0 + g, 0:n], ACT.Square,
                                       scale=pcol("k_k", g0 + g)).then_inc(*sq_ok.up(b))

            def gamma(b):
                n, l = tiles(b) * P, L(b)
                act.preload_act_table_set(LN_SET)
                act.wait_ge(dec_ok.sem, dec_ok.at(b, 5))
                act.activation(gview(b, False), segs(gin[:, :, 0:n], l), ACT.Exp,
                               scale=-0.5 * DECAY).then_inc(*gam_ok.up(b))
                act.wait_ge(gam_ok.sem, gam_ok.at(b, 1))
                act.activation(gin[:, :, 0:n], gin[:, :, 0:n], ACT.Exp, scale=0.5 * DECAY).then_inc(*gam_ok.up(b))

            def operands(b):
                n = tiles(b) * P
                if not is_sample(b):
                    act.wait_ge(bd_ok.sem, bd_ok.at(b, 0))
                act.wait_ge(mix_ok.sem, mix_ok.at(b, 20))
                act.activation(vv[:, :, 0:n], xm[:, 8:12, 0:n], ACT.Copy).then_inc(*vv_ok.up(b))

            def ends_of_gamma(b):
                n, l = tiles(b) * P, L(b)
                if not is_sample(b):
                    dve_s.wait_prev(act, b, 0, "S")
                act.wait_ge(gam_ok.sem, gam_ok.at(b, 2))
                act.activation(gL[:, :, 0:n // l], gview(b, False)[:, :, :, l - 1], ACT.Copy).then_inc(*vv_ok.up(b))

            def turned(b, ch):
                pe_s.wait_prev(act, b, ch, "y")
                pe_s.wait(act, b, ch, "turn")
                act.activation(Vc[:, :, :], half(R[2], 0), ACT.Copy).then_inc(*act_s.up(b))
                act_s.wait(act, b, ch, "Vc")
                for h in range(2):
                    rows = slice(64 * h, 64 * h + 64)
                    act.activation(bdV[rows, :, rows], Vc[rows, :, :], ACT.Copy).then_inc(*act_s.up(b))
                act.activation(bT[:, :, :], b4(R[0]), ACT.Copy).then_inc(*act_s.up(b))

            def turned_kappa(b, ch):
                pe_s.wait(act, b, ch, "turnk")
                act.activation(kT[:, :, :], b4(R[0]), ACT.Copy).then_inc(*act_s.up(b))

            def squared(b, ch, j):
                if j <= 5:
                    pe_s.wait(act, b, ch, "sq%d" % j)
                    for h in range(2):
                        rows = slice(64 * h, 64 * h + 64)
                        act.activation(bdBT[rows, :, rows], half(R[0], 0)[rows, :, :],
                                       ACT.Copy).then_inc(*act_s.up(b))
                    act.activation(PT[:, :, :], half(R[0], 0), ACT.Copy).then_inc(*act_s.up(b))

            def spread_u(b, ch):
                dve_s.wait(act, b, ch, "U")
                for h in range(2):
                    rows = slice(64 * h, 64 * h + 64)
                    act.activation(bdU[rows, :, rows], Uc[rows, :, :], ACT.Copy).then_inc(*act_s.up(b))

            def output(b, ch):
                pe_s.wait(act, b, ch, "y")
                i = 1 if is_sample(b) else ch // 2
                act.activation(yT[:, i, :, (ch % 2) * CH:(ch % 2 + 1) * CH], half(R[4], 0), ACT.Copy)\
                    .then_inc(*act_s.up(b))
                dve_s.wait(act, b, ch, "S")
                for h in range(2):
                    rows = slice(64 * h, 64 * h + 64)
                    act.activation(bdS[rows, :, rows], S[rows, :, :], ACT.Copy).then_inc(*act_s.up(b))

            def centred(tile):
                act.preload_act_table_set(LN_SET)
                act.wait_ge(gc_full.sem, gc_full.at(tile, 1))
                act.activation(y_squares, o_bank[0][:, :], ACT.Square).then_inc(*yc_ok.up(tile))
                act.activation(yT[:, tile.i], b4(o_bank[0]), ACT.Copy).then_inc(*yc_ok.up(tile))

            def deviation(tile):
                act.wait_ge(gc_full.sem, gc_full.at(tile, 2))
                act.activation(o_bank[0][:, :], o_bank[0][:, :], ACT.Ln, bias=const(K_GN)).then_inc(*gr_ok.up(tile))
                act.wait_ge(gr_ok.sem, gr_ok.at(tile, 1))
                act.activation(o_bank[0][:, :], o_bank[0][:, :], ACT.Exp, scale=-0.5).then_inc(*gr_ok.up(tile))

            def high_part(tile):
                act.wait_ge(post_ok.sem, post_ok.at(tile, 7))
                act.activation(m_hl[:, 1, 0], yT[:, tile.i], ACT.Copy).then_inc(*mh_ok.up(tile))

            def out_squares(tile, h):
                act.wait_ge(o_full.sem, o_full.at(tile, h + 1))
                if h == 0:
                    act.wait_ge(ml_ok.sem, ml_ok.at(tile, 1))
                else:
                    act.wait_ge(ss_ok.sem, ss_ok.at(tile, 1))
                act.activation(yT[:, tile.i].rearrange("p g t -> p (g t)"), o_bank[h][:, :], ACT.Square,
                               accum_out=st[:, h:h + 1]).then_inc(*ss_ok.up(tile))

            def out_rstd(tile):
                act.wait_ge(st_ok.sem, st_ok.at(tile, 1))
                act.activation(st[:, 4:5], st[:, 4:5], ACT.Ln, scale=1.0 / (D * (M_SCALE * W_SCALE) ** 2),
                               bias=const(K_RMS)).then_inc(*ss_ok.up(tile))
                act.wait_ge(ss_ok.sem, ss_ok.at(tile, 3))
                act.activation(st[:, 5:6], st[:, 4:5], ACT.Exp, scale=-0.5, bias=const(K_LNM)).then_inc(*ss_ok.up(tile))

            does = {"centre": centred, "variance": deviation, "high": high_part,
                    "squares0": lambda tile: out_squares(tile, 0), "squares1": lambda tile: out_squares(tile, 1),
                    "rstd": out_rstd, "gamma": gamma, "v_operand": operands}

            def body(b, has_next=True):
                slots = plan(b, has_next)
                does["piece"] = lambda p: PIECES[p][3] and projected(b + 1, PIECES[p][0])

                def fill(ch, k):
                    run_plan(slots, ch * SLOTS + k, does)

                if has_next:
                    load_h(b + 1)
                for ch in range(nchunks(b)):
                    turned(b, ch)
                    fill(ch, 0)
                    fill(ch, 1)
                    turned_kappa(b, ch)
                    fill(ch, 2)
                    for j in range(1, 7):
                        squared(b, ch, j)
                        fill(ch, 2 + j)
                    fill(ch, 9)
                    spread_u(b, ch)
                    fill(ch, 10)
                    output(b, ch)
                if has_next:
                    ends_of_gamma(b + 1)

            load_h(0)
            for r, kind in enumerate(ROUNDS):
                projected(0, r)
                if kind == "la2":
                    gamma(0)
            operands(0)
            ends_of_gamma(0)
            body(0)
            with act.Fori(1, LAST) as b:
                body(b)
            body(LAST, has_next=False)
            tile = Tile(LAST, 0)
            centred(tile)
            deviation(tile)
            high_part(tile)
            out_squares(tile, 0)
            out_squares(tile, 1)
            out_rstd(tile)

        @block.vector
        def _(dve):
            def projected(b, r):
                kind = ROUNDS[r]
                n, l = tiles(b) * P, L(b)
                pair = d_bank[r % 2][:, 0:2 * n].rearrange("p (g t) -> p g t", g=2)
                if kind[0] == "x":
                    k = XROUNDS.index(kind)
                    ng, g0 = (1, 12) if kind == "x12" else (2, int(kind[1:]))
                    m0 = 0 if kind == "x12" else 2 + 3 * (k - 1)
                    out = lor[:, 0:n].unsqueeze(1) if kind == "x12" else xm[:, g0:g0 + 2, 0:n]
                    if is_sample(b):
                        raw = praw[:, 0:ng, 0:STREAMS * (SLEN + 1)].rearrange("p g (s l) -> p g s l", l=SLEN + 1)
                        front, last = raw[:, :, :, 0], raw[:, :, :, SLEN]
                        before, now = raw[:, :, :, 0:SLEN], raw[:, :, :, 1:SLEN + 1]
                        kept = carry_s[:, g0:g0 + ng, :]
                        out = segs(out, SLEN)
                        if k == 0:
                            dve.wait_ge(sh_in.sem, 16)
                    else:
                        front, last = praw[:, 0:ng, 0:1], praw[:, 0:ng, n:n + 1]
                        before, now = praw[:, 0:ng, 0:n], praw[:, 0:ng, 1:n + 1]
                        kept = carry[:, g0:g0 + ng].unsqueeze(2)
                    if k == 0 and not is_sample(b):
                        dve.wait_ge(d_full.sem, d_full.at(b, 0))
                    dve.tensor_copy(front, kept).then_inc(*carry_ok.up(b))
                    dve.wait_ge(carry_ok.sem, carry_ok.at(b, 2 * k + 1))
                    dve.wait_ge(praw_ok.sem, praw_ok.at(b, k + 1))
                    dve.tensor_tensor(out, before, now, ALU.subtract).then_inc(*mix_ok.up(b))
                    dve.wait_ge(mix_ok.sem, mix_ok.at(b, m0 + 1))
                    for g in range(ng):
                        dve.scalar_tensor_tensor(out=out[:, g], in0=out[:, g], scalar=pcol("mu", g0 + g),
                                                 in1=now[:, g], op0=ALU.mult, op1=ALU.add).then_inc(*mix_ok.up(b))
                    dve.wait_ge(mix_ok.sem, mix_ok.at(b, m0 + 1 + ng))
                    dve.tensor_copy(kept, last).then_inc(*carry_ok.up(b))
                elif kind[0] == "k":
                    g0 = int(kind[2])
                    dve.wait_ge(d_full.sem, d_full.at(b, r + 1))
                    dve.tensor_scalar(pair, pair, 1e-24, None, ALU.max).then_inc(*clamp_ok.up(b))
                    dve.wait_ge(rn_ok.sem, rn_ok.at(b, g0 + 2))
                    for g in range(2):
                        dve.scalar_tensor_tensor(out=kk[:, g0 + g, 0:n], in0=xm[:, 4 + g0 + g, 0:n],
                                                 scalar=par_s("nkk", g0 + g), in1=pair[:, g, :],
                                                 op0=ALU.mult, op1=ALU.mult).then_inc(*kk_ok.up(b))

            def decay(b):
                n = tiles(b) * P
                dve.wait_ge(th_ok.sem, th_ok.at(b, 9))
                dve.tensor_scalar(gin[:, :, 0:n], gin[:, :, 0:n], 1.0, None, ALU.add).then_inc(*dec_ok.up(b))
                dve.wait_ge(dec_ok.sem, dec_ok.at(b, 1))
                if isinstance(b, int) and b == 1:
                    dve.wait_ge(remade.sem, N_RUN)
                for g in range(4):
                    dve.tensor_tensor_scan(gin[:, g, 0:n], run[:, 0:n], gin[:, g, 0:n], 0.0, ALU.mult,
                                           ALU.add).then_inc(*dec_ok.up(b))

            def k_factor(b):
                n = tiles(b) * P
                for g in range(4):
                    dve.tensor_scalar(scr[:, g, 0:n], ta[:, g, 0:n], par_s("kah", g), par_s("ka1", g),
                                      ALU.mult, ALU.add).then_inc(*kf_ok.up(b))

            def k_prime(b):
                n = tiles(b) * P
                dve.wait_ge(kf_ok.sem, kf_ok.at(b, 4))
                dve.wait_ge(kk_ok.sem, kk_ok.at(b, 4))
                dve.tensor_tensor(xm[:, 4:8, 0:n], xm[:, 4:8, 0:n], scr[:, :, 0:n], ALU.mult).then_inc(*kp_ok.up(b))
                dve.scalar_tensor_tensor(out=ta[:, :, 0:n], in0=ta[:, :, 0:n], scalar=1.0, in1=kk[:, :, 0:n],
                                         op0=ALU.add, op1=ALU.mult).then_inc(*kp_ok.up(b))

            def rkk(b):
                n = tiles(b) * P
                dve.wait_ge(kp_ok.sem, kp_ok.at(b, 2))
                for g in range(4):
                    dve.scalar_tensor_tensor(out=scr[:, g, 0:n], in0=xm[:, g, 0:n], scalar=par_s("rk", g),
                                             in1=xm[:, 4 + g, 0:n], op0=ALU.mult, op1=ALU.mult)\
                       .then_inc(*rkk_ok.up(b))

            def operands0(b):
                n = tiles(b) * P
                dve.wait_ge(gam_ok.sem, gam_ok.at(b, 2))
                if not is_sample(b):
                    dve.wait_ge(bd_ok.sem, bd_ok.at(b, 0))
                    pe_s.wait_prev(dve, b, 0, "scores")
                dve.tensor_tensor(kappa[:, :, 0:n], xm[:, 4:8, 0:n], gin[:, :, 0:n], ALU.mult).then_inc(*op_ok.up(b))
                dve.scalar_tensor_tensor(out=beta[:, :, 0:n], in0=ta[:, :, 0:n], scalar=-0.5, in1=gin[:, :, 0:n],
                                         op0=ALU.mult, op1=ALU.mult).then_inc(*op_ok.up(b))

            def operands1(b):
                n, l = tiles(b) * P, L(b)
                dve.tensor_tensor(segs(ar[:, :, 0, 0:n], l), segs(kk[:, :, 0:n], l), gview(b, True),
                                  ALU.mult).then_inc(*op_ok.up(b))
                if not (isinstance(b, int) and b == 1):
                    rho(b, 0, n - CH)

            def rho(b, start, end):
                l = L(b)
                s = slice(start, end)
                dve.tensor_tensor(segs(ar[:, :, 1, s], l), segs(xm[:, 0:4, s], l),
                                  gview(b, False)[:, :, start // l:end // l, :], ALU.mult).then_inc(*op_ok.up(b))

            def last_rho(b):
                n = tiles(b) * P
                if not is_sample(b):
                    dve.wait_ge(pe_s.s.sem, pe_s.s.at(b, 0))
                if isinstance(b, int) and b == 1:
                    rho(b, 0, n - CH)
                rho(b, n - CH, n)

            def masked(b, ch):
                pe_s.wait(dve, b, ch, "scores")
                if isinstance(b, int) and b == 1 or not isinstance(b, int):
                    if ch == 0:
                        dve.wait_ge(remade.sem, N_RUN + N_MASKS)

                def spread(out, src, mask):
                    return dve.tensor_tensor(blocks2(out[:, :, :]), bc(src, [P, 4, 2, CH], 2),
                                             bc(mask[:, :].rearrange("p (a t) -> p a t", a=2), [P, 4, 2, CH], 1),
                                             ALU.mult)

                def stacked(out, src, mask):
                    return dve.tensor_tensor(out, src, bc(mask[:, :], [P, 4, CH], 1), ALU.mult)

                spread(bdBT, half(R[2], 1), gt_bd).then_inc(*dve_s.up(b))
                stacked(PT[:, :, :], half(R[2], 1), gt_c).then_inc(*dve_s.up(b))
                spread(bdB, b4(R[3])[:, :, 0:CH], lt_bd).then_inc(*dve_s.up(b))
                stacked(PB[:, :, :], b4(R[3])[:, :, 0:CH], lt_c).then_inc(*dve_s.up(b))
                dve_s.wait(dve, b, ch, "PB")
                dve.tensor_tensor(Yc[:, :, :], PB[:, :, :], bc(ident2[:, :], [P, 4, CH], 1),
                                  ALU.add).then_inc(*dve_s.up(b))
                stacked(Aq[:, 0], b4(R[3])[:, :, CH:P], le_c).then_inc(*dve_s.up(b))
                spread(bdAak, b4(R[4])[:, :, 0:CH], lt_bd).then_inc(*dve_s.up(b))
                stacked(Aq[:, 1], b4(R[4])[:, :, CH:P], le_c).then_inc(*dve_s.up(b))

            def squared(b, ch, j):
                pe_s.wait(dve, b, ch, "sq%d" % j)
                if j == 1:
                    dve_s.wait(dve, b, ch, "Y0")
                if j <= 4:
                    dve.tensor_tensor(blocks2(bdB[:, :, :]), bc(b4(R[2])[:, :, 0:CH], [P, 4, 2, CH], 2),
                                      bc(headsum[:, :].rearrange("p (a t) -> p a t", a=2), [P, 4, 2, CH], 1),
                                      ALU.mult).then_inc(*dve_s.up(b))
                    dve.tensor_copy(PB[:, :, :], b4(R[2])[:, :, 0:CH]).then_inc(*dve_s.up(b))
                if 2 <= j <= 5:
                    dve.tensor_tensor(Yc[:, :, :], b4(R[2])[:, :, CH:P], Yc[:, :, :], ALU.add).then_inc(*dve_s.up(b))
                if j == 6:
                    dve_s.wait(dve, b, ch, "Y5")
                    for h in range(2):
                        rows = slice(64 * h, 64 * h + 64)
                        dve.tensor_tensor(bdY[rows, :, rows], b4(R[2])[:, :, CH:P][rows, :, :], Yc[rows, :, :],
                                          ALU.add).then_inc(*dve_s.up(b))

            def solved(b, ch):
                pe_s.wait(dve, b, ch, "Z")
                dve_s.wait(dve, b, ch, "Y6b")
                dve.tensor_copy(Zc[:, :, :], half(R[0], 0)).then_inc(*dve_s.up(b))
                if is_sample(b):
                    for j in range(4):
                        dve_s.wait(dve, b, ch, "Z%d" % (j - 1) if j else "Za")
                        dve.scalar_tensor_tensor(out=Zc[:, :, :], in0=half(R[3 + j // 2], j % 2),
                                                 scalar=seg_rows[:, j:j + 1], in1=Zc[:, :, :], op0=ALU.mult,
                                                 op1=ALU.add).then_inc(*dve_s.up(b))

            def states(b, ch):
                pe_s.wait(dve, b, ch, "U")
                dve.tensor_copy(Uc[:, :, :], half(R[0], 1)).then_inc(*dve_s.up(b))
                if not is_sample(b):
                    pe_s.wait(dve, b, ch, "state")
                    dve.tensor_tensor(S[:, :, :], half(R[3], 0), S[:, :, :], ALU.add).then_inc(*dve_s.up(b))
                    dve_s.wait(dve, b, ch, "Ssum")
                    if ch == 0:
                        dve.wait_ge(vv_ok.sem, vv_ok.at(b, 2))
                    if ch:
                        act_s.wait(dve, b, ch - 1, "bdS1")
                    dve.tensor_tensor(S[:, :, :], S[:, :, :], bc(gL[:, :, ch], [P, 4, CH], 2),
                                      ALU.mult).then_inc(*dve_s.up(b))
                    return
                for j in range(4):
                    if j:
                        pe_s.wait(dve, b, ch, "y%d" % (j - 1))
                    for h in range(2):
                        rows = slice(64 * h, 64 * h + 64)
                        dve.tensor_copy(bdS[rows, :, rows], Ss[rows, j]).then_inc(*dve_s.up(b))
                pe_s.wait(dve, b, ch, "y")
                dve.wait_ge(vv_ok.sem, vv_ok.at(b, 2))
                for j in range(4):
                    if j:
                        pe_s.wait(dve, b, ch, "s%d" % (j - 1))
                    dve_s.wait(dve, b, ch, "U")
                    for src, at in ((Uc, 0), (Vc, CH)):
                        dve.tensor_scalar(bdAak[:, :, at:at + CH], src[:, :, :], seg_rows[:, j:j + 1], None,
                                          ALU.mult).then_inc(*dve_s.up(b))
                    pe_s.wait(dve, b, ch, "s%d" % j if j < 3 else "state")
                    dve.tensor_tensor(Ss[:, j], half(R[3], 0), Ss[:, j], ALU.add).then_inc(*dve_s.up(b))
                    dve_s.wait(dve, b, ch, "sum%d" % j if j < 3 else "Ssum")
                    dve.tensor_tensor(Ss[:, j], Ss[:, j], bc(gL[:, :, 4 * ch + j], [P, 4, CH], 2),
                                      ALU.mult).then_inc(*dve_s.up(b))

            def normed(tile):
                y = yT[:, tile.i]
                dve.wait_ge(gr_ok.sem, gr_ok.at(tile, 2))
                dve.tensor_tensor(y, y, b4(o_bank[0]), ALU.mult).then_inc(*post_ok.up(tile))
                dve.wait_ge(post_ok.sem, post_ok.at(tile, 1))
                for g in range(4):
                    dve.tensor_scalar(y[:, g, :], y[:, g, :], par_s("lnw", g), lnb_s[:, g:g + 1], ALU.mult,
                                      ALU.add).then_inc(*post_ok.up(tile))

            def gated(tile):
                y = yT[:, tile.i]
                dve.wait_ge(post_ok.sem, post_ok.at(tile, 5))
                dve.tensor_tensor(y, y, bonus[:, :, tile.i * P:(tile.i + 1) * P], ALU.add).then_inc(*post_ok.up(tile))
                dve.wait_ge(post_ok.sem, post_ok.at(tile, 6))
                dve.wait_ge(zr_in.sem, zr_in.at(tile, 1))
                dve.tensor_tensor(y, y, zr[:, :, :], ALU.mult).then_inc(*post_ok.up(tile))

            def low_part(tile):
                dve.wait_ge(mh_ok.sem, mh_ok.at(tile, 1))
                dve.tensor_tensor(m_hl[:, 1, 1], yT[:, tile.i], m_hl[:, 1, 0],
                                  ALU.subtract).then_inc(*ml_ok.up(tile))

            def bonuses(b, k):
                n, start = tiles(b) * P, P if is_sample(b) else 0
                dve.wait_ge(gb_full.sem, gb_full.at(b, k + 1))
                dve.tensor_tensor(bonus[:, 2 * k:2 * k + 2, start:start + n],
                                  o_bank[1][:, 0:2 * n].rearrange("p (g t) -> p g t", g=2),
                                  xm[:, 8 + 2 * k:10 + 2 * k, 0:n], ALU.mult).then_inc(*bonus_ok.up(b))

            def out_sum(tile):
                dve.wait_ge(ss_ok.sem, ss_ok.at(tile, 2))
                dve.tensor_reduce(st[:, 4:5], st[:, 0:2], mybir.AxisListType.X, ALU.add).then_inc(*st_ok.up(tile))

            def finish(tile):
                dve.wait_ge(xy_in.sem, xy_in.at(tile, 1))
                dve.wait_ge(ss_ok.sem, ss_ok.at(tile, 4))
                for h in range(2):
                    dve.scalar_tensor_tensor(out=o_bank[h][:, :], in0=o_bank[h][:, :], scalar=st[:, 5:6],
                                             in1=npost[:, h * 512:(h + 1) * 512], op0=ALU.mult,
                                             op1=ALU.mult).then_inc(*fin_ok.up(tile))
                    dve.wait_ge(fin_ok.sem, fin_ok.at(tile, 2 * h + 1))
                    dve.tensor_tensor(x_y[:, h * 512:(h + 1) * 512], o_bank[h][:, :], x_y[:, h * 512:(h + 1) * 512],
                                      ALU.add).then_inc(*fin_ok.up(tile))

            does = {"gate0": normed, "gate1": gated, "low": low_part, "bonus0": lambda b: bonuses(b, 0),
                    "bonus1": lambda b: bonuses(b, 1), "sum": out_sum, "finish": finish, "decay": decay,
                    "k_factor": k_factor, "k_prime": k_prime, "rkk": rkk, "operands0": operands0,
                    "operands1": operands1}

            def body(b, has_next=True):
                slots = plan(b, has_next)
                does["piece"] = lambda p: PIECES[p][3] and projected(b + 1, PIECES[p][0])

                def fill(ch, k):
                    run_plan(slots, ch * SLOTS + k, does)

                for ch in range(nchunks(b)):
                    fill(ch, 0)
                    masked(b, ch)
                    fill(ch, 1)
                    fill(ch, 2)
                    for j in range(1, 7):
                        squared(b, ch, j)
                        fill(ch, 2 + j)
                    solved(b, ch)
                    fill(ch, 9)
                    states(b, ch)
                    fill(ch, 10)
                if has_next:
                    last_rho(b + 1)

            for r, kind in enumerate(ROUNDS):
                projected(0, r)
                if kind == "la2":
                    decay(0)
                if kind == "kn2":
                    k_factor(0)
                    k_prime(0)
                    rkk(0)
            operands0(0)
            operands1(0)
            last_rho(0)
            body(0)
            with dve.Fori(1, LAST) as b:
                body(b)
            body(LAST, has_next=False)
            tile = Tile(LAST, 0)
            normed(tile)
            gated(tile)
            low_part(tile)
            out_sum(tile)
            finish(tile)

        for s in signals:
            s.check()



def channels(a):
    return np.ascontiguousarray(a.reshape(-1, P).T)


def kernel(**inputs):
    from concourse import bacc
    from concourse.bass_utils import run_bass_kernel_spmd

    a = {k: np.asarray(v) for k, v in inputs.items()}
    mu = a["rwkv_mu"][0]
    ins = {
        "x": np.concatenate([a["x_sample"].reshape(1, P, D), a["x_prompt"].reshape(SEQ // P, P, D)]),
        "w_in": a["w_in"][0],
        "w_out": a["w_out"][0],
        "gla_a_up": a["gla_a_up"][0],
        "rwkv_w_up": a["rwkv_w_up"][0],
        "rwkv_a_up": a["rwkv_a_up"][0],
        "norm_post": a["norm_post"],
        "state_gla": a["state_gla"][0].reshape(8, 2, 2, 64, 128).transpose(2, 3, 0, 1, 4).reshape(P, 8, 2, 128),
        "state_rwkv": a["state_rwkv"][0].reshape(8, 4, 2, 64, 64).transpose(2, 4, 0, 1, 3).reshape(P, 8, 4, 64),
        "state_shift": a["state_shift"][0].reshape(8, 13, P).transpose(2, 1, 0),
        "par": np.concatenate([channels(a[k]) for k in (
            "norm_pre", "gla_a_bias", "gla_norm", "rwkv_mu", "rwkv_w0", "rwkv_a0", "rwkv_k_k", "rwkv_k_a",
            "rwkv_r_k", "rwkv_ln_w", "rwkv_ln_b")], axis=1),
    }
    outs = {
        "y": (1 + SEQ // P, P, D),
        "gla_prompt": (P, 2, P), "gla_sample": (P, 8, 2, P),
        "rwkv_prompt": (P, 4, 64), "rwkv_sample": (P, 8, 4, 64),
        "shift_prompt": (P, 13), "shift_sample": (P, 13, 8),
    }
    scratch = {"hT": ((NB, P, 2, KT, BLK), F16), "zr": ((NB, P, 4, BLK), F32), "mg": ((NB, P, 2, 2, 4, P), F16)}
    nc = bacc.Bacc("TRN2", target_bir_lowering=False, num_devices=1)
    t, arrays = {}, {}
    for name, v in ins.items():
        arrays["in_" + name] = np.ascontiguousarray(v)
        t[name] = nc.dram_tensor("in_" + name, v.shape, mybir.dt.from_np(v.dtype), kind="ExternalInput").ap()
    for name, shape in outs.items():
        t[name] = nc.dram_tensor("out_" + name, shape, F32, kind="ExternalOutput").ap()
    for name, (shape, dt) in scratch.items():
        t[name] = nc.dram_tensor("scratch_" + name, shape, dt, kind="Internal").ap()
    build(nc, t)
    r = run_bass_kernel_spmd(nc, [arrays], core_ids=[0]).results[0]

    def heads(o, n):
        return o.reshape((2, 64) + o.shape[1:])

    gp = heads(r["out_gla_prompt"], 0).transpose(2, 0, 1, 3).reshape(1, 1, 4, 64, 128)
    gs = heads(r["out_gla_sample"], 0).transpose(2, 3, 0, 1, 4).reshape(1, 8, 4, 64, 128)
    rp = heads(r["out_rwkv_prompt"], 0).transpose(2, 0, 3, 1).reshape(1, 1, 8, 64, 64)
    rs = heads(r["out_rwkv_sample"], 0).transpose(2, 3, 0, 4, 1).reshape(1, 8, 8, 64, 64)
    return (r["out_y"][1:].reshape(1, SEQ, D), r["out_y"][0].reshape(8, 16, D), gp, gs, rp, rs,
            r["out_shift_prompt"].T.reshape(1, 1, SHIFT_W), r["out_shift_sample"].transpose(2, 1, 0).reshape(1, 8, SHIFT_W))
```
